# Optimizing a Trainium2 kernel written in Bass

```python
import jax, jax.numpy as jnp
from jax import lax
import numpy as np

D_MODEL = 1024
BATCH = 1
SEQ = 256
DEPTH = 1

CHUNK = 64
HG_HEADS = 8
HG_DK = 64
HG_DV = 64
HG_WIDTH = HG_HEADS * HG_DK
CONV_WIDTH = 512
CONV_K = 3
N_BRANCH = 2
PEER_HEADS = 8
PEER_NKEYS = 128
PEER_N = PEER_NKEYS * PEER_NKEYS
PEER_QDIM = 256
PEER_HALF = PEER_QDIM // 2
PEER_TOPK = 16
PEER_BLOCK = 128
EPS = 1e-6
IN_SPLITS = [HG_WIDTH] * 4 + [CONV_WIDTH] * 3 + [N_BRANCH * D_MODEL]
IN_COLS = sum(IN_SPLITS)


def rmsnorm(x, g):
    xf = x.astype(jnp.float32)
    y = xf * lax.rsqrt(jnp.mean(xf * xf, axis=-1, keepdims=True) + EPS)
    return (y * g.astype(jnp.float32)).astype(x.dtype)

def hgrn2_chunkwise(q, k, log_f, v):
    b_, s_, h_, dk = q.shape
    dv = v.shape[-1]
    nc = s_ // CHUNK

    def to_chunks(t):
        return t.astype(jnp.float32).reshape(b_, nc, CHUNK, h_, t.shape[-1]).transpose(1, 0, 3, 2, 4)

    qc, kc, fc, vc = to_chunks(q), to_chunks(k), to_chunks(log_f), to_chunks(v)
    causal = jnp.tril(jnp.ones((CHUNK, CHUNK), dtype=bool))

    def step(state, inp):
        q_, k_, lf, v_ = inp
        b = jnp.cumsum(lf, axis=-2)
        b_last = b[..., -1:, :]
        o_inter = jnp.einsum('bhtd,bhde->bhte', q_ * jnp.exp(b), state)
        rel = jnp.where(causal[:, :, None], b[..., :, None, :] - b[..., None, :, :], -jnp.inf)
        scores = jnp.einsum('bhtd,bhsd,bhtsd->bhts', q_, k_, jnp.exp(rel))
        o = o_inter + jnp.einsum('bhts,bhse->bhte', scores, v_)
        new_state = (jnp.exp(b_last[..., 0, :])[..., None] * state
                     + jnp.einsum('bhsd,bhse->bhde', k_ * jnp.exp(b_last - b), v_))
        return new_state, o

    s0 = jnp.zeros((b_, h_, dk, dv), jnp.float32)
    _, o = lax.scan(step, s0, (qc, kc, fc, vc))
    return o.transpose(1, 0, 3, 2, 4).reshape(b_, s_, h_, dv)

def causal_depthwise_conv(u, w):
    c = u.shape[-1]
    return lax.conv_general_dilated(
        u, w[:, None, :].astype(u.dtype), window_strides=(1,), padding=[(CONV_K - 1, 0)],
        dimension_numbers=('NWC', 'WIO', 'NWC'), feature_group_count=c)

def peer_ffn(h, w_query, keys1, keys2, expert_u, expert_v):
    b_, s_, d = h.shape
    t = b_ * s_
    hf = h.reshape(t, d)
    q = (hf @ w_query).reshape(t, PEER_HEADS, 2, PEER_HALF)
    s1 = jnp.einsum('thc,hnc->thn', q[:, :, 0], keys1)
    s2 = jnp.einsum('thc,hnc->thn', q[:, :, 1], keys2)
    v1, i1 = lax.top_k(s1, PEER_TOPK)
    v2, i2 = lax.top_k(s2, PEER_TOPK)
    cand_s = (v1[..., :, None] + v2[..., None, :]).reshape(t, PEER_HEADS, PEER_TOPK * PEER_TOPK)
    cand_i = (i1[..., :, None] * PEER_NKEYS + i2[..., None, :]).reshape(t, PEER_HEADS, PEER_TOPK * PEER_TOPK)
    top_s, top_pos = lax.top_k(cand_s, PEER_TOPK)
    idx = jnp.take_along_axis(cand_i, top_pos, axis=-1)
    gate = jax.nn.softmax(top_s.astype(jnp.float32), axis=-1).astype(h.dtype)
    nb = t // PEER_BLOCK

    def block(args):
        hb, ib, gb = args
        act = jax.nn.gelu(jnp.einsum('thkd,td->thk', expert_u[ib], hb), approximate=False)
        return jnp.einsum('thk,thkd->td', gb * act, expert_v[ib])

    out = lax.map(block, (hf.reshape(nb, PEER_BLOCK, d),
                          idx.reshape(nb, PEER_BLOCK, PEER_HEADS, PEER_TOPK),
                          gate.reshape(nb, PEER_BLOCK, PEER_HEADS, PEER_TOPK)))
    return out.reshape(b_, s_, d)

def first_inputs(seed: int = 0) -> dict:
    key = jax.random.key(seed)
    ks = jax.random.split(key, 18)
    f32 = jnp.float32
    nrm = lambda k, shape, scale: jax.random.normal(k, shape, f32) * scale
    gain = lambda k, shape: 1.0 + 0.02 * jax.random.normal(k, shape, f32)
    return {
        "x": jax.random.normal(ks[0], (BATCH, SEQ, D_MODEL), f32),
        "norm_mix_g": gain(ks[1], (DEPTH, D_MODEL)),
        "w_in": nrm(ks[2], (DEPTH, D_MODEL, IN_COLS), D_MODEL ** -0.5),
        "hg_lb_logits": nrm(ks[3], (DEPTH + 1, HG_WIDTH), 0.1),
        "hg_out_norm_g": gain(ks[4], (DEPTH, HG_WIDTH)),
        "conv_w": nrm(ks[5], (DEPTH, CONV_K, CONV_WIDTH), CONV_K ** -0.5),
        "w_branch_hg": nrm(ks[6], (DEPTH, HG_WIDTH, D_MODEL), HG_WIDTH ** -0.5),
        "w_branch_conv": nrm(ks[7], (DEPTH, CONV_WIDTH, D_MODEL), CONV_WIDTH ** -0.5),
        "w_out": nrm(ks[8], (DEPTH, D_MODEL, D_MODEL), D_MODEL ** -0.5),
        "norm_ffn_g": gain(ks[9], (DEPTH, D_MODEL)),
        "peer_w_query": nrm(ks[10], (DEPTH, D_MODEL, PEER_HEADS * PEER_QDIM), D_MODEL ** -0.5),
        "peer_keys1": nrm(ks[11], (DEPTH, PEER_HEADS, PEER_NKEYS, PEER_HALF), PEER_HALF ** -0.5),
        "peer_keys2": nrm(ks[12], (DEPTH, PEER_HEADS, PEER_NKEYS, PEER_HALF), PEER_HALF ** -0.5),
        "peer_u": nrm(ks[13], (DEPTH, PEER_N, D_MODEL), D_MODEL ** -0.5),
        "peer_v": nrm(ks[14], (DEPTH, PEER_N, D_MODEL), PEER_HEADS ** -0.5),
        "norm_final_g": gain(ks[15], (D_MODEL,)),
    }

def first_block(x, norm_mix_g, w_in, hg_lb_logits, hg_out_norm_g, conv_w, w_branch_hg,
              w_branch_conv, w_out, norm_ffn_g, peer_w_query, peer_keys1, peer_keys2,
              peer_u, peer_v, norm_final_g):
    b_, s_, _ = x.shape
    lb_all = jnp.cumsum(jax.nn.softmax(hg_lb_logits.astype(jnp.float32), axis=0), axis=0)
    split_at = list(np.cumsum(IN_SPLITS)[:-1])
    for l in range(DEPTH):
        h = rmsnorm(x, norm_mix_g[l])
        proj = h @ w_in[l]
        hq, hf, hi, hg, cb, cc, ch, gates = jnp.split(proj, split_at, axis=-1)

        lb = lb_all[l]
        q = jax.nn.silu(hq.astype(jnp.float32)) * (HG_DK ** -0.5)
        sig = jax.nn.sigmoid(hf.astype(jnp.float32))
        forget = lb + (1.0 - lb) * sig
        k = 1.0 - forget
        log_f = jnp.log(forget)
        rs = lambda t: t.reshape(b_, s_, HG_HEADS, -1)
        o = hgrn2_chunkwise(rs(q), rs(k), rs(log_f), rs(hi))
        o = o * lax.rsqrt(jnp.mean(o * o, axis=-1, keepdims=True) + EPS)
        o = o * hg_out_norm_g[l].astype(jnp.float32).reshape(HG_HEADS, HG_DV)
        y_a = (o.reshape(b_, s_, HG_WIDTH) * jax.nn.silu(hg.astype(jnp.float32))).astype(x.dtype)

        y_b = cb * causal_depthwise_conv(cc * ch, conv_w[l])

        g_a, g_b = jnp.split(jax.nn.sigmoid(gates), 2, axis=-1)
        merged = g_a * (y_a @ w_branch_hg[l]) + g_b * (y_b @ w_branch_conv[l])
        x = x + merged @ w_out[l]

        x = x + peer_ffn(rmsnorm(x, norm_ffn_g[l]), peer_w_query[l], peer_keys1[l],
                         peer_keys2[l], peer_u[l], peer_v[l])
    return rmsnorm(x, norm_final_g)


DEPTH_2 = 2

HEAD_DIM = 64
SB_HEADS = 8
SB_WIDTH = SB_HEADS * HEAD_DIM
POOL_WINDOWS = (2, 4, 8, 16)
POOL_WIDTH = D_MODEL // 2
POOL_GROUP = POOL_WIDTH // len(POOL_WINDOWS)
EVEN_IN = 3 * SB_WIDTH + POOL_WIDTH
EVEN_MIX = SB_WIDTH + POOL_WIDTH
MOBA_HEADS = D_MODEL // HEAD_DIM
MOBA_WIDTH = MOBA_HEADS * HEAD_DIM
MOBA_BLOCK = 256
MOBA_TOPK = 3
MOBA_QCHUNK = 16
Q_BLOCK = 128
D_FF = 2816
N_EVEN = (DEPTH_2 + 1) // 2
N_ODD = DEPTH_2 // 2
RMS_EPS = 1e-6


def rmsnorm_2(x, g):
    xf = x.astype(jnp.float32)
    y = xf * lax.rsqrt(jnp.mean(xf * xf, axis=-1, keepdims=True) + RMS_EPS)
    return (y * g.astype(jnp.float32)).astype(x.dtype)

def swiglu(h, w_gate, w_up, w_down):
    return (jax.nn.silu(h @ w_gate) * (h @ w_up)) @ w_down

def split_heads(t, n):
    b, s, _ = t.shape
    return t.reshape(b, s, n, HEAD_DIM).transpose(0, 2, 1, 3)

def merge_heads(t):
    b, h, s, dh = t.shape
    return t.transpose(0, 2, 1, 3).reshape(b, s, h * dh)

def alibi_slopes(n):
    return jnp.asarray(2.0 ** (-8.0 * np.arange(1, n + 1) / n), dtype=jnp.float32)

def stick_breaking_attention(q, k, v):
    s_len = q.shape[2]
    scale = HEAD_DIM ** -0.5
    outs = []
    for i in range(s_len // Q_BLOCK):
        q0 = i * Q_BLOCK
        kv_len = q0 + Q_BLOCK
        qb = q[:, :, q0:kv_len]
        kb = k[:, :, :kv_len]
        vb = v[:, :, :kv_len]
        z = jnp.einsum('bhtd,bhsd->bhts', qb, kb).astype(jnp.float32) * scale
        tpos = q0 + jnp.arange(Q_BLOCK)[:, None]
        spos = jnp.arange(kv_len)[None, :]
        past = spos < tpos
        log_1m = jnp.where(past, jax.nn.log_sigmoid(-z), 0.0)
        later = lax.cumsum(log_1m, axis=3, reverse=True) - log_1m
        a = jnp.where(past, jnp.exp(jax.nn.log_sigmoid(z) + later), 0.0)
        outs.append(jnp.einsum('bhts,bhsd->bhtd', a.astype(v.dtype), vb))
    return jnp.concatenate(outs, axis=2)

def multiscale_pool(u, w_pool, pool_scale):
    b, s, _ = u.shape
    uf = u.astype(jnp.float32)
    cs = jnp.concatenate([jnp.zeros((b, 1, POOL_WIDTH), jnp.float32), jnp.cumsum(uf, axis=1)], axis=1)
    t = jnp.arange(s)
    groups = []
    for g, w in enumerate(POOL_WINDOWS):
        sl = slice(g * POOL_GROUP, (g + 1) * POOL_GROUP)
        start = jnp.maximum(t + 1 - w, 0)
        win_sum = cs[:, 1:, sl] - cs[:, start, sl]
        count = jnp.minimum(t + 1, w).astype(jnp.float32)[None, :, None]
        groups.append(win_sum / count - uf[:, :, sl])
    pooled = jnp.stack(groups, axis=2).astype(u.dtype)
    mixed = jnp.einsum('bsgc,gcd->bsgd', pooled, w_pool).reshape(b, s, POOL_WIDTH)
    return mixed * pool_scale

def moba_attention(q, k, v):
    b, h, s, dh = q.shape
    nb = -(-s // MOBA_BLOCK)
    pad = nb * MOBA_BLOCK - s
    kp = jnp.pad(k, ((0, 0), (0, 0), (0, pad), (0, 0)))
    vp = jnp.pad(v, ((0, 0), (0, 0), (0, pad), (0, 0)))
    k_blocks = kp.reshape(b, h, nb, MOBA_BLOCK, dh)
    v_blocks = vp.reshape(b, h, nb, MOBA_BLOCK, dh)
    k_mean = jnp.mean(k_blocks.astype(jnp.float32), axis=3).astype(k.dtype)
    gate = jnp.einsum('bhtd,bhnd->bhtn', q, k_mean).astype(jnp.float32)
    qblk_all = jnp.arange(s) // MOBA_BLOCK
    past_blk = jnp.arange(nb)[None, :] < qblk_all[:, None]
    gate = jnp.where(past_blk, gate, -jnp.inf)
    topk = min(MOBA_TOPK, nb)
    _, sel = lax.top_k(gate, topk)
    scale = dh ** -0.5
    slopes = alibi_slopes(h)
    bi = jnp.arange(b)[:, None, None, None]
    hi = jnp.arange(h)[None, :, None, None]

    def chunk(c):
        t0 = c * MOBA_QCHUNK
        qc = lax.dynamic_slice_in_dim(q, t0, MOBA_QCHUNK, axis=2)
        sel_c = lax.dynamic_slice_in_dim(sel, t0, MOBA_QCHUNK, axis=2)
        tq = t0 + jnp.arange(MOBA_QCHUNK)
        blk0 = (t0 // MOBA_BLOCK) * MOBA_BLOCK
        k_own = lax.dynamic_slice_in_dim(kp, blk0, MOBA_BLOCK, axis=2)
        v_own = lax.dynamic_slice_in_dim(vp, blk0, MOBA_BLOCK, axis=2)
        own_pos = blk0 + jnp.arange(MOBA_BLOCK)
        k_sel = k_blocks[bi, hi, sel_c]
        v_sel = v_blocks[bi, hi, sel_c]
        sel_pos = sel_c[..., None] * MOBA_BLOCK + jnp.arange(MOBA_BLOCK)
        sel_ok = (sel_c < (tq // MOBA_BLOCK)[:, None])[..., None]
        d_own = (tq[:, None] - own_pos[None, :]).astype(jnp.float32)
        s_own = (jnp.einsum('bhtd,bhsd->bhts', qc, k_own).astype(jnp.float32) * scale
                 - slopes[None, :, None, None] * d_own)
        s_own = jnp.where(own_pos[None, :] <= tq[:, None], s_own, -jnp.inf)
        d_sel = (tq[:, None, None] - sel_pos).astype(jnp.float32)
        s_sel = (jnp.einsum('bhtd,bhtksd->bhtks', qc, k_sel).astype(jnp.float32) * scale
                 - slopes[None, :, None, None, None] * d_sel)
        s_sel = jnp.where(sel_ok, s_sel, -jnp.inf).reshape(b, h, MOBA_QCHUNK, topk * MOBA_BLOCK)
        p = jax.nn.softmax(jnp.concatenate([s_own, s_sel], axis=-1), axis=-1)
        p_own = p[..., :MOBA_BLOCK].astype(v.dtype)
        p_sel = p[..., MOBA_BLOCK:].reshape(b, h, MOBA_QCHUNK, topk, MOBA_BLOCK).astype(v.dtype)
        return (jnp.einsum('bhts,bhsd->bhtd', p_own, v_own)
                + jnp.einsum('bhtks,bhtksd->bhtd', p_sel, v_sel))

    outs = lax.map(chunk, jnp.arange(s // MOBA_QCHUNK))
    return outs.transpose(1, 2, 0, 3, 4).reshape(b, h, s, dh)

def even_mixer(h, w_in, w_pool, pool_scale, w_out):
    proj = h @ w_in
    q, k, v, u = jnp.split(proj, [SB_WIDTH, 2 * SB_WIDTH, 3 * SB_WIDTH], axis=-1)
    a = stick_breaking_attention(split_heads(q, SB_HEADS), split_heads(k, SB_HEADS), split_heads(v, SB_HEADS))
    p = multiscale_pool(u, w_pool, pool_scale)
    return jnp.concatenate([merge_heads(a), p], axis=-1) @ w_out

def odd_mixer(h, w_qkv, w_o):
    q, k, v = jnp.split(h @ w_qkv, 3, axis=-1)
    o = moba_attention(split_heads(q, MOBA_HEADS), split_heads(k, MOBA_HEADS), split_heads(v, MOBA_HEADS))
    return merge_heads(o) @ w_o

def second_inputs(seed: int = 0) -> dict:
    key = jax.random.key(seed)
    ks = jax.random.split(key, 20)
    f32 = jnp.float32

    def w(k, shape, fan_in):
        return jax.random.normal(k, shape, f32) * (fan_in ** -0.5)

    def gain(k, shape):
        return 1.0 + 0.05 * jax.random.normal(k, shape, f32)

    return {
        "x": jax.random.normal(ks[0], (BATCH, SEQ, D_MODEL), f32),
        "norm_ffn1": gain(ks[1], (DEPTH_2, D_MODEL)),
        "ffn1_gate": w(ks[2], (DEPTH_2, D_MODEL, D_FF), D_MODEL),
        "ffn1_up": w(ks[3], (DEPTH_2, D_MODEL, D_FF), D_MODEL),
        "ffn1_down": w(ks[4], (DEPTH_2, D_FF, D_MODEL), D_FF),
        "norm_mix": gain(ks[5], (DEPTH_2, D_MODEL)),
        "norm_ffn2": gain(ks[6], (DEPTH_2, D_MODEL)),
        "ffn2_gate": w(ks[7], (DEPTH_2, D_MODEL, D_FF), D_MODEL),
        "ffn2_up": w(ks[8], (DEPTH_2, D_MODEL, D_FF), D_MODEL),
        "ffn2_down": w(ks[9], (DEPTH_2, D_FF, D_MODEL), D_FF),
        "even_w_in": w(ks[10], (N_EVEN, D_MODEL, EVEN_IN), D_MODEL),
        "even_w_pool": w(ks[11], (N_EVEN, len(POOL_WINDOWS), POOL_GROUP, POOL_GROUP), POOL_GROUP),
        "even_pool_scale": gain(ks[12], (N_EVEN, POOL_WIDTH)),
        "even_w_out": w(ks[13], (N_EVEN, EVEN_MIX, D_MODEL), EVEN_MIX),
        "odd_w_qkv": w(ks[14], (N_ODD, D_MODEL, 3 * MOBA_WIDTH), D_MODEL),
        "odd_w_o": w(ks[15], (N_ODD, MOBA_WIDTH, D_MODEL), MOBA_WIDTH),
        "norm_final": gain(ks[16], (D_MODEL,)),
    }

def second_block(x, norm_ffn1, ffn1_gate, ffn1_up, ffn1_down, norm_mix, norm_ffn2,
              ffn2_gate, ffn2_up, ffn2_down, even_w_in, even_w_pool, even_pool_scale,
              even_w_out, odd_w_qkv, odd_w_o, norm_final):
    for layer in range(DEPTH_2):
        x = x + 0.5 * swiglu(rmsnorm_2(x, norm_ffn1[layer]), ffn1_gate[layer], ffn1_up[layer], ffn1_down[layer])
        h = rmsnorm_2(x, norm_mix[layer])
        i = layer // 2
        if layer % 2 == 0:
            x = x + even_mixer(h, even_w_in[i], even_w_pool[i], even_pool_scale[i], even_w_out[i])
        else:
            x = x + odd_mixer(h, odd_w_qkv[i], odd_w_o[i])
        x = x + 0.5 * swiglu(rmsnorm_2(x, norm_ffn2[layer]), ffn2_gate[layer], ffn2_up[layer], ffn2_down[layer])
    return rmsnorm_2(x, norm_final)


def setup_inputs(seed=0):
    out = dict(first_inputs(seed))
    for name, value in second_inputs(seed + 1).items():
        if name != "x":
            out[name + "_2"] = value
    return out


def reference(
    x, norm_mix_g, w_in, hg_lb_logits, hg_out_norm_g, conv_w, w_branch_hg, w_branch_conv, w_out,
    norm_ffn_g, peer_w_query, peer_keys1, peer_keys2, peer_u, peer_v, norm_final_g, norm_ffn1_2,
    ffn1_gate_2, ffn1_up_2, ffn1_down_2, norm_mix_2, norm_ffn2_2, ffn2_gate_2, ffn2_up_2,
    ffn2_down_2, even_w_in_2, even_w_pool_2, even_pool_scale_2, even_w_out_2, odd_w_qkv_2,
    odd_w_o_2, norm_final_2,
):
    x = first_block(
        x, norm_mix_g, w_in, hg_lb_logits, hg_out_norm_g, conv_w, w_branch_hg, w_branch_conv,
        w_out, norm_ffn_g, peer_w_query, peer_keys1, peer_keys2, peer_u, peer_v, norm_final_g,
    )
    return second_block(
        x, norm_ffn1_2, ffn1_gate_2, ffn1_up_2, ffn1_down_2, norm_mix_2, norm_ffn2_2,
        ffn2_gate_2, ffn2_up_2, ffn2_down_2, even_w_in_2, even_w_pool_2, even_pool_scale_2,
        even_w_out_2, odd_w_qkv_2, odd_w_o_2, norm_final_2,
    )


_drawn_inputs = setup_inputs


def setup_inputs(seed=0):
    import zlib

    import numpy as np

    out = dict(_drawn_inputs(seed))
    spreads = {}
    factors = {'hg_lb_logits': 3.942, 'hg_out_norm_g': 3.575, 'norm_ffn_g': 2.842}
    for name, (base, spread) in spreads.items():
        noise = np.random.default_rng([zlib.crc32(name.encode()), seed]).standard_normal(out[name].shape)
        drawn = base * np.exp(spread * noise) if base else spread * noise
        out[name] = __import__('jax').numpy.asarray(drawn.astype(out[name].dtype))
    for name, factor in factors.items():
        out[name] = (out[name] * factor).astype(out[name].dtype)
    return out
```

```python
from contextlib import ExitStack

import numpy as np

import concourse.bass as bass
from concourse import mybir
from concourse.alu_op_type import AluOpType as ALU

STOP = None

ACT = mybir.ActivationFunctionType
AX_X = mybir.AxisListType.X
F32 = mybir.dt.float32
F32R = mybir.dt.float32r
U32 = mybir.dt.uint32

P = 128
T = 256
D = 1024
KT = D // P
TT = T // P
HEADS = 8
DH = 64
CHUNK = 64
NKEYS = 128
TOPK = 16
PEER_GROUPS = 16
D_FF = 2816
FT = D_FF // P
ODD_HEADS = 16
WINDOWS = (2, 4, 8, 16)
PAD = 16
RING = 4
EPS = 1e-6
NEG = -3.0e38
SCALE = DH ** -0.5

STREAM = [
    ("w_in", 44), ("branch", 8), ("w_out", 8), ("wquery", 16), ("peer", 2 * NKEYS),
    ("ffn0", 3 * FT), ("even_in", 16), ("even_out", 8), ("ffn1", 3 * FT),
    ("ffn2", 3 * FT), ("qkv", 24), ("w_o", 8), ("ffn3", 3 * FT),
]
ENDS = {"mix": "w_out", "peer": "peer", "ffn0": "ffn0", "even": "even_out", "ffn1": "ffn1",
        "ffn2": "ffn2", "odd": "w_o", "all": "ffn3"}

GAINS = ["norm_mix_g", "norm_ffn_g", "norm_final_g", "norm_ffn1_0", "norm_mix_0", "norm_ffn2_0",
         "norm_ffn1_1", "norm_mix_1", "norm_ffn2_1", "norm_final"]
COL = {name: KT * i for i, name in enumerate(GAINS)}
COL["lb0"] = KT * len(GAINS)
COL["lb1"] = COL["lb0"] + 4
COL["out_g"] = COL["lb1"] + 4
COL["conv"] = COL["out_g"] + 4
COL["pool_scale"] = COL["conv"] + 12
COL["eps"] = COL["pool_scale"] + 4
N_COLS = COL["eps"] + 1

LEVELS = [64, 32, 16, 8, 4, 2, 1]


def mixer_constants():
    i = np.arange(P)
    s, t = i[:, None], i[None, :]
    head_ones = (s // DH == t // DH).astype(np.float32)
    masks = []
    for m in LEVELS:
        masks.append((s // (2 * m) == t // (2 * m)) & (s % (2 * m) < m) & (t % (2 * m) >= m))
    chunk = np.broadcast_to((np.arange(T) % CHUNK != 0).astype(np.float32), (P, T))
    return np.concatenate([np.eye(P, dtype=np.float32), head_ones]
                          + [m.astype(np.float32) for m in masks] + [chunk], 1)


def attention_constants():
    i = np.arange(P)
    s, t = i[:, None], i[None, :]
    later = (s > t).astype(np.float32)
    past = (s < t).astype(np.float32)
    past_neg = np.concatenate([-past, -np.ones((P, P), np.float32), -past], 1)
    dist0 = np.where(t <= s, t - s, -1.0e30)
    dist1 = np.concatenate([np.broadcast_to(t - s - P, (P, P)), dist0], 1)
    dist = np.concatenate([dist0, dist1], 1).astype(np.float32)
    inv = [1.0 / np.minimum(np.arange(T) + 1, w) for w in WINDOWS]
    inv = np.broadcast_to(np.concatenate(inv).astype(np.float32), (P, 4 * T))
    return np.concatenate([np.eye(P, dtype=np.float32), later, past_neg, dist, inv], 1)


N_MIXC = P * (2 + len(LEVELS)) + T
N_ATTC = P * 2 + 3 * P + 3 * P + 4 * T

BASE = 16512
RAW, W_HI, W_LO = 0, RING * D, 2 * RING * D
H_HI = 3 * RING * D
H_LO = H_HI + KT * T
MID = H_LO + KT * T
COLS = MID + 4 * 2 * T
ONES = COLS + P
RSTD = ONES + 2 * P
ARENA = RSTD + T
X_AT = ARENA + P * T - KT * T
assert (BASE + 4 * (ARENA + P * T)) <= 229344


def stream_plan():
    names = [n for n, _ in STREAM]
    end = names.index(ENDS[STOP or "all"]) + 1
    first, at = {}, 0
    for name, n in STREAM[:end]:
        first[name] = at
        at += n
    if STOP:
        at += RING
    return first, at


def tile_readers(first):
    order = []
    order += ["act"] * 20 + ["dve"] * 8 + ["act"] * 16
    order += ["dve"] * 8 + ["dve"] * 8
    if "wquery" in first:
        order += ["act"] * 16
    if "even_in" in first:
        order += ["act"] * 16 + ["dve"] * 4 + ["dve"] * 8
    if "qkv" in first:
        order += ["act"] * 24 + ["dve"] * 8
    return order


def build(nc, stream, x_in, cols_in, ones_in, keys_in, wpool_in, mixc_in, attc_in, out):
    first, NSLAB = stream_plan()
    readers = tile_readers(first)
    tile_at = {}
    at = 0
    for name, n in (("w_in", 44), ("branch", 8), ("w_out", 8), ("wquery", 16), ("even_in", 16),
                    ("pooled", 4), ("even_out", 8), ("qkv", 24), ("w_o", 8)):
        if name in first or name == "pooled" and "even_in" in first:
            tile_at[name] = at
            at += n

    def slab_of(name, i):
        return first[name] + i

    def tile_buf(j, half=0):
        return tile[:, 2 * (j % 2) + half, :]

    def reads(engine, j):
        return sum(r == engine for r in readers[:j + 1])

    with ExitStack() as ctx:
        def sb(name, at, shape, dt=F32):
            return nc.alloc_sbuf_tensor_at(name, [P] + shape, dt, offset=BASE + 4 * at)

        def sem(name):
            return ctx.enter_context(nc.semaphore(name))

        raw = sb("raw", RAW, [RING, D])
        w_hi = sb("w_hi", W_HI, [RING, D], F32R)
        w_lo = sb("w_lo", W_LO, [RING, D], F32R)
        h_hi = sb("h_hi", H_HI, [KT, T], F32R)
        h_lo = sb("h_lo", H_LO, [KT, T], F32R)
        gate = sb("gate", MID, [2, T])
        hid = sb("hid", MID + 2 * T, [2, T])
        mid_hi = sb("mid_hi", MID + 4 * T, [2, T], F32R)
        mid_lo = sb("mid_lo", MID + 6 * T, [2, T], F32R)
        cols = sb("cols", COLS, [N_COLS])
        lane = sb("lane", ONES, [2, P])
        ones, iota = lane[:, 0, :], lane[:, 1, :]
        rstd = sb("rstd", RSTD, [T])
        pick1 = sb("pick1", MID, [4, P])
        pick2 = sb("pick2", MID + 4 * P, [4, P])
        idx1_T = sb("idx1_T", MID + 8 * P, [T])
        idx2_T = sb("idx2_T", MID + 8 * P + T, [T])
        gate_T = sb("gate_T", MID + 8 * P + 2 * T, [T])
        G = sb("G", ARENA, [T, P])
        x = sb("x", X_AT, [KT, T])
        h32 = sb("h32", ARENA + 2560, [KT, T])
        sq = sb("sq", ARENA + 4608, [KT, T])

        A = ARENA + 6656
        mixc = sb("mixc", ARENA, [N_MIXC])
        ident = mixc[:, 0:P]
        head_ones = mixc[:, P:2 * P]
        level_mask = {m: mixc[:, (2 + i) * P:(3 + i) * P] for i, m in enumerate(LEVELS)}
        chunk_mask = mixc[:, N_MIXC - T:N_MIXC]
        kk = sb("kk", A, [4, T])
        qq = sb("qq", A + 1024, [4, T])
        hgs = sb("hgs", A + 2048, [4, T])
        bb = sb("bb", A + 3072, [4, T])
        lf = sb("lf", A + 4096, [4, T])
        vv = sb("vv", A + 5120, [TT, 512])
        cc = sb("cc", A + 6144, [4, T])
        uu = sb("uu", A + 7168, [4, T + 2])
        conv = sb("conv", A + 8208, [4, T])
        sg = sb("sg", A + 9232, [16, T])
        y_hi = sb("y_hi", A + 13376, [KT, T], F32R)
        y_lo = sb("y_lo", A + 15424, [KT, T], F32R)
        y32 = sb("y32", A + 17472, [KT, T])
        S = sb("S", A + 19520, [4, 4, P])
        S_off = sb("S_off", A + 21568, [2, 4, P])
        lbw = sb("lbw", A + 22592, [8, 4])
        dec = sb("dec", A + 22624, [4, 4])
        assert A + 22640 <= X_AT
        X = sb("X", ARENA + 2560, [2, 4, T])
        osq = sb("osq", ARENA + 4608, [4, T])
        orr = sb("orr", ARENA + 5632, [4, T])
        keysT = sb("keysT", A, [PEER_GROUPS, NKEYS])
        qT = sb("qT", A + 2048, [PEER_GROUPS, T])
        top_v = sb("top_v", A + 6144, [TT, PEER_GROUPS, TOPK])
        top_i = sb("top_i", A + 6656, [TT, PEER_GROUPS, TOPK], U32)
        top_f = sb("top_f", A + 7168, [TT, PEER_GROUPS, TOPK])
        rest = sb("rest", A + 7680, [NKEYS])
        cand = sb("cand", A + 7808, [2, TOPK, TOPK])
        best = sb("best", A + 8320, [TT, HEADS, TOPK])
        pos = sb("pos", A + 8576, [TT, HEADS, TOPK], U32)
        pos1 = sb("pos1", A + 8832, [TT, HEADS, TOPK], U32)
        pos2 = sb("pos2", A + 9088, [TT, HEADS, TOPK], U32)
        posf = sb("posf", A + 9344, [2, TT, HEADS, TOPK])
        onehot = sb("onehot", A + 9856, [HEADS, TOPK, TOPK])
        idx = sb("idx", A + 11904, [2, TT, HEADS, TOPK])
        gts = sb("gts", A + 12416, [TT, HEADS, TOPK])
        gsum = sb("gsum", A + 12672, [TT, HEADS, 2])
        attc = sb("attc", ARENA, [N_ATTC])
        ident2 = attc[:, 0:P]
        later = attc[:, P:2 * P]
        past_neg = attc[:, 2 * P:5 * P]
        dist = attc[:, 5 * P:8 * P]
        inv_count = attc[:, 8 * P:8 * P + 4 * T].rearrange("p (g t) -> p g t", g=4)
        wpool = sb("wpool", ARENA + N_ATTC, [4, P])
        assert N_ATTC + 4 * P <= 2560
        aq = sb("aq", A, [4, T])
        ak = sb("ak", A + 1024, [4, T])
        av = sb("av", A + 2048, [TT, 512])
        pu = sb("pu", A + 3072, [4, PAD + T])
        az = sb("az", A + 4160, [HEADS, 3 * P])
        asp = sb("asp", A + 7232, [HEADS, 3 * P])
        aL = sb("aL", A + 10304, [HEADS, 3 * P])
        win = sb("win", ARENA + 2560, [2, PAD + T])
        pooled = sb("pooled", ARENA + 4608, [4, T])
        bq = sb("bq", A, [KT, T])
        bk = sb("bk", A + 2048, [KT, T])
        bv = sb("bv", A + 4096, [TT, D])
        sc = sb("sc", A + 6144, [2, 3 * P])
        pT = sb("pT", A + 6912, [2, 3 * P])
        st = sb("st", A + 7680, [3, 2, 2])

        acc = ctx.enter_context(nc.psum_tensor("acc", [P, KT, T], F32))
        front = ctx.enter_context(nc.psum_tensor("front", [P, 2, 2 * T], F32))
        tile = ctx.enter_context(nc.psum_tensor("tile", [P, 4, T], F32))
        banks = acc[:, :, :].rearrange("p (b a) t -> p b (a t)", b=4)
        fronts = front[:, :, :]

        landed = [sem(f"slab_landed{i}") for i in range(RING)]
        hi_ready = sem("slab_hi_ready")
        lo_ready = sem("slab_lo_ready")
        slab_used = sem("slab_used")
        pool_done = sem("pool_products_done")
        tile_read = {"act": sem("tile_read_by_act"), "dve": sem("tile_read_by_dve")}
        small_in = sem("small_inputs_landed")
        keys_in_sem = sem("keys_landed")
        attc_sem = sem("attention_constants_landed")
        dve_own = sem("dve_own_steps")
        act_own = sem("act_own_steps")
        x_ready = sem("x_ready")
        squares = sem("norm_squares")
        sums = sem("norm_sums")
        roots = sem("norm_roots")
        h32_ready = sem("norm_h32")
        nh_hi = sem("norm_h_hi")
        nh_lo = sem("norm_h_lo")
        gate_ready = sem("gate_ready")
        hid_ready = sem("hid_ready")
        mid_hi_ready = sem("mid_hi_ready")
        mid_lo_ready = sem("mid_lo_ready")
        out_done = sem("out_done")
        forget_ready = sem("forget_ready")
        logf_ready = sem("logf_ready")
        lb_diff = sem("lb_diff")
        lb_exp = sem("lb_exp")
        level_diff = sem("level_diff")
        level_exp = sem("level_exp")
        level_ready = sem("level_operands_ready")
        level_done = sem("level_scores_done")
        level_read = sem("level_scores_read")
        o_done = sem("hgrn_o_done")
        o_sq = sem("hgrn_o_squares")
        o_sum = sem("hgrn_o_sums")
        o_root = sem("hgrn_o_roots")
        y32_ready = sem("y32_ready")
        y_hi_ready = sem("y_hi_ready")
        y_lo_ready = sem("y_lo_ready")
        merged_ready = sem("merged_ready")
        merged_hi = sem("merged_hi")
        merged_lo = sem("merged_lo")
        keys_done = sem("key_scores_done")
        keys_read = sem("key_scores_read")
        gate_diff = sem("gate_diff")
        gate_exp = sem("gate_exp")
        picks_ready = sem("picks_ready")
        picks_turned = sem("picks_turned")
        picks_copied = sem("picks_copied")
        pick_ready = sem("pick_rows_ready")
        pick_used = sem("pick_rows_used")
        g_copied = sem("G_copied")
        x_seeded = sem("x_seeded")
        z_done = sem("stick_z_done")
        z_read = sem("stick_z_read")
        ln_ready = sem("stick_ln_ready")
        stick_L = sem("stick_L_ready")
        later_done = sem("stick_later_done")
        stick_w = sem("stick_w_ready")
        stick_e = sem("stick_exp_ready")
        stick_a = sem("stick_a_ready")
        ao_done = sem("stick_o_done")
        u_ready = sem("pool_u_ready")
        pooled_ready = sem("pooled_ready")
        sc_done = sem("odd_scores_done")
        sc_read = sem("odd_scores_read")
        p_exp = sem("odd_exp_ready")
        p_norm = sem("odd_p_ready")
        p_turned = sem("odd_p_turned")
        p_copied = sem("odd_p_copied")
        bo_done = sem("odd_o_done")

        block = ctx.enter_context(nc.Block())

        def layer_stages():
            for name, stage in (("ffn0", ("ffn", 0)), ("even_in", ("even", 0)), ("ffn1", ("ffn", 1)),
                                ("ffn2", ("ffn", 2)), ("qkv", ("odd", 0)), ("ffn3", ("ffn", 3))):
                if name in first:
                    yield stage

        FFN_GAIN = ["norm_ffn1_0", "norm_ffn2_0", "norm_ffn1_1", "norm_ffn2_1"]

        @block.sync
        def _(sp):
            sp.dma_start(x[:, :, :], x_in).then_inc(small_in, 16)
            sp.dma_start(cols[:, :], cols_in).then_inc(small_in, 16)
            sp.dma_start(lane[:, :, :], ones_in).then_inc(small_in, 16)
            for s in range(RING):
                sp.dma_start(raw[:, s, :], stream[s, :, :]).then_inc(landed[s], 16)
            sp.dma_start(mixc[:, :], mixc_in).then_inc(small_in, 16)
            with sp.Fori(1, NSLAB // RING) as turn:
                for s in range(RING):
                    sp.wait_ge(lo_ready, turn * RING + (s + 1 - RING))
                    sp.dma_start(raw[:, s, :], stream[bass.ds(turn * RING + s, 1), :, :]
                                 .rearrange("a p n -> (a p) n")).then_inc(landed[s], 16)
            for n in range(NSLAB // RING * RING, NSLAB):
                sp.wait_ge(lo_ready, n + 1 - RING)
                sp.dma_start(raw[:, n % RING, :], stream[n, :, :]).then_inc(landed[n % RING], 16)
            sp.wait_ge(x_ready, X_FINAL)
            sp.dma_start(out, (h32 if STOP is None else x)[:, :, :]).then_inc(out_done, 16)
            sp.wait_ge(out_done, 16)

        @block.scalar
        def _(act):
            own = [0]

            def link(ins):
                ins.then_inc(act_own, 1)
                own[0] += 1
                act.wait_ge(act_own, own[0])

            def split_hi(n, turn=None, per=0):
                if turn is None and n >= NSLAB:
                    return
                s = n % RING
                loads = n // RING + 1
                if turn is None:
                    act.wait_ge(landed[s], 16 * loads)
                    if n >= RING:
                        act.wait_ge(slab_used, n + 1 - RING)
                else:
                    act.wait_ge(landed[s], turn * (16 * per // RING) + 16 * loads)
                    act.wait_ge(slab_used, turn * per + (n + 1 - RING))
                nc.scalar.copy(w_hi[:, s, :], raw[:, s, :]).then_inc(hi_ready, 1)

            def norm(q, x_count):
                if q == 0:
                    act.wait_ge(small_in, 64)
                else:
                    act.wait_ge(x_ready, x_count)
                nc.scalar.activation(sq[:, :, :], x[:, :, :], ACT.Square).then_inc(squares, 1)
                act.wait_ge(sums, q + 1)
                nc.scalar.activation(rstd[:, :], front[:, 0, 0:T], ACT.Sqrt, scale=1.0 / D,
                                     bias=cols[:, COL["eps"]:COL["eps"] + 1]).then_inc(roots, 1)

            def norm_hi(i):
                for half in range(2):
                    act.wait_ge(h32_ready, 2 * i + half + 1)
                    nc.scalar.copy(h_hi[:, 4 * half:4 * half + 4, :],
                                   h32[:, 4 * half:4 * half + 4, :]).then_inc(nh_hi, 1)

            def take(name, i, out, func=ACT.Copy, scale=1.0):
                j = tile_at[name] + i
                act.wait_ge(slab_used, slab_of(name, i) + 1)
                nc.scalar.activation(out, tile_buf(j), func, scale=scale).then_inc(tile_read["act"], 1)

            def take_v(name, i, c, v, width):
                j = tile_at[name] + i
                act.wait_ge(slab_used, slab_of(name, i) + 1)
                nc.scalar.copy(v[:, :, c * P:(c + 1) * P],
                               tile_buf(j).rearrange("p (a n) -> p a n", a=TT)).then_inc(tile_read["act"], 1)

            def mlp(func, n0, steps, fronts_, done):
                per_step = fronts_ + 1

                def step(s, n, turn=None, turns=0):
                    S0 = done + s
                    k = s % 2
                    spt, slt = turns, turns * per_step

                    if fronts_ == 2:
                        split_hi(n + RING, turn, slt)
                    used = n + fronts_
                    act.wait_ge(slab_used, used if turn is None else turn * slt + used)
                    nc.scalar.activation(gate[:, k, :], fronts[:, k, 0:T], func).then_inc(gate_ready, 1)
                    split_hi(n + fronts_ - 1 + RING, turn, slt)
                    act.wait_ge(hid_ready, S0 + 1 if turn is None else turn * spt + (S0 + 1))
                    nc.scalar.copy(mid_hi[:, k, :], hid[:, k, :]).then_inc(mid_hi_ready, 1)

                step(0, n0)
                n = n0 + fronts_
                turns = 4 if fronts_ == 2 else 2
                loops = (steps - 1) // turns
                with act.Fori(0, loops) as turn:
                    for c in range(turns):
                        step(1 + c, n + c * per_step, turn, turns)
                        split_hi(n + c * per_step + fronts_ + RING, turn, turns * per_step)
                for s in range(1 + loops * turns, steps):
                    m = n + (s - 1) * per_step
                    step(s, m)
                    split_hi(m + fronts_ + RING)
                split_hi(n0 + steps * per_step - 1 + RING)

            norm(0, 0)
            for n in range(RING):
                split_hi(n)
            norm_hi(0)

            act.wait_ge(lb_diff, 1)
            nc.scalar.activation(lbw[:, 3:5, :], lbw[:, 1:3, :], ACT.Exp).then_inc(lb_exp, 1)
            n = first["w_in"]
            for i in range(44):
                if i < 4:
                    take("w_in", i, kk[:, i, :], ACT.Sigmoid)
                elif i < 8:
                    take("w_in", i, qq[:, i - 4, :], ACT.Silu)
                elif i < 12:
                    take_v("w_in", i, i - 8, vv, 512)
                elif i < 16:
                    take("w_in", i, hgs[:, i - 12, :], ACT.Silu)
                elif i < 20:
                    take("w_in", i, cc[:, i - 16, :])
                elif i >= 28:
                    take("w_in", i, sg[:, i - 28, :], ACT.Sigmoid)
                else:
                    act.wait_ge(slab_used, n + i + 1)
                split_hi(n + i + RING)
            act.wait_ge(forget_ready, 1)
            nc.scalar.activation(lf[:, :, :], lf[:, :, :], ACT.Ln).then_inc(logf_ready, 1)
            for l in range(8):
                act.wait_ge(level_diff, l + 1)
                nc.scalar.activation(X[:, l % 2, :, :], X[:, l % 2, :, :], ACT.Exp).then_inc(level_exp, 1)
            act.wait_ge(o_done, 1)
            nc.scalar.activation(osq[:, :, :], fronts.rearrange("p b (a t) -> p (b a) t", a=2),
                                 ACT.Square).then_inc(o_sq, 1)
            act.wait_ge(o_sum, 1)
            nc.scalar.activation(orr[:, :, :], acc[:, 0:4, :], ACT.Sqrt, scale=1.0 / DH,
                                 bias=cols[:, COL["eps"]:COL["eps"] + 1]).then_inc(o_root, 1)
            for half in (1, 0):
                if half:
                    act.wait_ge(tile_read["dve"], reads("dve", tile_at["w_in"] + 27))
                else:
                    act.wait_ge(y32_ready, 1)
                nc.scalar.copy(y_hi[:, 4 * half:4 * half + 4, :],
                               y32[:, 4 * half:4 * half + 4, :]).then_inc(y_hi_ready, 1)
            n = first["branch"]
            for m in range(8):
                act.wait_ge(slab_used, n + m + 1)
                split_hi(n + m + RING)
                act.wait_ge(merged_ready, m + 1)
                nc.scalar.copy(h_hi[:, m, :], h32[:, m, :]).then_inc(merged_hi, 1)
            n = first["w_out"]
            for m in range(8):
                act.wait_ge(slab_used, n + m + 1)
                split_hi(n + m + RING)
            if "peer" in first:
                norm(1, 1)
                act.wait_ge(y_lo_ready, 2)
                nc.scalar.dma_start(keysT[:, :, :], keys_in).then_inc(keys_in_sem, 16)
                norm_hi(1)
                n = first["wquery"]
                for i in range(16):
                    take("wquery", i, qT[:, i, :])
                    split_hi(n + i + RING)
                act.wait_ge(gate_diff, 1)
                nc.scalar.activation(gts[:, :, :, :], gts[:, :, :, :], ACT.Exp).then_inc(gate_exp, 1)
                act.wait_ge(picks_turned, 1)
                for i, to in enumerate((idx1_T, idx2_T, gate_T)):
                    nc.scalar.copy(to[:, :], tile[:, i, :]).then_inc(picks_copied, 1)
                act.wait_ge(x_seeded, 1)
                with act.Fori(0, T // 16) as turn:
                    for b in range(4):
                        act.wait_ge(pick_used, turn * 16 + 4 * b + 4)
                        src = (fronts[:, b, :] if b < 2
                               else tile[:, 2 * b - 4:2 * b - 2, :].rearrange("p a t -> p (a t)"))
                        nc.scalar.copy(G[:, bass.ds(turn * 16 + 4 * b, 4), :],
                                       src.rearrange("p (t j) -> p t j", t=4)).then_inc(g_copied, 1)
                act.wait_ge(pick_used, T)
                mlp(ACT.Gelu, first["peer"], NKEYS, 1, 0)
                norm(2, 2)
            stage_norm = 2
            done = NKEYS
            x_count = 3
            attc_loaded = False
            for kind, i in layer_stages():
                norm(stage_norm + 1, x_count)
                if not attc_loaded:
                    attc_loaded = True
                    nc.scalar.dma_start(attc[:, :], attc_in).then_inc(attc_sem, 16)
                    nc.scalar.dma_start(wpool[:, :, :], wpool_in).then_inc(attc_sem, 16)
                norm_hi(stage_norm)
                stage_norm += 1
                x_count += 1
                if kind == "ffn":
                    mlp(ACT.Silu, first[f"ffn{i}"], FT, 2, done)
                    done += FT
                elif kind == "even":
                    n = first["even_in"]
                    for i in range(16):
                        if i < 4:
                            take("even_in", i, aq[:, i, :])
                        elif i < 8:
                            take("even_in", i, ak[:, i - 4, :])
                        elif i < 12:
                            take_v("even_in", i, i - 8, av, 512)
                        else:
                            if i == 12:
                                act.wait_ge(u_ready, 1)
                            take("even_in", i, pu[:, i - 12, PAD:PAD + T])
                        split_hi(n + i + RING)
                    for h in range(HEADS):
                        act.wait_ge(z_done, h + 1)
                        nc.scalar.activation(az[:, h, :], banks[:, h % 4, 0:3 * P], ACT.Copy,
                                             scale=SCALE).then_inc(z_read, 1)
                    for g in range(2):
                        a, b = 4 * g, 4 * g + 4
                        act.wait_ge(z_read, b)
                        link(nc.scalar.activation(asp[:, a:b, :], az[:, a:b, :], ACT.Abs))
                        link(nc.scalar.activation(asp[:, a:b, :], asp[:, a:b, :], ACT.Exp, scale=-1.0))
                        nc.scalar.activation(asp[:, a:b, :], asp[:, a:b, :], ACT.Ln, bias=1.0)\
                            .then_inc(ln_ready, 1)
                    for g in range(2):
                        a, b = 4 * g, 4 * g + 4
                        act.wait_ge(stick_w, b)
                        nc.scalar.activation(az[:, a:b, :], az[:, a:b, :], ACT.Exp).then_inc(stick_e, 1)
                    act.wait_ge(ao_done, 1)
                    nc.scalar.copy(y32[:, 0:4, :], fronts.rearrange("p b (a t) -> p (b a) t", a=2))\
                        .then_inc(act_own, 1)
                    own[0] += 1
                    act.wait_ge(act_own, own[0])
                    nc.scalar.copy(y_hi[:, 0:4, :], y32[:, 0:4, :]).then_inc(y_hi_ready, 1)
                    act.wait_ge(tile_read["dve"], reads("dve", tile_at["pooled"] + 3))
                    nc.scalar.copy(y_hi[:, 4:8, :], y32[:, 4:8, :]).then_inc(y_hi_ready, 1)
                    n = first["even_out"]
                    for m in range(8):
                        act.wait_ge(slab_used, n + m + 1)
                        split_hi(n + m + RING)
                else:
                    n = first["qkv"]
                    for i in range(24):
                        if i < 8:
                            take("qkv", i, bq[:, i, :], scale=SCALE)
                        elif i < 16:
                            take("qkv", i, bk[:, i - 8, :])
                        else:
                            take_v("qkv", i, i - 16, bv, D)
                        split_hi(n + i + RING)

                    def take_heads(half):
                        act.wait_ge(bo_done, 8 * half + 8)
                        link(nc.scalar.copy(y32[:, 4 * half:4 * half + 4, :], tile[:, :, :]))
                        nc.scalar.copy(y_hi[:, 4 * half:4 * half + 4, :],
                                       y32[:, 4 * half:4 * half + 4, :]).then_inc(y_hi_ready, 1)

                    for h in range(ODD_HEADS + 1):
                        if h < ODD_HEADS:
                            k = h % 2
                            act.wait_ge(sc_read, h + 1)
                            nc.scalar.activation(sc[:, k, 0:P], sc[:, k, 0:P], ACT.Exp,
                                                 bias=st[:, 0, k, 0:1], accum_out=st[:, 1, k, 0:1])\
                                .then_inc(p_exp, 1)
                            nc.scalar.activation(sc[:, k, P:3 * P], sc[:, k, P:3 * P], ACT.Exp,
                                                 bias=st[:, 0, k, 1:2], accum_out=st[:, 1, k, 1:2])\
                                .then_inc(p_exp, 1)
                        if h >= 1:
                            act.wait_ge(p_turned, h)
                            if h >= 3:
                                act.wait_ge(bo_done, h - 2)
                            nc.scalar.copy(pT[:, (h - 1) % 2, :], fronts[:, (h - 1) % 2, 0:3 * P])\
                                .then_inc(p_copied, 1)
                        if h == 10:
                            take_heads(0)
                    take_heads(1)
                    n = first["w_o"]
                    for m in range(8):
                        act.wait_ge(slab_used, n + m + 1)
                        split_hi(n + m + RING)
            if STOP is None:
                norm(stage_norm + 1, x_count)

        @block.vector
        def _(dve):
            own = [0]

            def link(ins):
                ins.then_inc(dve_own, 1)
                own[0] += 1
                dve.wait_ge(dve_own, own[0])

            def split_lo(n, turn=None, per=0):
                if turn is None and n >= NSLAB:
                    return
                s = n % RING
                dve.wait_ge(hi_ready, n + 1 if turn is None else turn * per + (n + 1))
                nc.vector.tensor_tensor(w_lo[:, s, :], raw[:, s, :], w_hi[:, s, :].bitcast(F32),
                                        ALU.subtract).then_inc(lo_ready, 1)

            def col(name, i=0):
                return cols[:, COL[name] + i:COL[name] + i + 1]

            def norm_scale(q, gain, to, after=None):
                dve.wait_ge(roots, q + 1)
                link(nc.vector.reciprocal(rstd[:, :], rstd[:, :]))
                for k in range(KT):
                    ins = nc.vector.scalar_tensor_tensor(to[:, k, :], x[:, k, :], col(gain, k), rstd[:, :],
                                                         ALU.mult, ALU.mult)
                    if after is None:
                        ins.then_inc(dve_own, 1)
                        own[0] += 1
                    elif k % 4 == 3:
                        ins.then_inc(after, 1)

            def norm(q, i, gain):
                norm_scale(q, gain, h32, h32_ready)
                for half in range(2):
                    dve.wait_ge(nh_hi, 2 * i + half + 1)
                    nc.vector.tensor_tensor(h_lo[:, 4 * half:4 * half + 4, :],
                                            h32[:, 4 * half:4 * half + 4, :],
                                            h_hi[:, 4 * half:4 * half + 4, :].bitcast(F32),
                                            ALU.subtract).then_inc(nh_lo, 1)

            def y_low(count, a, b):
                dve.wait_ge(y_hi_ready, count)
                nc.vector.tensor_tensor(y_lo[:, a:b, :], y32[:, a:b, :], y_hi[:, a:b, :].bitcast(F32),
                                        ALU.subtract).then_inc(y_lo_ready, 1)

            def mlp(n0, steps, fronts_, done):
                per_step = fronts_ + 1

                def step(s, n, turn=None, turns=0):
                    S0 = done + s
                    k = s % 2
                    spt, slt = turns, turns * per_step

                    def wait(sm, v):
                        dve.wait_ge(sm, v if turn is None else turn * spt + v)
                    if fronts_ == 2:
                        split_lo(n + RING, turn, slt)
                    wait(gate_ready, S0 + 1)
                    if fronts_ == 2:
                        other = fronts[:, k, T:2 * T]
                    else:
                        other = (G[:, :, s] if turn is None
                                 else G[:, :, bass.ds(turn * turns + s, 1)].rearrange("p t a -> p (t a)"))
                    nc.vector.tensor_tensor(hid[:, k, :], gate[:, k, :], other, ALU.mult)\
                        .then_inc(hid_ready, 1)
                    split_lo(n + fronts_ - 1 + RING, turn, slt)
                    wait(mid_hi_ready, S0 + 1)
                    nc.vector.tensor_tensor(mid_lo[:, k, :], hid[:, k, :], mid_hi[:, k, :].bitcast(F32),
                                            ALU.subtract).then_inc(mid_lo_ready, 1)

                step(0, n0)
                n = n0 + fronts_
                turns = 4 if fronts_ == 2 else 2
                loops = (steps - 1) // turns
                with dve.Fori(0, loops) as turn:
                    for c in range(turns):
                        step(1 + c, n + c * per_step, turn, turns)
                        split_lo(n + c * per_step + fronts_ + RING, turn, turns * per_step)
                for s in range(1 + loops * turns, steps):
                    m = n + (s - 1) * per_step
                    step(s, m)
                    split_lo(m + fronts_ + RING)
                split_lo(n0 + steps * per_step - 1 + RING)

            def add_tile(name, m):
                j = tile_at[name] + m
                dve.wait_ge(slab_used, slab_of(name, m) + 1)
                nc.vector.tensor_tensor(x[:, m, :], tile_buf(j), x[:, m, :], ALU.add)\
                    .then_inc(tile_read["dve"], 1)

            dve.wait_ge(small_in, 64)
            link(nc.vector.tensor_tensor(lbw[:, 0, :], cols[:, COL["lb0"]:COL["lb0"] + 4],
                                         cols[:, COL["lb1"]:COL["lb1"] + 4], ALU.max))
            nc.vector.tensor_tensor(lbw[:, 1, :], cols[:, COL["lb0"]:COL["lb0"] + 4], lbw[:, 0, :],
                                    ALU.subtract)
            nc.vector.tensor_tensor(lbw[:, 2, :], cols[:, COL["lb1"]:COL["lb1"] + 4], lbw[:, 0, :],
                                    ALU.subtract).then_inc(lb_diff, 1)
            nc.vector.memset(uu[:, :, 0:2], 0.0)
            norm_scale(0, "norm_mix_g", h32, h32_ready)
            for n in range(RING):
                split_lo(n)
            for half in range(2):
                dve.wait_ge(nh_hi, half + 1)
                nc.vector.tensor_tensor(h_lo[:, 4 * half:4 * half + 4, :], h32[:, 4 * half:4 * half + 4, :],
                                        h_hi[:, 4 * half:4 * half + 4, :].bitcast(F32),
                                        ALU.subtract).then_inc(nh_lo, 1)
            dve.wait_ge(lb_exp, 1)
            link(nc.vector.tensor_tensor(lbw[:, 5, :], lbw[:, 3, :], lbw[:, 4, :], ALU.add))
            link(nc.vector.reciprocal(lbw[:, 5, :], lbw[:, 5, :]))
            link(nc.vector.tensor_tensor(lbw[:, 6, :], lbw[:, 3, :], lbw[:, 5, :], ALU.mult))
            link(nc.vector.tensor_scalar(lbw[:, 7, :], lbw[:, 6, :], -1.0, 1.0, ALU.mult, ALU.add))

            n = first["w_in"]
            j0 = tile_at["w_in"]
            for i in range(44):
                if i < 4:
                    dve.wait_ge(tile_read["act"], reads("act", j0 + i))
                    ins = nc.vector.tensor_scalar(lf[:, i, :], kk[:, i, :], lbw[:, 7, i:i + 1],
                                                  lbw[:, 6, i:i + 1], ALU.mult, ALU.add)
                    link(ins)
                    ins = nc.vector.tensor_scalar(kk[:, i, :], lf[:, i, :], -1.0, 1.0, ALU.mult, ALU.add)
                    if i == 3:
                        ins.then_inc(forget_ready, 1)
                elif i < 8:
                    dve.wait_ge(tile_read["act"], reads("act", j0 + i))
                    nc.vector.tensor_scalar(qq[:, i - 4, :], qq[:, i - 4, :], SCALE, None, ALU.mult)
                elif 20 <= i < 24:
                    dve.wait_ge(slab_used, n + i + 1)
                    c = i - 20
                    dve.wait_ge(tile_read["act"], reads("act", j0 + 19))
                    nc.vector.tensor_tensor(uu[:, c, 2:T + 2], tile_buf(j0 + i), cc[:, c, :],
                                            ALU.mult).then_inc(tile_read["dve"], 1)
                    dve.wait_ge(tile_read["dve"], reads("dve", j0 + i))
                    link(nc.vector.tensor_scalar(conv[:, c, :], uu[:, c, 0:T], col("conv", c), None, ALU.mult))
                    for tap in (1, 2):
                        link(nc.vector.scalar_tensor_tensor(conv[:, c, :], uu[:, c, tap:tap + T],
                                                            col("conv", 4 * tap + c), conv[:, c, :],
                                                            ALU.mult, ALU.add))
                elif 24 <= i < 28:
                    c = i - 24
                    dve.wait_ge(slab_used, n + i + 1)
                    nc.vector.tensor_tensor(y32[:, 4 + c, :], tile_buf(j0 + i), conv[:, c, :],
                                            ALU.mult).then_inc(tile_read["dve"], 1)
                split_lo(n + i + RING)

            dve.wait_ge(logf_ready, 1)
            for i in range(4):
                ins = nc.vector.tensor_tensor_scan(bb[:, i, :], chunk_mask, lf[:, i, :], 0.0,
                                                   ALU.mult, ALU.add)
            link(ins)

            def halves(ap, m):
                flat = ap.rearrange("p a t -> p (a t)")
                v = flat.rearrange("p (n h m) -> p n h m", h=2, m=m)
                return v[:, :, 0, :], v[:, :, 1, :]

            seq = LEVELS + [128]

            def level_prepare(l):
                m = seq[l]
                to = X[:, l % 2, :, :]
                if l >= 2:
                    dve.wait_ge(level_done, l)
                if m < CHUNK:
                    b_lo, b_up = halves(bb[:, :, :], m)
                    x_lo, x_up = halves(to, m)
                    ref = b_lo[:, :, m - 1:m].broadcast_to([P, 4 * T // (2 * m), m])
                    nc.vector.tensor_tensor(x_up, b_up, ref, ALU.subtract)
                    nc.vector.tensor_tensor(x_lo, ref, b_lo, ALU.subtract).then_inc(level_diff, 1)
                elif m == CHUNK:
                    b_lo, b_up = halves(bb[:, :, :], m)
                    x_lo, x_up = halves(to, m)
                    ref = b_lo[:, :, m - 1:m].broadcast_to([P, 8, m])
                    nc.vector.tensor_copy(x_up, b_up)
                    nc.vector.tensor_tensor(x_lo, ref, b_lo, ALU.subtract).then_inc(level_diff, 1)
                else:
                    ends = bb[:, :, CHUNK - 1:T:CHUNK]
                    link(nc.vector.tensor_tensor(dec[:, :, 0:1], ends[:, :, 0:1], ends[:, :, 1:2], ALU.add))
                    for c, op, a, b in ((2, None, None, None),
                                        (3, ALU.add, None, ends[:, :, 2:3]),
                                        (1, ALU.subtract, ends[:, :, 1:2], None),
                                        (0, ALU.subtract, dec[:, :, 0:1], None)):
                        o = to[:, :, c * CHUNK:(c + 1) * CHUNK]
                        bc = bb[:, :, c * CHUNK:(c + 1) * CHUNK]
                        if op is None:
                            ins = nc.vector.tensor_copy(o, bc)
                        elif b is not None:
                            ins = nc.vector.tensor_tensor(o, bc, b.broadcast_to([P, 4, CHUNK]), op)
                        else:
                            ins = nc.vector.tensor_tensor(o, a.broadcast_to([P, 4, CHUNK]), bc, op)
                    ins.then_inc(level_diff, 1)

            def level_operands(l):
                m = seq[l]
                dve.wait_ge(level_exp, l + 1)
                to = X[:, l % 2, :, :]
                x_lo, x_up = halves(to, m)
                q_up = halves(qq[:, :, :], m)[1]
                k_lo = halves(kk[:, :, :], m)[0]
                nc.vector.tensor_tensor(x_up, x_up, q_up, ALU.mult)
                nc.vector.tensor_tensor(x_lo, x_lo, k_lo, ALU.mult).then_inc(level_ready, 1)

            def level_pick(l):
                dve.wait_ge(level_done, l + 2)
                if l == len(seq) - 1:
                    nc.vector.tensor_copy(S_off[:, :, :, :],
                                          banks[:, 2:4, :].rearrange("p b (a t) -> p b a t", a=4))\
                        .then_inc(level_read, 1)
                    return
                mask = ident if l < 0 else level_mask[seq[l]]
                for b in range(4):
                    ins = nc.vector.copy_predicated(
                        S[:, b, :, :], mask.bitcast(U32).unsqueeze(1).broadcast_to([P, 4, P]),
                        banks[:, b, :].rearrange("p (a t) -> p a t", a=4))
                ins.then_inc(level_read, 1)

            nc.vector.memset(S[:, :, :, :], 0.0)
            level_prepare(0)
            for l in range(8):
                if l < 7:
                    level_prepare(l + 1)
                level_operands(l)
                level_pick(l - 1)
            level_pick(7)
            y_low(1, 4, 8)
            dve.wait_ge(o_root, 1)
            link(nc.vector.reciprocal(orr[:, :, :], orr[:, :, :]))
            link(nc.vector.tensor_tensor(orr[:, :, :], fronts.rearrange("p b (a t) -> p (b a) t", a=2),
                                         orr[:, :, :], ALU.mult))
            for i in range(4):
                ins = nc.vector.scalar_tensor_tensor(y32[:, i, :], orr[:, i, :], col("out_g", i),
                                                     hgs[:, i, :], ALU.mult, ALU.mult)
            ins.then_inc(y32_ready, 1)
            y_low(2, 0, 4)
            n = first["branch"]
            j0 = tile_at["branch"]
            for m in range(8):
                j = j0 + m
                dve.wait_ge(slab_used, n + m + 1)
                nc.vector.tensor_tensor(h32[:, m, :], tile_buf(j), sg[:, m, :], ALU.mult)
                nc.vector.tensor_tensor(sq[:, m, :], tile_buf(j, 1), sg[:, 8 + m, :], ALU.mult)\
                    .then_inc(tile_read["dve"], 1)
                dve.wait_ge(tile_read["dve"], reads("dve", j))
                nc.vector.tensor_tensor(h32[:, m, :], h32[:, m, :], sq[:, m, :], ALU.add)\
                    .then_inc(merged_ready, 1)
                split_lo(n + m + RING)
                dve.wait_ge(merged_hi, m + 1)
                nc.vector.tensor_tensor(h_lo[:, m, :], h32[:, m, :], h_hi[:, m, :].bitcast(F32),
                                        ALU.subtract).then_inc(merged_lo, 1)
            n = first["w_out"]
            for m in range(8):
                add_tile("w_out", m)
                split_lo(n + m + RING)
            def x_updated():
                dve.wait_ge(tile_read["dve"], x_reads[0])
                dve.sem_inc(x_ready, 1)

            x_reads = [reads("dve", tile_at["w_out"] + 7)]
            x_updated()
            if "peer" in first:
                norm(1, 1, "norm_ffn_g")
                n = first["wquery"]

                def best_keys(i):
                    dve.wait_ge(keys_done, i + 1)
                    for tt in range(TT):
                        s = fronts[:, i % 2, tt * P:(tt + 1) * P]
                        v, ix = top_v[:, tt, i, :], top_i[:, tt, i, :]
                        link(nc.vector.max(v[:, 0:8], s))
                        nc.vector.max_index(ix[:, 0:8], v[:, 0:8], s)
                        link(nc.vector.match_replace(rest[:, :], v[:, 0:8], s, NEG))
                        link(nc.vector.max(v[:, 8:16], rest[:, :]))
                        ins = nc.vector.max_index(ix[:, 8:16], v[:, 8:16], rest[:, :])
                        link(ins)
                    nc.vector.tensor_copy(top_f[:, :, i, :], top_i[:, :, i, :]).then_inc(keys_read, 1)

                for i in range(16):
                    dve.wait_ge(slab_used, n + i + 1)
                    split_lo(n + i + RING)
                    if i >= 1:
                        best_keys(i - 1)
                best_keys(15)
                for tt in range(TT):
                    for h in range(HEADS):
                        k = h % 2
                        c = cand[:, k, :, :]
                        cf = c.rearrange("p a b -> p (a b)")
                        link(nc.vector.tensor_tensor(
                            c, top_v[:, tt, 2 * h, :].unsqueeze(2).broadcast_to([P, TOPK, TOPK]),
                            top_v[:, tt, 2 * h + 1, :].unsqueeze(1).broadcast_to([P, TOPK, TOPK]), ALU.add))
                        v, ix = best[:, tt, h, :], pos[:, tt, h, :]
                        link(nc.vector.max(v[:, 0:8], cf))
                        link(nc.vector.max_index(ix[:, 0:8], v[:, 0:8], cf))
                        link(nc.vector.match_replace(cf, v[:, 0:8], cf, NEG))
                        link(nc.vector.max(v[:, 8:16], cf))
                        link(nc.vector.max_index(ix[:, 8:16], v[:, 8:16], cf))
                nc.vector.tensor_tensor(gts[:, :, :, :], best[:, :, :, :],
                                        best[:, :, :, 0:1].broadcast_to([P, TT, HEADS, TOPK]),
                                        ALU.subtract).then_inc(gate_diff, 1)
                link(nc.vector.tensor_scalar(pos1[:, :, :, :], pos[:, :, :, :], 4, None,
                                             ALU.logical_shift_right))
                link(nc.vector.tensor_scalar(pos2[:, :, :, :], pos[:, :, :, :], 15, None,
                                             ALU.bitwise_and))
                nc.vector.tensor_copy(posf[:, 0, :, :, :], pos1[:, :, :, :])
                link(nc.vector.tensor_copy(posf[:, 1, :, :, :], pos2[:, :, :, :]))
                for side in range(2):
                    for tt in range(TT):
                        flat = onehot[:, :, :, :].rearrange("p h k a -> p (h k) a")
                        link(nc.vector.tensor_tensor(
                            flat, posf[:, side, tt, :, :].rearrange("p h k -> p (h k)").unsqueeze(2)
                            .broadcast_to([P, P, TOPK]),
                            iota[:, 0:TOPK].unsqueeze(1).broadcast_to([P, P, TOPK]), ALU.is_equal))
                        link(nc.vector.tensor_tensor(
                            onehot[:, :, :, :], onehot[:, :, :, :],
                            top_f[:, tt, side:PEER_GROUPS:2, :].unsqueeze(2)
                            .broadcast_to([P, HEADS, TOPK, TOPK]), ALU.mult))
                        link(nc.vector.tensor_reduce(
                            idx[:, side, tt, :, :].rearrange("p h k -> p (h k)"), flat, AX_X, ALU.add))
                dve.wait_ge(gate_exp, 1)
                link(nc.vector.tensor_reduce(gsum[:, :, :, 0], gts[:, :, :, :], AX_X, ALU.add))
                link(nc.vector.reciprocal(gsum[:, :, :, 1], gsum[:, :, :, 0]))
                nc.vector.tensor_tensor(gts[:, :, :, :], gts[:, :, :, :],
                                        gsum[:, :, :, 1:2].broadcast_to([P, TT, HEADS, TOPK]),
                                        ALU.mult).then_inc(picks_ready, 1)
                dve.wait_ge(picks_copied, 3)

                def pick_rows(t, k):
                    nc.vector.tensor_scalar(pick1[:, k, :], iota, idx1_T[:, t], gate_T[:, t],
                                            ALU.is_equal, ALU.mult)
                    nc.vector.tensor_scalar(pick2[:, k, :], iota, idx2_T[:, t], None, ALU.is_equal)\
                        .then_inc(pick_ready, 1)

                for t in range(4):
                    pick_rows(slice(t, t + 1), t)
                with dve.Fori(0, (T - 4) // 4) as turn:
                    for c in range(4):
                        dve.wait_ge(pick_used, turn * 4 + (c + 1))
                        pick_rows(bass.ds(turn * 4 + (c + 4), 1), c)
                dve.wait_ge(g_copied, T // 4)
                dve.wait_ge(pick_used, T)
                mlp(first["peer"], NKEYS, 1, 0)
                dve.wait_ge(slab_used, first["peer"] + 2 * NKEYS)
                ins = nc.vector.tensor_copy(x[:, :, :], acc[:, :, :])
                ins.then_inc(x_ready, 1)
                norm_scale(2, "norm_final_g", x)
                dve.wait_ge(dve_own, own[0])
                dve.sem_inc(x_ready, 1)
            done = NKEYS
            i_norm = 2
            ys = 2
            for kind, i in layer_stages():
                gain = FFN_GAIN[i] if kind == "ffn" else {"even": "norm_mix_0", "odd": "norm_mix_1"}[kind]
                norm(i_norm + 1, i_norm, gain)
                i_norm += 1
                if kind == "ffn":
                    mlp(first[f"ffn{i}"], FT, 2, done)
                    done += FT
                    dve.wait_ge(slab_used, first[f"ffn{i}"] + 3 * FT)
                    for b in range(4):
                        ins = nc.vector.scalar_tensor_tensor(x[:, 2 * b:2 * b + 2, :],
                                                             acc[:, 2 * b:2 * b + 2, :], 0.5,
                                                             x[:, 2 * b:2 * b + 2, :], ALU.mult, ALU.add)
                    ins.then_inc(x_ready, 1)
                elif kind == "even":
                    dve.wait_ge(attc_sem, 32)
                    dve.wait_ge(nh_lo, 2 * i_norm)
                    nc.vector.memset(pu[:, :, 0:PAD], 0.0).then_inc(u_ready, 1)
                    nc.vector.memset(win[:, :, 0:PAD], 0.0)
                    n = first["even_in"]
                    for i in range(16):
                        dve.wait_ge(slab_used, n + i + 1)
                        split_lo(n + i + RING)
                    j0 = tile_at["even_in"]
                    dve.wait_ge(tile_read["act"], reads("act", j0 + 15))
                    for g, w in enumerate(WINDOWS):
                        src = pu[:, g, :]
                        if g:
                            dve.wait_ge(pooled_ready, g)
                        for r in range(g + 1):
                            to = win[:, r % 2, :]
                            link(nc.vector.tensor_tensor(to[:, PAD:], src[:, PAD:],
                                                         src[:, PAD - 2 ** r:PAD - 2 ** r + T], ALU.add))
                            src = to
                        link(nc.vector.tensor_tensor(src[:, PAD:], src[:, PAD:], inv_count[:, g, :],
                                                     ALU.mult))
                        nc.vector.tensor_tensor(pooled[:, g, :], src[:, PAD:], pu[:, g, PAD:],
                                                ALU.subtract).then_inc(pooled_ready, 1)
                    for g in range(2):
                        a, b = 4 * g, 4 * g + 4
                        dve.wait_ge(ln_ready, g + 1)
                        link(nc.vector.scalar_tensor_tensor(asp[:, a:b, :], az[:, a:b, :], 0.0,
                                                            asp[:, a:b, :], ALU.max, ALU.add))
                        nc.vector.tensor_tensor(aL[:, a:b, :], asp[:, a:b, :],
                                                past_neg.unsqueeze(1).broadcast_to([P, 4, 3 * P]),
                                                ALU.mult).then_inc(stick_L, 1)
                        link(nc.vector.tensor_tensor(az[:, a:b, :], az[:, a:b, :], asp[:, a:b, :],
                                                     ALU.subtract))
                    for h in range(HEADS):
                        dve.wait_ge(later_done, h + 1)
                        nc.vector.tensor_tensor(az[:, h, :], banks[:, h % 4, 0:3 * P], az[:, h, :],
                                                ALU.add).then_inc(stick_w, 1)
                    for g in range(2):
                        a, b = 4 * g, 4 * g + 4
                        dve.wait_ge(stick_e, g + 1)
                        nc.vector.scalar_tensor_tensor(az[:, a:b, :], az[:, a:b, :], -1.0,
                                                       past_neg.unsqueeze(1).broadcast_to([P, 4, 3 * P]),
                                                       ALU.mult, ALU.mult).then_inc(stick_a, 1)
                    dve.wait_ge(pool_done, 4)
                    for g in range(4):
                        nc.vector.tensor_scalar(y32[:, 4 + g, :], tile[:, g, :],
                                                col("pool_scale", g), None, ALU.mult)\
                            .then_inc(tile_read["dve"], 1)
                    y_low(ys + 1, 0, 4)
                    y_low(ys + 2, 4, 8)
                    ys += 2
                    n = first["even_out"]
                    for m in range(8):
                        add_tile("even_out", m)
                        split_lo(n + m + RING)
                    x_reads[0] = reads("dve", tile_at["even_out"] + 7)
                    x_updated()
                else:
                    n = first["qkv"]
                    for i in range(24):
                        dve.wait_ge(slab_used, n + i + 1)
                        split_lo(n + i + RING)
                    for h in range(ODD_HEADS + 1):
                        if h < ODD_HEADS:
                            k = h % 2
                            slope = float(2.0 ** (-8.0 * (h + 1) / ODD_HEADS))
                            dve.wait_ge(sc_done, h + 1)
                            if h >= 2:
                                dve.wait_ge(p_turned, h - 1)
                            link(nc.vector.scalar_tensor_tensor(sc[:, k, :], dist, slope,
                                                                banks[:, h % 4, 0:3 * P],
                                                                ALU.mult, ALU.add))
                            nc.vector.tensor_reduce(st[:, 0, k, 0:1], sc[:, k, 0:P], AX_X, ALU.max,
                                                    negate=True)
                            nc.vector.tensor_reduce(st[:, 0, k, 1:2], sc[:, k, P:3 * P], AX_X, ALU.max,
                                                    negate=True).then_inc(sc_read, 1)
                        if h >= 1:
                            k = (h - 1) % 2
                            dve.wait_ge(p_exp, 2 * h)
                            link(nc.vector.reciprocal(st[:, 2, k, :], st[:, 1, k, :]))
                            nc.vector.tensor_scalar(sc[:, k, 0:P], sc[:, k, 0:P], st[:, 2, k, 0:1], None,
                                                    ALU.mult)
                            nc.vector.tensor_scalar(sc[:, k, P:3 * P], sc[:, k, P:3 * P],
                                                    st[:, 2, k, 1:2], None, ALU.mult).then_inc(p_norm, 1)
                    y_low(ys + 1, 0, 4)
                    y_low(ys + 2, 4, 8)
                    ys += 2
                    n = first["w_o"]
                    for m in range(8):
                        add_tile("w_o", m)
                        split_lo(n + m + RING)
                    x_reads[0] = reads("dve", tile_at["w_o"] + 7)
                    x_updated()
            if STOP is None:
                norm_scale(i_norm + 1, "norm_final", h32)
                dve.wait_ge(dve_own, own[0])
                dve.sem_inc(x_ready, 1)

        @block.tensor
        def _(pe):
            def mm(out, lhsT, rhs, start, stop, **kw):
                return nc.tensor.matmul(out, lhsT, rhs, start=start, stop=stop, **kw)

            def wait_slab(n, turn=None, per=0):
                pe.wait_ge(lo_ready, n + 1 if turn is None else turn * per + (n + 1))

            def three(out, s, c, r_hi, r_lo, start, stop, **kw):
                hi, lo = w_hi[:, s, c:c + P], w_lo[:, s, c:c + P]
                mm(out, hi, r_hi, start, False, **kw)
                mm(out, hi, r_lo, False, False, **kw)
                return mm(out, lo, r_hi, False, stop, **kw)

            def free_tile(j):
                if j >= 2:
                    r = readers[j - 2]
                    pe.wait_ge(tile_read[r], reads(r, j - 2))

            def project(name, i, n, hi, lo):
                j = tile_at[name] + i
                free_tile(j)
                wait_slab(n)
                for k in range(KT):
                    ins = three(tile_buf(j), n % RING, k * P, hi[:, k, :], lo[:, k, :],
                                k == 0, k == KT - 1)
                ins.then_inc(slab_used, 1)

            def project_tokens(name, i, n, hi, lo):
                j = tile_at[name] + i
                free_tile(j)
                wait_slab(n)
                s = n % RING
                for tt in range(TT):
                    o = tile_buf(j)[:, tt * P:(tt + 1) * P]
                    for k in range(KT):
                        a, b = hi[:, k, tt * P:(tt + 1) * P], lo[:, k, tt * P:(tt + 1) * P]
                        c = slice(k * P, (k + 1) * P)
                        mm(o, a, w_hi[:, s, c], k == 0, False)
                        mm(o, b, w_hi[:, s, c], False, False)
                        ins = mm(o, a, w_lo[:, s, c], False, k == KT - 1)
                ins.then_inc(slab_used, 1)

            def norm(q):
                pe.wait_ge(squares, q + 1)
                for k in range(KT):
                    ins = mm(front[:, 0, 0:T], ones, sq[:, k, :], k == 0, k == KT - 1)
                ins.then_inc(sums, 1)

            def mlp(n0, steps, fronts_, done, seeded):
                per_step = fronts_ + 1

                def wait(turn, turns, sm, v):
                    if turn is None:
                        pe.wait_ge(sm, v)
                    else:
                        pe.wait_ge(sm, turn * turns + v)

                def feed(s, n, turn=None, turns=0):
                    S0 = done + s
                    if s >= 2 or turn is not None:
                        wait(turn, turns, hid_ready, S0 - 1)
                    for f in range(fronts_):
                        wait_slab(n + f, turn, turns * per_step)
                        for k in range(KT):
                            ins = three(fronts[:, s % 2, f * T:(f + 1) * T], (n + f) % RING, k * P,
                                        h_hi[:, k, :], h_lo[:, k, :], k == 0, k == KT - 1)
                        ins.then_inc(slab_used, 1)

                def drain(s, n, turn=None, turns=0):
                    S0 = done + s
                    wait(turn, turns, mid_lo_ready, S0 + 1)
                    wait_slab(n, turn, turns * per_step)
                    begin = s == 0 and not seeded and turn is None
                    for m in range(KT):
                        ins = three(acc[:, m, :], n % RING, m * P, mid_hi[:, s % 2, :], mid_lo[:, s % 2, :],
                                    begin and m % 2 == 0, False, skip_group_check=True)
                    ins.then_inc(slab_used, 1)

                feed(0, n0)
                n = n0 + fronts_
                turns = 4 if fronts_ == 2 else 2
                feed(1, n)
                drain(0, n + fronts_)
                n += per_step
                loops = (steps - 2) // turns
                with pe.Fori(0, loops) as turn:
                    for c in range(turns):
                        feed(2 + c, n + c * per_step, turn, turns)
                        drain(1 + c, n + c * per_step + fronts_, turn, turns)
                for s in range(2 + loops * turns, steps):
                    m = n + (s - 2) * per_step
                    feed(s, m)
                    drain(s - 1, m + fronts_)
                drain(steps - 1, n0 + steps * per_step - 1)

            norm(0)
            pe.wait_ge(nh_lo, 2)
            n = first["w_in"]
            for i in range(44):
                (project_tokens if 8 <= i < 12 else project)("w_in", i, n + i, h_hi, h_lo)
            def head(ap, h, tt):
                p = DH * (h % 2)
                return ap[p:p + DH, h // 2, tt * P:(tt + 1) * P]

            for l in range(-1, 8):
                if l >= 0:
                    pe.wait_ge(level_ready, l + 1)
                    pe.wait_ge(level_read, l + 1)
                else:
                    pe.wait_ge(forget_ready, 1)
                    pe.wait_ge(level_diff, 1)
                for tt in range(TT):
                    if l == 7 and tt == 0:
                        continue
                    for h in range(HEADS):
                        if l < 0:
                            a, b = head(kk, h, tt), head(qq, h, tt)
                        else:
                            a = head(X[:, l % 2, :, :], h, tt if l < 7 else 0)
                            b = head(X[:, l % 2, :, :], h, tt)
                        o = banks[:, 2 * tt + h % 2, (h // 2) * P:(h // 2 + 1) * P]
                        ins = mm(o, a, b, True, True)
                ins.then_inc(level_done, 1)
            pe.wait_ge(level_read, 9)

            def outputs(v, h, to, scores):
                p = DH * (h % 2)
                w = [v[:, tt, h * DH:(h + 1) * DH] for tt in range(TT)]
                o = to[p:p + DH, :]
                mm(o[:, 0:P], w[0], scores[0], True, True)
                mm(o[:, P:T], w[0], scores[1], True, False)
                return mm(o[:, P:T], w[1], scores[2], False, True)

            fr = fronts.rearrange("p b (a t) -> p (b a) t", a=2)
            pe.wait_ge(tile_read["act"], reads("act", tile_at["w_in"] + 43))
            for h in range(HEADS):
                ins = outputs(vv, h, fr[:, h // 2, :],
                              (S[:, h % 2, h // 2, :], S_off[:, h % 2, h // 2, :], S[:, 2 + h % 2, h // 2, :]))
            ins.then_inc(o_done, 1)
            pe.wait_ge(o_sq, 1)
            for b in range(2):
                ins = mm(banks[:, b, :], head_ones, osq[:, 2 * b:2 * b + 2, :].rearrange("p a t -> p (a t)"),
                         True, True)
            ins.then_inc(o_sum, 1)
            pe.wait_ge(y_lo_ready, 2)
            n = first["branch"]
            for m in range(8):
                wait_slab(n + m)
                j = tile_at["branch"] + m
                free_tile(j)
                for half in range(2):
                    for k in range(4):
                        kk_ = 4 * half + k
                        ins = three(tile_buf(j, half), (n + m) % RING, kk_ * P, y_hi[:, kk_, :],
                                    y_lo[:, kk_, :], k == 0, k == 3)
                ins.then_inc(slab_used, 1)
            pe.wait_ge(merged_lo, 8)
            n = first["w_out"]
            for m in range(8):
                project("w_out", m, n + m, h_hi, h_lo)
            if "peer" in first:
                norm(1)
                for m in range(KT):
                    ins = mm(acc[:, m, :], ident, x[:, m, :], m % 2 == 0, False, skip_group_check=True)
                ins.then_inc(x_seeded, 1)
                pe.wait_ge(nh_lo, 4)
                pe.wait_ge(keys_in_sem, 16)
                n = first["wquery"]

                def key_scores(i):
                    j = tile_at["wquery"] + i
                    pe.wait_ge(tile_read["act"], reads("act", j))
                    if i >= 2:
                        pe.wait_ge(keys_read, i - 1)
                    for tt in range(TT):
                        ins = mm(fronts[:, i % 2, tt * P:(tt + 1) * P], qT[:, i, tt * P:(tt + 1) * P],
                                 keysT[:, i, :], True, True)
                    ins.then_inc(keys_done, 1)

                for i in range(16):
                    project("wquery", i, n + i, h_hi, h_lo)
                    if i >= 1:
                        key_scores(i - 1)
                key_scores(15)
                pe.wait_ge(picks_ready, 1)
                for i in range(3):
                    for tt in range(TT):
                        src = gts[:, tt, :, :] if i == 2 else idx[:, i, tt, :, :]
                        ins = nc.tensor.transpose(tile[:, i, tt * P:(tt + 1) * P],
                                                  src.rearrange("p h k -> p (h k)"), ident)
                ins.then_inc(picks_turned, 1)
                def weights(b, c, k):
                    if b < 2:
                        o = fronts[:, b, c * P:(c + 1) * P]
                    else:
                        o = tile[:, 2 * b - 4 + c // 2, (c % 2) * P:(c % 2 + 1) * P]
                    mm(o, pick1[:, k, :], pick2[:, k, :], True, True).then_inc(pick_used, 1)

                pe.wait_ge(picks_copied, 3)
                for t in range(16):
                    pe.wait_ge(pick_ready, t + 1)
                    weights(t // 4, t % 4, t % 4)
                with pe.Fori(0, T // 16 - 1) as turn:
                    for b in range(4):
                        pe.wait_ge(g_copied, turn * 4 + (b + 1))
                        for c in range(4):
                            pe.wait_ge(pick_ready, turn * 16 + (16 + 4 * b + c + 1))
                            weights(b, c, c)
                pe.wait_ge(g_copied, T // 4)
                mlp(first["peer"], NKEYS, 1, 0, True)
                norm(2)
            done = NKEYS
            q = 3
            lows = 4
            ys = 2
            for kind, i in layer_stages():
                norm(q)
                q += 1
                lows += 2
                pe.wait_ge(nh_lo, lows)
                if kind == "ffn":
                    mlp(first[f"ffn{i}"], FT, 2, done, False)
                    done += FT
                elif kind == "even":
                    n = first["even_in"]
                    for i in range(16):
                        (project_tokens if 8 <= i < 12 else project)("even_in", i, n + i, h_hi, h_lo)
                    for h in range(HEADS):
                        p = DH * (h % 2)
                        if h == 0:
                            pe.wait_ge(tile_read["act"], reads("act", tile_at["even_in"] + 15))
                        if h >= 4:
                            pe.wait_ge(z_read, h - 3)
                        k_ = ak[p:p + DH, h // 2, :]
                        q_ = aq[p:p + DH, h // 2, :]
                        mm(banks[:, h % 4, 0:T], k_[:, 0:P], q_, True, True)
                        mm(banks[:, h % 4, T:T + P], k_[:, P:T], q_[:, P:T], True, True)\
                            .then_inc(z_done, 1)
                    for g in range(4):
                        pe.wait_ge(pooled_ready, g + 1)
                        mm(tile[:, g, :], wpool[:, g, :], pooled[:, g, :], True, True)\
                            .then_inc(pool_done, 1)
                    for h in range(HEADS):
                        pe.wait_ge(stick_L, h // 4 + 1)
                        if h < 4:
                            pe.wait_ge(z_read, 8)
                        else:
                            pe.wait_ge(stick_w, h - 3)
                        o = banks[:, h % 4, 0:3 * P]
                        mm(o, later, aL[:, h, :], True, True)
                        mm(o[:, P:2 * P], ones, aL[:, h, 2 * P:3 * P], False, True, skip_group_check=True)\
                            .then_inc(later_done, 1)
                    for h in range(HEADS):
                        pe.wait_ge(stick_a, h // 4 + 1)
                        ins = outputs(av, h, fr[:, h // 2, :], [az[:, h, c * P:(c + 1) * P] for c in range(3)])
                    ins.then_inc(ao_done, 1)
                    pe.wait_ge(y_lo_ready, ys + 2)
                    ys += 2
                    n = first["even_out"]
                    for m in range(8):
                        project("even_out", m, n + m, y_hi, y_lo)
                else:
                    n = first["qkv"]
                    for i in range(24):
                        (project_tokens if i >= 16 else project)("qkv", i, n + i, h_hi, h_lo)
                    pe.wait_ge(tile_read["act"], reads("act", tile_at["qkv"] + 23))
                    for h in range(ODD_HEADS + 2):
                        if h < ODD_HEADS:
                            p = DH * (h % 2)
                            if h >= 4:
                                pe.wait_ge(sc_read, h - 3)
                            k_ = bk[p:p + DH, h // 2, :]
                            q_ = bq[p:p + DH, h // 2, :]
                            mm(banks[:, h % 4, 0:P], q_[:, 0:P], k_[:, 0:P], True, True)
                            mm(banks[:, h % 4, P:3 * P], q_[:, P:T], k_, True, True).then_inc(sc_done, 1)
                        if 1 <= h <= ODD_HEADS:
                            g = h - 1
                            pe.wait_ge(p_norm, g + 1)
                            if g >= 2:
                                pe.wait_ge(p_copied, g - 1)
                            o = fronts[:, g % 2, :]
                            nc.tensor.transpose(o[:, 0:P], sc[:, g % 2, 0:P], ident2)
                            nc.tensor.transpose(o[:, P:2 * P], sc[:, g % 2, P:2 * P], ident2)
                            nc.tensor.transpose(o[:, 2 * P:3 * P], sc[:, g % 2, 2 * P:3 * P], ident2)\
                                .then_inc(p_turned, 1)
                        if h >= 2:
                            g = h - 2
                            pe.wait_ge(p_copied, g + 1)
                            if g == 8:
                                pe.wait_ge(y_hi_ready, ys + 1)
                            outputs(bv, g, tile[:, (g // 2) % 4, :],
                                    [pT[:, g % 2, c * P:(c + 1) * P] for c in range(3)]).then_inc(bo_done, 1)
                    pe.wait_ge(y_lo_ready, ys + 2)
                    ys += 2
                    n = first["w_o"]
                    for m in range(8):
                        project("w_o", m, n + m, y_hi, y_lo)
            if STOP is None:
                norm(q)


X_FINAL = {None: 10, "mix": 1, "peer": 3, "ffn0": 4, "even": 5, "ffn1": 6, "ffn2": 7, "odd": 8}[STOP]


def tiles(w):
    K, N = w.shape
    return w.reshape(K // P, P, N // P, P).transpose(2, 1, 0, 3).reshape(N // P, P, K)


def slabs(inputs):
    w_in = inputs["w_in"][0]
    order = [512, 0, 1024, 1536, 2560, 3072, 2048]
    parts = [tiles(w_in[:, o:o + 512]) for o in order] + [tiles(w_in[:, 3584:])]
    wa, wb = tiles(inputs["w_branch_hg"][0]), tiles(inputs["w_branch_conv"][0])
    parts.append(np.concatenate([wa, wb], 2))
    parts.append(tiles(inputs["w_out"][0]))
    parts.append(tiles(inputs["peer_w_query"][0]))
    u = inputs["peer_u"][0].reshape(P, P, KT, P).transpose(1, 3, 2, 0).reshape(P, P, D)
    v = inputs["peer_v"][0].reshape(P, P, D).transpose(1, 0, 2)
    pair = np.stack([u[1:], v[:-1]], 1).reshape(2 * (P - 1), P, D)
    parts += [u[0:1], pair, v[-1:]]

    def ffn(pre, layer):
        g = tiles(inputs[f"{pre}_gate_2"][layer])
        up = tiles(inputs[f"{pre}_up_2"][layer])
        down = inputs[f"{pre}_down_2"][layer].reshape(FT, P, D)
        body = np.stack([g[1:], up[1:], down[:-1]], 1).reshape(3 * (FT - 1), P, D)
        return [g[0:1], up[0:1], body, down[-1:]]

    parts += ffn("ffn1", 0)
    parts += [tiles(inputs["even_w_in_2"][0]), tiles(inputs["even_w_out_2"][0])]
    parts += ffn("ffn2", 0) + ffn("ffn1", 1)
    parts += [tiles(inputs["odd_w_qkv_2"][0]), tiles(inputs["odd_w_o_2"][0])]
    parts += ffn("ffn2", 1)
    return np.concatenate(parts, 0)


def by_feature(v):
    return v.reshape(-1, P).T


def kernel(**inputs):
    import concourse.bacc as _bacc
    from concourse.bass_utils import run_bass_kernel_spmd as _run

    inputs = {k: np.asarray(v) for k, v in inputs.items()}
    n = stream_plan()[1]
    vectors = [inputs["norm_mix_g"][0], inputs["norm_ffn_g"][0], inputs["norm_final_g"]]
    for layer in range(2):
        vectors += [inputs["norm_ffn1_2"][layer], inputs["norm_mix_2"][layer], inputs["norm_ffn2_2"][layer]]
    vectors += [inputs["norm_final_2"], inputs["hg_lb_logits"][0], inputs["hg_lb_logits"][1],
                inputs["hg_out_norm_g"][0], *inputs["conv_w"][0], inputs["even_pool_scale_2"][0]]
    k1, k2 = inputs["peer_keys1"][0], inputs["peer_keys2"][0]
    arrays = {
        "stream": slabs(inputs)[:n],
        "x_t": inputs["x"][0].T.reshape(KT, P, T).transpose(1, 0, 2),
        "columns": np.concatenate([by_feature(v) for v in vectors] + [np.full((P, 1), EPS, np.float32)], 1),
        "lanes": np.stack([np.ones((P, P), np.float32),
                           np.broadcast_to(np.arange(P, dtype=np.float32), (P, P))], 1),
        "keys_t": np.stack([k1, k2], 1).reshape(PEER_GROUPS, NKEYS, P).transpose(2, 0, 1),
        "w_pool": inputs["even_w_pool_2"][0].transpose(1, 0, 2),
        "mixer_constants": mixer_constants(),
        "attention_constants": attention_constants(),
    }
    nc = _bacc.Bacc("TRN2", target_bir_lowering=False, num_devices=1)
    args = []
    for name in arrays:
        arrays[name] = np.ascontiguousarray(arrays[name])
        args.append(nc.dram_tensor(name, arrays[name].shape, F32, kind="ExternalInput").ap())
    args.append(nc.dram_tensor("out_t", (P, KT, T), F32, kind="ExternalOutput").ap())
    build(nc, *args)
    r = _run(nc, [arrays], core_ids=[0])
    got = r.results[0]["out_t"]
    return got.transpose(1, 0, 2).reshape(D, T).T.reshape(1, T, D)
```

```python
from contextlib import ExitStack

import numpy as np

import concourse.bass as bass
from concourse import mybir
from concourse.alu_op_type import AluOpType as ALU

STOP = None

ACT = mybir.ActivationFunctionType
AX_X = mybir.AxisListType.X
F32 = mybir.dt.float32
F32R = mybir.dt.float32r
U32 = mybir.dt.uint32

P = 128
T = 256
D = 1024
KT = D // P
TT = T // P
HEADS = 8
DH = 64
CHUNK = 64
NKEYS = 128
TOPK = 16
PEER_GROUPS = 16
D_FF = 2816
FT = D_FF // P
ODD_HEADS = 16
WINDOWS = (2, 4, 8, 16)
PAD = 16
RING = 4
EPS = 1e-6
NEG = -3.0e38
SCALE = DH ** -0.5

STREAM = [
    ("w_in", 44), ("branch", 8), ("w_out", 8), ("wquery", 16), ("peer", 2 * NKEYS),
    ("ffn0", 3 * FT), ("even_in", 16), ("even_out", 8), ("ffn1", 3 * FT),
    ("ffn2", 3 * FT), ("qkv", 24), ("w_o", 8), ("ffn3", 3 * FT),
]
ENDS = {"mix": "w_out", "peer": "peer", "ffn0": "ffn0", "even": "even_out", "ffn1": "ffn1",
        "ffn2": "ffn2", "odd": "w_o", "all": "ffn3"}

GAINS = ["norm_mix_g", "norm_ffn_g", "norm_final_g", "norm_ffn1_0", "norm_mix_0", "norm_ffn2_0",
         "norm_ffn1_1", "norm_mix_1", "norm_ffn2_1", "norm_final"]
COL = {name: KT * i for i, name in enumerate(GAINS)}
COL["lb0"] = KT * len(GAINS)
COL["lb1"] = COL["lb0"] + 4
COL["out_g"] = COL["lb1"] + 4
COL["conv"] = COL["out_g"] + 4
COL["pool_scale"] = COL["conv"] + 12
COL["eps"] = COL["pool_scale"] + 4
N_COLS = COL["eps"] + 1

LEVELS = [64, 32, 16, 8, 4, 2, 1]


def mixer_constants():
    i = np.arange(P)
    s, t = i[:, None], i[None, :]
    head_ones = (s // DH == t // DH).astype(np.float32)
    masks = []
    for m in LEVELS:
        masks.append((s // (2 * m) == t // (2 * m)) & (s % (2 * m) < m) & (t % (2 * m) >= m))
    chunk = np.broadcast_to((np.arange(T) % CHUNK != 0).astype(np.float32), (P, T))
    return np.concatenate([np.eye(P, dtype=np.float32), head_ones]
                          + [m.astype(np.float32) for m in masks] + [chunk], 1)


def attention_constants():
    i = np.arange(P)
    s, t = i[:, None], i[None, :]
    later = (s > t).astype(np.float32)
    past = (s < t).astype(np.float32)
    past_neg = np.concatenate([-past, -np.ones((P, P), np.float32), -past], 1)
    dist0 = np.where(t <= s, t - s, -1.0e30)
    dist1 = np.concatenate([np.broadcast_to(t - s - P, (P, P)), dist0], 1)
    dist = np.concatenate([dist0, dist1], 1).astype(np.float32)
    inv = [1.0 / np.minimum(np.arange(T) + 1, w) for w in WINDOWS]
    inv = np.broadcast_to(np.concatenate(inv).astype(np.float32), (P, 4 * T))
    return np.concatenate([np.eye(P, dtype=np.float32), later, past_neg, dist, inv], 1)


FIRST_LEVEL = 15

N_MIXC = P * (2 + len(LEVELS)) + T
N_ATTC = P * 2 + 3 * P + 3 * P + 4 * T

BASE = 16512
RAW, W_HI, W_LO = 0, RING * D, 2 * RING * D
H_HI = 3 * RING * D
H_LO = H_HI + KT * T
MID = H_LO + KT * T
COLS = MID + 5 * 2 * T
ONES = COLS + P
RSTD = ONES + 2 * P
R_COL = RSTD + T
ARENA = R_COL + 8
X_AT = ARENA + P * T - KT * T
GATES = ARENA + P * T
assert BASE + 4 * (GATES + T) <= 229344


N_NORMS = {None: 10, "mix": 1, "peer": 3, "ffn0": 4, "even": 5, "ffn1": 6, "ffn2": 7, "odd": 8}[STOP]


def stream_plan():
    names = [n for n, _ in STREAM]
    end = names.index(ENDS[STOP or "all"]) + 1
    first, at = {}, 0
    for name, n in STREAM[:end]:
        first[name] = at
        at += n
    if STOP:
        at += RING
    return first, at


def tile_readers(first):
    order = []
    order += ["act"] * 20 + ["dve"] * 8 + ["act"] * 16
    order += ["dve"] * 8 + ["dve"] * 8
    if "wquery" in first:
        order += ["act"] * 16
    if "even_in" in first:
        order += ["dve"] * 8 + ["act"] * 4 + ["dve"] * 4 + ["dve"] * 4 + ["dve"] * 8
    if "qkv" in first:
        order += ["dve"] * 16 + ["act"] * 8 + ["dve"] * 8
    return order


def build(nc, stream, x_in, cols_in, ones_in, keys_in, wpool_in, mixc_in, attc_in, out):
    first, NSLAB = stream_plan()
    readers = tile_readers(first)
    tile_at = {}
    at = 0
    for name, n in (("w_in", 44), ("branch", 8), ("w_out", 8), ("wquery", 16), ("even_in", 16),
                    ("pooled", 4), ("even_out", 8), ("qkv", 24), ("w_o", 8)):
        if name in first or name == "pooled" and "even_in" in first:
            tile_at[name] = at
            at += n

    def slab_of(name, i):
        return first[name] + i

    def tile_buf(j, half=0):
        return tile[:, 2 * (j % 2) + half, :]

    def pair_buf(c, tt):
        return tile[:, 2 * (c // 2 % 2) + tt, :]

    def reads(engine, j):
        return sum(r == engine for r in readers[:j + 1])

    with ExitStack() as ctx:
        def sb(name, at, shape, dt=F32):
            return nc.alloc_sbuf_tensor_at(name, [P] + shape, dt, offset=BASE + 4 * at)

        def sem(name):
            return ctx.enter_context(nc.semaphore(name))

        raw = sb("raw", RAW, [RING, D])
        w_hi = sb("w_hi", W_HI, [RING, D], F32R)
        w_lo = sb("w_lo", W_LO, [RING, D], F32R)
        h_hi = sb("h_hi", H_HI, [KT, T], F32R)
        h_lo = sb("h_lo", H_LO, [KT, T], F32R)
        scaled = sb("scaled", MID, [2, 2 * T])
        hid = sb("hid", MID + 4 * T, [2, T])
        mid_hi = sb("mid_hi", MID + 6 * T, [2, T], F32R)
        mid_lo = sb("mid_lo", MID + 8 * T, [2, T], F32R)
        cols = sb("cols", COLS, [N_COLS])
        lane = sb("lane", ONES, [2, P])
        ones, iota = lane[:, 0, :], lane[:, 1, :]
        rstd = sb("rstd", RSTD, [T])
        r_col = sb("r_col", R_COL, [TT])
        pick1 = sb("pick1", MID, [2, 4, P])
        pick2 = sb("pick2", MID + 8 * P, [2, 4, P])
        idx1_T = sb("idx1_T", MID + 16 * P, [T])
        idx2_T = sb("idx2_T", MID + 16 * P + T, [T])
        gate_T = sb("gate_T", GATES, [T])
        G = sb("G", ARENA, [T, P])
        x = sb("x", X_AT, [KT, T])
        h32 = sb("h32", ARENA + 2560, [KT, T])
        sq = sb("sq", ARENA + 4608, [KT, T])

        A = ARENA + 6656
        mixc = sb("mixc", ARENA, [N_MIXC])
        ident = mixc[:, 0:P]
        head_ones = mixc[:, P:2 * P]
        level_mask = {m: mixc[:, (2 + i) * P:(3 + i) * P] for i, m in enumerate(LEVELS)}
        chunk_mask = mixc[:, N_MIXC - T:N_MIXC]
        kk = sb("kk", A, [4, T])
        qq = sb("qq", A + 1024, [4, T])
        hgs = sb("hgs", A + 2048, [4, T])
        bb = sb("bb", A + 3072, [4, T])
        lf = sb("lf", A + 4096, [4, T])
        vv = sb("vv", A + 5120, [TT, 512])
        cc = sb("cc", A + 6144, [4, T])
        uu = sb("uu", A + 7168, [4, T + 2])
        conv = sb("conv", A + 8208, [4, T])
        sg = sb("sg", A + 9232, [16, T])
        y_hi = sb("y_hi", A + 13376, [KT, T], F32R)
        y_lo = sb("y_lo", A + 15424, [KT, T], F32R)
        y32 = sb("y32", A + 17472, [KT, T])
        S = sb("S", A + 19520, [4, 4, P])
        S_off = sb("S_off", A + 21568, [2, 4, P])
        lbw = sb("lbw", A + 22592, [8, 4])
        dec = sb("dec", A + 22624, [4, 4])
        assert A + 22640 <= X_AT
        X = sb("X", ARENA + 2560, [2, 4, T])
        osq = sb("osq", ARENA + 4608, [4, T])
        orr = sb("orr", ARENA + 5632, [4, T])
        keysT = sb("keysT", A, [PEER_GROUPS, NKEYS])
        qT = sb("qT", A + 2048, [PEER_GROUPS, T])
        top_v = sb("top_v", A + 6144, [TT, PEER_GROUPS, TOPK])
        top_i = sb("top_i", A + 6656, [TT, PEER_GROUPS, TOPK], U32)
        top_f = sb("top_f", A + 7168, [TT, PEER_GROUPS, TOPK])
        rest = sb("rest", A + 12704, [TT, NKEYS])
        cand = sb("cand", A + 7808, [2, TOPK, TOPK])
        best = sb("best", A + 8320, [TT, HEADS, TOPK])
        pos = sb("pos", A + 8576, [TT, HEADS, TOPK], U32)
        pos1 = sb("pos1", A + 8832, [TT, HEADS, TOPK], U32)
        pos2 = sb("pos2", A + 9088, [TT, HEADS, TOPK], U32)
        posf = sb("posf", A + 9344, [2, TT, HEADS, TOPK])
        onehot = sb("onehot", A + 9856, [HEADS, TOPK, TOPK])
        idx = sb("idx", A + 11904, [2, TT, HEADS, TOPK])
        gts = sb("gts", A + 12416, [TT, HEADS, TOPK])
        gsum = sb("gsum", A + 12672, [TT, HEADS, 2])
        attc = sb("attc", ARENA, [N_ATTC])
        ident2 = attc[:, 0:P]
        later = attc[:, P:2 * P]
        past_neg = attc[:, 2 * P:5 * P]
        dist = attc[:, 5 * P:8 * P]
        inv_count = attc[:, 8 * P:8 * P + 4 * T].rearrange("p (g t) -> p g t", g=4)
        wpool = sb("wpool", ARENA + N_ATTC, [4, P])
        assert N_ATTC + 4 * P <= 2560
        aq = sb("aq", A, [4, T])
        ak = sb("ak", A + 1024, [4, T])
        av = sb("av", A + 2048, [TT, 512])
        pu = sb("pu", A + 3072, [4, PAD + T])
        az = sb("az", A + 4160, [HEADS, 3 * P])
        asp = sb("asp", A + 7232, [HEADS, 3 * P])
        aL = sb("aL", A + 10304, [HEADS, 3 * P])
        win = sb("win", ARENA + 2560, [2, PAD + T])
        pooled = sb("pooled", ARENA + 4608, [4, T])
        bq = sb("bq", A, [KT, T])
        bk = sb("bk", A + 2048, [KT, T])
        bv = sb("bv", A + 4096, [TT, D])
        sc = sb("sc", A + 6144, [4, 3 * P])
        pT = sb("pT", A + 7680, [2, 3 * P])
        st = sb("st", A + 8448, [3, 4, 2])

        acc = ctx.enter_context(nc.psum_tensor("acc", [P, KT, T], F32))
        front = ctx.enter_context(nc.psum_tensor("front", [P, 2, 2 * T], F32))
        tile = ctx.enter_context(nc.psum_tensor("tile", [P, 4, T], F32))
        banks = acc[:, :, :].rearrange("p (b a) t -> p b (a t)", b=4)
        fronts = front[:, :, :]

        landed = [sem(f"slab_landed{i}") for i in range(RING)]
        hi_ready = sem("slab_hi_ready")
        lo_ready = sem("slab_lo_ready")
        slab_used = sem("slab_used")
        pool_done = sem("pool_products_done")
        tile_read = {"act": sem("tile_read_by_act"), "dve": sem("tile_read_by_dve")}
        small_in = sem("small_inputs_landed")
        keys_in_sem = sem("keys_landed")
        attc_sem = sem("attention_constants_landed")
        dve_own = sem("dve_own_steps")
        act_own = sem("act_own_steps")
        x_ready = sem("x_pairs_ready")
        result_ready = sem("result_ready")
        squares = sem("norm_squares")
        sums = sem("norm_sums")
        sq_summed = sem("norm_squares_added")
        roots = sem("norm_roots")
        rstd_ready = sem("rstd_ready")
        r_turned = sem("rstd_turned")
        r_col_ready = sem("rstd_columns_ready")
        scaled_ready = sem("front_scaled")
        h32_ready = sem("norm_h32")
        nh_hi = sem("norm_h_hi")
        nh_lo = sem("norm_h_lo")
        gate_ready = sem("gate_ready")
        hid_ready = sem("hid_ready")
        mid_hi_ready = sem("mid_hi_ready")
        mid_lo_ready = sem("mid_lo_ready")
        out_done = sem("out_done")
        forget_ready = sem("forget_ready")
        logf_ready = sem("logf_ready")
        lb_diff = sem("lb_diff")
        lb_exp = sem("lb_exp")
        level_diff = sem("level_diff")
        level_exp = sem("level_exp")
        level_ready = sem("level_operands_ready")
        level_done = sem("level_scores_done")
        level_read = sem("level_scores_read")
        o_done = sem("hgrn_o_done")
        o_sq = sem("hgrn_o_squares")
        o_sum = sem("hgrn_o_sums")
        o_root = sem("hgrn_o_roots")
        y32_ready = sem("y32_ready")
        y_hi_ready = sem("y_hi_ready")
        y_lo_ready = sem("y_lo_ready")
        merged_ready = sem("merged_ready")
        merged_hi = sem("merged_hi")
        merged_lo = sem("merged_lo")
        keys_done = sem("key_scores_done")
        keys_read = sem("key_scores_read")
        gate_diff = sem("gate_diff")
        gate_exp = sem("gate_exp")
        picks_ready = sem("picks_ready")
        picks_turned = sem("picks_turned")
        picks_copied = sem("picks_copied")
        pick1_there = sem("pick_rows_of_first_keys_there")
        pick1_ready = sem("pick_rows_with_gates_ready")
        pick2_ready = sem("pick_rows_of_second_keys_ready")
        pick_used = sem("pick_rows_used")
        g_copied = sem("G_copied")
        x_seeded = sem("x_seeded")
        z_done = sem("stick_z_done")
        z_read = sem("stick_z_read")
        ln_ready = sem("stick_ln_ready")
        stick_L = sem("stick_L_ready")
        later_done = sem("stick_later_done")
        stick_w = sem("stick_w_ready")
        stick_e = sem("stick_exp_ready")
        stick_a = sem("stick_a_ready")
        ao_done = sem("stick_o_done")
        u_ready = sem("pool_u_ready")
        pooled_ready = sem("pooled_ready")
        sc_done = sem("odd_scores_done")
        sc_read = sem("odd_scores_read")
        p_exp = sem("odd_exp_ready")
        p_norm = sem("odd_p_ready")
        p_turned = sem("odd_p_turned")
        p_copied = sem("odd_p_copied")
        bo_done = sem("odd_o_done")

        block = ctx.enter_context(nc.Block())

        def layer_stages():
            for name, stage in (("ffn0", ("ffn", 0)), ("even_in", ("even", 0)), ("ffn1", ("ffn", 1)),
                                ("ffn2", ("ffn", 2)), ("qkv", ("odd", 0)), ("ffn3", ("ffn", 3))):
                if name in first:
                    yield stage

        FFN_GAIN = ["norm_ffn1_0", "norm_ffn2_0", "norm_ffn1_1", "norm_ffn2_1"]

        def stage_gain(kind, i):
            return FFN_GAIN[i] if kind == "ffn" else {"even": "norm_mix_0", "odd": "norm_mix_1"}[kind]

        sources = [None, "w_out", 0]
        x_pairs = 4
        for kind, i in layer_stages():
            sources.append({"ffn": x_pairs, "even": x_pairs, "odd": x_pairs}[kind]
                           if (kind, i) not in (("ffn", 1), ("ffn", 3))
                           else {1: "even_out", 3: "w_o"}[i])
            if kind == "ffn":
                x_pairs += 4
        sources.append(x_pairs if STOP in (None, "ffn0", "ffn1", "ffn2") else None)

        def wait_x(eng, q, k):
            src = sources[q]
            if isinstance(src, str):
                eng.wait_ge(tile_read["dve"], reads("dve", tile_at[src] + k))
            else:
                eng.wait_ge(x_ready, src + k // 2 + 1)

        SUM_AT = {"mlp": tile[:, 0, :], "project": front[:, 0, 0:T]}
        sum_at = [SUM_AT["project"]] * 2 + [SUM_AT["project"]]
        for kind, i in layer_stages():
            sum_at.append(SUM_AT["mlp" if kind == "ffn" else "project"])
        sum_at.append(SUM_AT["mlp"])

        @block.sync
        def _(sp):
            sp.dma_start(x[:, :, :], x_in).then_inc(small_in, 16)
            sp.dma_start(cols[:, :], cols_in).then_inc(small_in, 16)
            sp.dma_start(lane[:, :, :], ones_in).then_inc(small_in, 16)
            for s in range(RING):
                sp.dma_start(raw[:, s, :], stream[s, :, :]).then_inc(landed[s], 16)
            sp.dma_start(mixc[:, :], mixc_in).then_inc(small_in, 16)
            with sp.Fori(1, NSLAB // RING) as turn:
                for s in range(RING):
                    sp.wait_ge(lo_ready, turn * RING + (s + 1 - RING))
                    sp.dma_start(raw[:, s, :], stream[bass.ds(turn * RING + s, 1), :, :]
                                 .rearrange("a p n -> (a p) n")).then_inc(landed[s], 16)
            for n in range(NSLAB // RING * RING, NSLAB):
                sp.wait_ge(lo_ready, n + 1 - RING)
                sp.dma_start(raw[:, n % RING, :], stream[n, :, :]).then_inc(landed[n % RING], 16)
            sp.wait_ge(result_ready, 1)
            sp.dma_start(out, (h32 if STOP is None else x)[:, :, :]).then_inc(out_done, 16)
            sp.wait_ge(out_done, 16)

        @block.gpsimd
        def _(pool):
            def pick_gates(t, k):
                nc.gpsimd.tensor_tensor(pick1[:, k, :, :], pick1[:, k, :, :],
                                        gate_T[:, t].unsqueeze(2).broadcast_to([P, 4, P]),
                                        ALU.mult).then_inc(pick1_ready, 4)

            for q in range(1, N_NORMS):
                if q == 2:
                    for n in range(first["wquery"] + RING, first["peer"] + RING):
                        pool.wait_ge(lo_ready, n)
                        pool.wait_ge(hi_ready, n + 1)
                        nc.gpsimd.tensor_tensor(w_lo[:, n % RING, :], raw[:, n % RING, :],
                                                w_hi[:, n % RING, :].bitcast(F32),
                                                ALU.subtract).then_inc(lo_ready, 1)
                    pool.wait_ge(picks_copied, 3)
                    for k in range(2):
                        pool.wait_ge(pick1_there, 4 * k + 4)
                        pick_gates(slice(4 * k, 4 * k + 4), k)
                    with pool.Fori(0, (T - 8) // 8) as turn:
                        for k in range(2):
                            pool.wait_ge(pick1_there, turn * 8 + (12 + 4 * k))
                            pick_gates(bass.ds(turn * 8 + (8 + 4 * k), 4), k)
                for k in range(0, KT, 2):
                    wait_x(pool, q, k + 1)
                    if k == 0:
                        pool.wait_ge(sums, q)
                    nc.gpsimd.tensor_tensor(sq[:, k:k + 2, :], x[:, k:k + 2, :], x[:, k:k + 2, :], ALU.mult)\
                        .then_inc(squares, 1)

        @block.scalar
        def _(act):
            own = [0]

            def link(ins):
                ins.then_inc(act_own, 1)
                own[0] += 1
                act.wait_ge(act_own, own[0])

            def split_hi(n, turn=None, per=0):
                if turn is None and n >= NSLAB:
                    return
                s = n % RING
                loads = n // RING + 1
                if turn is None:
                    act.wait_ge(landed[s], 16 * loads)
                    if n >= RING:
                        act.wait_ge(slab_used, n + 1 - RING)
                else:
                    act.wait_ge(landed[s], turn * (16 * per // RING) + 16 * loads)
                    act.wait_ge(slab_used, turn * per + (n + 1 - RING))
                nc.scalar.copy(w_hi[:, s, :], raw[:, s, :]).then_inc(hi_ready, 1)

            def root(q):
                act.wait_ge(sums, q + 1)
                nc.scalar.activation(rstd[:, :], sum_at[q], ACT.Sqrt, scale=1.0 / D,
                                     bias=cols[:, COL["eps"]:COL["eps"] + 1]).then_inc(roots, 1)

            def operand_hi(q, i, gain):
                for k in range(KT):
                    wait_x(act, q, k)
                    nc.scalar.activation(h_hi[:, k, :], x[:, k, :], ACT.Copy,
                                         scale=cols[:, COL[gain] + k:COL[gain] + k + 1]).then_inc(nh_hi, 1)

            def take(name, i, out, func=ACT.Copy, scale=1.0):
                j = tile_at[name] + i
                act.wait_ge(slab_used, slab_of(name, i) + 1)
                nc.scalar.activation(out, tile_buf(j), func, scale=scale).then_inc(tile_read["act"], 1)

            def take_v(name, i, c, v, scaled_=True):
                act.wait_ge(slab_used, slab_of(name, i) + 2)
                for tt in range(TT):
                    ins = nc.scalar.activation(v[:, tt, c * P:(c + 2) * P], pair_buf(c, tt), ACT.Copy,
                                               scale=r_col[:, tt:tt + 1] if scaled_ else 1.0)
                ins.then_inc(tile_read["act"], 2)

            def mlp(func, n0, steps, fronts_, done):
                per_step = fronts_ + 1

                def step(s, n, turn=None, turns=0):
                    S0 = done + s
                    k = s % 2
                    spt, slt = turns, turns * per_step

                    if fronts_ == 2:
                        split_hi(n + RING, turn, slt)
                    act.wait_ge(scaled_ready, S0 + 1 if turn is None else turn * spt + (S0 + 1))
                    nc.scalar.activation(scaled[:, k, 0:T], scaled[:, k, 0:T], func).then_inc(gate_ready, 1)
                    split_hi(n + fronts_ - 1 + RING, turn, slt)
                    act.wait_ge(hid_ready, S0 + 1 if turn is None else turn * spt + (S0 + 1))
                    nc.scalar.copy(mid_hi[:, k, :], hid[:, k, :]).then_inc(mid_hi_ready, 1)

                step(0, n0)
                n = n0 + fronts_
                turns = 4 if fronts_ == 2 else 2
                loops = (steps - 1) // turns
                with act.Fori(0, loops) as turn:
                    for c in range(turns):
                        step(1 + c, n + c * per_step, turn, turns)
                        split_hi(n + c * per_step + fronts_ + RING, turn, turns * per_step)
                for s in range(1 + loops * turns, steps):
                    m = n + (s - 1) * per_step
                    step(s, m)
                    split_hi(m + fronts_ + RING)
                split_hi(n0 + steps * per_step - 1 + RING)

            act.wait_ge(small_in, 64)
            nc.scalar.activation(sq[:, :, :], x[:, :, :], ACT.Square).then_inc(squares, 1)
            root(0)
            for n in range(RING):
                split_hi(n)
            for half in range(2):
                act.wait_ge(h32_ready, 2 * half + 2)
                nc.scalar.copy(h_hi[:, 4 * half:4 * half + 4, :],
                               h32[:, 4 * half:4 * half + 4, :]).then_inc(nh_hi, 4)

            act.wait_ge(lb_diff, 1)
            nc.scalar.activation(lbw[:, 3:5, :], lbw[:, 1:3, :], ACT.Exp).then_inc(lb_exp, 1)
            n = first["w_in"]
            for i in range(44):
                if i < 4:
                    take("w_in", i, kk[:, i, :], ACT.Sigmoid)
                elif i < 8:
                    take("w_in", i, qq[:, i - 4, :], ACT.Silu)
                elif i < 12:
                    if i % 2:
                        take_v("w_in", i - 1, i - 9, vv, False)
                elif i < 16:
                    take("w_in", i, hgs[:, i - 12, :], ACT.Silu)
                elif i < 20:
                    take("w_in", i, cc[:, i - 16, :])
                elif i >= 28:
                    take("w_in", i, sg[:, i - 28, :], ACT.Sigmoid)
                else:
                    act.wait_ge(slab_used, n + i + 1)
                split_hi(n + i + RING)
                if i == 12:
                    act.wait_ge(forget_ready, 1)
                    nc.scalar.activation(lf[:, :, :], lf[:, :, :], ACT.Ln).then_inc(logf_ready, 1)
                l = (i - FIRST_LEVEL) // 2
                if i >= FIRST_LEVEL and (i - FIRST_LEVEL) % 2 == 0 and l < 8:
                    act.wait_ge(level_diff, l + 1)
                    nc.scalar.activation(X[:, l % 2, :, :], X[:, l % 2, :, :], ACT.Exp).then_inc(level_exp, 1)
                if i == FIRST_LEVEL + 18:
                    act.wait_ge(tile_read["dve"], reads("dve", tile_at["w_in"] + 27))
                    nc.scalar.copy(y_hi[:, 4:8, :], y32[:, 4:8, :]).then_inc(y_hi_ready, 1)
                if i == FIRST_LEVEL + 20:
                    act.wait_ge(o_done, 1)
                    nc.scalar.activation(osq[:, :, :], fronts.rearrange("p b (a t) -> p (b a) t", a=2),
                                         ACT.Square).then_inc(o_sq, 1)
                if i == FIRST_LEVEL + 22:
                    act.wait_ge(o_sum, 1)
                    nc.scalar.activation(orr[:, :, :], acc[:, 0:4, :], ACT.Sqrt, scale=1.0 / DH,
                                         bias=cols[:, COL["eps"]:COL["eps"] + 1]).then_inc(o_root, 1)
                if i == FIRST_LEVEL + 25:
                    act.wait_ge(y32_ready, 1)
                    nc.scalar.copy(y_hi[:, 0:4, :], y32[:, 0:4, :]).then_inc(y_hi_ready, 1)
            n = first["branch"]
            for m in range(8):
                act.wait_ge(slab_used, n + m + 1)
                split_hi(n + m + RING)
                act.wait_ge(merged_ready, m + 1)
                nc.scalar.copy(h_hi[:, m, :], h32[:, m, :]).then_inc(merged_hi, 1)
            n = first["w_out"]
            for m in range(8):
                act.wait_ge(slab_used, n + m + 1)
                split_hi(n + m + RING)
            if "peer" in first:
                nc.scalar.dma_start(keysT[:, :, :], keys_in).then_inc(keys_in_sem, 16)
                operand_hi(1, 1, "norm_ffn_g")
                root(1)
                n = first["wquery"]
                for i in range(16):
                    take("wquery", i, qT[:, i, :])
                    split_hi(n + i + RING)
                act.wait_ge(gate_diff, 1)
                nc.scalar.activation(gts[:, :, :, :], gts[:, :, :, :], ACT.Exp).then_inc(gate_exp, 1)
                act.wait_ge(picks_turned, 1)
                for i, to in enumerate((idx1_T, idx2_T, gate_T)):
                    nc.scalar.copy(to[:, :], tile[:, i, :]).then_inc(picks_copied, 1)
                act.wait_ge(x_seeded, 1)
                with act.Fori(0, T // 16) as turn:
                    for b in range(4):
                        act.wait_ge(pick_used, turn * 16 + 4 * b + 4)
                        src = (fronts[:, b, :] if b < 2
                               else tile[:, 2 * b - 4:2 * b - 2, :].rearrange("p a t -> p (a t)"))
                        nc.scalar.copy(G[:, bass.ds(turn * 16 + 4 * b, 4), :],
                                       src.rearrange("p (t j) -> p t j", t=4)).then_inc(g_copied, 1)
                act.wait_ge(pick_used, T)
                mlp(ACT.Gelu, first["peer"], NKEYS, 1, 0)
                root(2)
            q = 3
            done = NKEYS
            attc_loaded = False
            for kind, i in layer_stages():
                operand_hi(q, q - 1, stage_gain(kind, i))
                root(q)
                if not attc_loaded:
                    attc_loaded = True
                    nc.scalar.dma_start(attc[:, :], attc_in).then_inc(attc_sem, 16)
                    nc.scalar.dma_start(wpool[:, :, :], wpool_in).then_inc(attc_sem, 16)
                q += 1
                if kind == "ffn":
                    mlp(ACT.Silu, first[f"ffn{i}"], FT, 2, done)
                    done += FT
                elif kind == "even":
                    n = first["even_in"]
                    for i in range(16):
                        act.wait_ge(slab_used, n + i + 1)
                        split_hi(n + i + RING)
                        if i in (9, 11):
                            if i == 9:
                                act.wait_ge(r_col_ready, 2)
                            take_v("even_in", i - 1, i - 9, av)
                    for h in range(HEADS):
                        act.wait_ge(z_done, h + 1)
                        nc.scalar.activation(az[:, h, :], banks[:, h % 4, 0:3 * P], ACT.Copy,
                                             scale=SCALE).then_inc(z_read, 1)
                    for g in range(2):
                        a, b = 4 * g, 4 * g + 4
                        act.wait_ge(z_read, b)
                        link(nc.scalar.activation(asp[:, a:b, :], az[:, a:b, :], ACT.Abs))
                        link(nc.scalar.activation(asp[:, a:b, :], asp[:, a:b, :], ACT.Exp, scale=-1.0))
                        nc.scalar.activation(asp[:, a:b, :], asp[:, a:b, :], ACT.Ln, bias=1.0)\
                            .then_inc(ln_ready, 1)
                    for g in range(2):
                        a, b = 4 * g, 4 * g + 4
                        act.wait_ge(stick_w, b)
                        nc.scalar.activation(az[:, a:b, :], az[:, a:b, :], ACT.Exp).then_inc(stick_e, 1)
                    act.wait_ge(ao_done, 1)
                    nc.scalar.copy(y32[:, 0:4, :], fronts.rearrange("p b (a t) -> p (b a) t", a=2))\
                        .then_inc(act_own, 1)
                    own[0] += 1
                    act.wait_ge(act_own, own[0])
                    nc.scalar.copy(y_hi[:, 0:4, :], y32[:, 0:4, :]).then_inc(y_hi_ready, 1)
                    act.wait_ge(tile_read["dve"], reads("dve", tile_at["pooled"] + 3))
                    nc.scalar.copy(y_hi[:, 4:8, :], y32[:, 4:8, :]).then_inc(y_hi_ready, 1)
                    n = first["even_out"]
                    for m in range(8):
                        act.wait_ge(slab_used, n + m + 1)
                        split_hi(n + m + RING)
                else:
                    n = first["qkv"]
                    for i in range(24):
                        act.wait_ge(slab_used, n + i + 1)
                        split_hi(n + i + RING)
                        if i >= 16 and i % 2:
                            if i == 17:
                                act.wait_ge(r_col_ready, 3)
                            take_v("qkv", i - 1, i - 17, bv)

                    def take_heads(half):
                        act.wait_ge(bo_done, 8 * half + 8)
                        link(nc.scalar.copy(y32[:, 4 * half:4 * half + 4, :], tile[:, :, :]))
                        nc.scalar.copy(y_hi[:, 4 * half:4 * half + 4, :],
                                       y32[:, 4 * half:4 * half + 4, :]).then_inc(y_hi_ready, 1)

                    for h in range(ODD_HEADS + 2):
                        if h < ODD_HEADS:
                            k = h % 4
                            act.wait_ge(sc_read, h + 1)
                            nc.scalar.activation(sc[:, k, 0:P], sc[:, k, 0:P], ACT.Exp,
                                                 bias=st[:, 0, k, 0:1], accum_out=st[:, 1, k, 0:1])\
                                .then_inc(p_exp, 1)
                            nc.scalar.activation(sc[:, k, P:3 * P], sc[:, k, P:3 * P], ACT.Exp,
                                                 bias=st[:, 0, k, 1:2], accum_out=st[:, 1, k, 1:2])\
                                .then_inc(p_exp, 1)
                        if h >= 2:
                            g = h - 2
                            act.wait_ge(p_turned, g + 1)
                            if g >= 2:
                                act.wait_ge(bo_done, g - 1)
                            nc.scalar.copy(pT[:, g % 2, :], fronts[:, g % 2, 0:3 * P])\
                                .then_inc(p_copied, 1)
                        if h == 11:
                            take_heads(0)
                    take_heads(1)
                    n = first["w_o"]
                    for m in range(8):
                        act.wait_ge(slab_used, n + m + 1)
                        split_hi(n + m + RING)
            if STOP is None:
                root(q)

        @block.vector
        def _(dve):
            own = [0]

            def link(ins):
                ins.then_inc(dve_own, 1)
                own[0] += 1
                dve.wait_ge(dve_own, own[0])

            def split_lo(n, turn=None, per=0):
                if turn is None and n >= NSLAB:
                    return
                s = n % RING
                dve.wait_ge(hi_ready, n + 1 if turn is None else turn * per + (n + 1))
                nc.vector.tensor_tensor(w_lo[:, s, :], raw[:, s, :], w_hi[:, s, :].bitcast(F32),
                                        ALU.subtract).then_inc(lo_ready, 1)

            def col(name, i=0):
                return cols[:, COL[name] + i:COL[name] + i + 1]

            def inverse_rms(q):
                if q:
                    dve.wait_ge(squares, 1 + 4 * q)
                    link(nc.vector.tensor_tensor(sq[:, 0:4, :], sq[:, 0:4, :], sq[:, 4:8, :], ALU.add))
                    link(nc.vector.tensor_tensor(sq[:, 0:2, :], sq[:, 0:2, :], sq[:, 2:4, :], ALU.add))
                    nc.vector.tensor_tensor(sq[:, 0, :], sq[:, 0, :], sq[:, 1, :], ALU.add)\
                        .then_inc(sq_summed, 1)
                dve.wait_ge(roots, q + 1)
                nc.vector.reciprocal(rstd[:, :], rstd[:, :]).then_inc(rstd_ready, 1)
                dve.wait_ge(rstd_ready, q + 1)

            def operand_lo(q, i, gain):
                for k in range(KT):
                    dve.wait_ge(nh_hi, 8 * i + k + 1)
                    nc.vector.scalar_tensor_tensor(h_lo[:, k, :], x[:, k, :], col(gain, k),
                                                   h_hi[:, k, :].bitcast(F32), ALU.mult, ALU.subtract)\
                        .then_inc(nh_lo, 1)

            def r_columns(count):
                dve.wait_ge(r_turned, count)
                nc.vector.tensor_copy(r_col[:, :], front[:, 1, 0:T:P]).then_inc(r_col_ready, 1)

            def scale_x(gain, to, after=None):
                for k in range(KT):
                    ins = nc.vector.scalar_tensor_tensor(to[:, k, :], x[:, k, :], col(gain, k), rstd[:, :],
                                                         ALU.mult, ALU.mult)
                    if after is not None and k % 2 == 1:
                        ins.then_inc(after, 1)
                return ins

            def take(name, i, out, scale=None):
                j = tile_at[name] + i
                dve.wait_ge(slab_used, slab_of(name, i) + 1)
                if scale is None:
                    ins = nc.vector.tensor_tensor(out, tile_buf(j), rstd[:, :], ALU.mult)
                else:
                    ins = nc.vector.scalar_tensor_tensor(out, tile_buf(j), scale, rstd[:, :], ALU.mult,
                                                         ALU.mult)
                ins.then_inc(tile_read["dve"], 1)

            def y_low(count, a, b):
                dve.wait_ge(y_hi_ready, count)
                nc.vector.tensor_tensor(y_lo[:, a:b, :], y32[:, a:b, :], y_hi[:, a:b, :].bitcast(F32),
                                        ALU.subtract).then_inc(y_lo_ready, 1)

            def mlp(n0, steps, fronts_, done):
                per_step = fronts_ + 1

                def step(s, n, turn=None, turns=0):
                    S0 = done + s
                    k = s % 2
                    spt, slt = turns, turns * per_step

                    def wait(sm, v):
                        dve.wait_ge(sm, v if turn is None else turn * spt + v)

                    used = n + fronts_
                    dve.wait_ge(slab_used, used if turn is None else turn * slt + used)
                    r = rstd[:, :]
                    if fronts_ == 2:
                        r = r.unsqueeze(1).broadcast_to([P, 2, T])
                        nc.vector.tensor_tensor(scaled[:, k, :].rearrange("p (a t) -> p a t", a=2),
                                                fronts[:, k, :].rearrange("p (a t) -> p a t", a=2), r,
                                                ALU.mult).then_inc(scaled_ready, 1)
                        split_lo(n + RING, turn, slt)
                    else:
                        nc.vector.tensor_tensor(scaled[:, k, 0:T], fronts[:, k, 0:T], r, ALU.mult)\
                            .then_inc(scaled_ready, 1)
                    wait(gate_ready, S0 + 1)
                    if fronts_ == 2:
                        other = scaled[:, k, T:2 * T]
                    else:
                        other = (G[:, :, s] if turn is None
                                 else G[:, :, bass.ds(turn * turns + s, 1)].rearrange("p t a -> p (t a)"))
                    nc.vector.tensor_tensor(hid[:, k, :], scaled[:, k, 0:T], other, ALU.mult)\
                        .then_inc(hid_ready, 1)
                    split_lo(n + fronts_ - 1 + RING, turn, slt)
                    wait(mid_hi_ready, S0 + 1)
                    nc.vector.tensor_tensor(mid_lo[:, k, :], hid[:, k, :], mid_hi[:, k, :].bitcast(F32),
                                            ALU.subtract).then_inc(mid_lo_ready, 1)

                step(0, n0)
                n = n0 + fronts_
                turns = 4 if fronts_ == 2 else 2
                loops = (steps - 1) // turns
                with dve.Fori(0, loops) as turn:
                    for c in range(turns):
                        step(1 + c, n + c * per_step, turn, turns)
                        split_lo(n + c * per_step + fronts_ + RING, turn, turns * per_step)
                for s in range(1 + loops * turns, steps):
                    m = n + (s - 1) * per_step
                    step(s, m)
                    split_lo(m + fronts_ + RING)
                split_lo(n0 + steps * per_step - 1 + RING)

            def add_tile(name, m):
                j = tile_at[name] + m
                dve.wait_ge(slab_used, slab_of(name, m) + 1)
                nc.vector.tensor_tensor(x[:, m, :], tile_buf(j), x[:, m, :], ALU.add)\
                    .then_inc(tile_read["dve"], 1)

            dve.wait_ge(small_in, 64)
            link(nc.vector.tensor_tensor(lbw[:, 0, :], cols[:, COL["lb0"]:COL["lb0"] + 4],
                                         cols[:, COL["lb1"]:COL["lb1"] + 4], ALU.max))
            nc.vector.tensor_tensor(lbw[:, 1, :], cols[:, COL["lb0"]:COL["lb0"] + 4], lbw[:, 0, :],
                                    ALU.subtract)
            nc.vector.tensor_tensor(lbw[:, 2, :], cols[:, COL["lb1"]:COL["lb1"] + 4], lbw[:, 0, :],
                                    ALU.subtract).then_inc(lb_diff, 1)
            nc.vector.memset(uu[:, :, 0:2], 0.0)
            inverse_rms(0)
            scale_x("norm_mix_g", h32, h32_ready)
            for n in range(RING):
                split_lo(n)
            for half in range(2):
                dve.wait_ge(nh_hi, 4 * half + 4)
                nc.vector.tensor_tensor(h_lo[:, 4 * half:4 * half + 4, :], h32[:, 4 * half:4 * half + 4, :],
                                        h_hi[:, 4 * half:4 * half + 4, :].bitcast(F32),
                                        ALU.subtract).then_inc(nh_lo, 4)
            dve.wait_ge(lb_exp, 1)
            link(nc.vector.tensor_tensor(lbw[:, 5, :], lbw[:, 3, :], lbw[:, 4, :], ALU.add))
            link(nc.vector.reciprocal(lbw[:, 5, :], lbw[:, 5, :]))
            link(nc.vector.tensor_tensor(lbw[:, 6, :], lbw[:, 3, :], lbw[:, 5, :], ALU.mult))
            link(nc.vector.tensor_scalar(lbw[:, 7, :], lbw[:, 6, :], -1.0, 1.0, ALU.mult, ALU.add))

            def halves(ap, m):
                flat = ap.rearrange("p a t -> p (a t)")
                v = flat.rearrange("p (n h m) -> p n h m", h=2, m=m)
                return v[:, :, 0, :], v[:, :, 1, :]

            seq = LEVELS + [128]

            def level_prepare(l):
                m = seq[l]
                to = X[:, l % 2, :, :]
                if l >= 2:
                    dve.wait_ge(level_done, 4 * l)
                if m < CHUNK:
                    b_lo, b_up = halves(bb[:, :, :], m)
                    x_lo, x_up = halves(to, m)
                    ref = b_lo[:, :, m - 1:m].broadcast_to([P, 4 * T // (2 * m), m])
                    nc.vector.tensor_tensor(x_up, b_up, ref, ALU.subtract)
                    nc.vector.tensor_tensor(x_lo, ref, b_lo, ALU.subtract).then_inc(level_diff, 1)
                elif m == CHUNK:
                    b_lo, b_up = halves(bb[:, :, :], m)
                    x_lo, x_up = halves(to, m)
                    ref = b_lo[:, :, m - 1:m].broadcast_to([P, 8, m])
                    nc.vector.tensor_copy(x_up, b_up)
                    nc.vector.tensor_tensor(x_lo, ref, b_lo, ALU.subtract).then_inc(level_diff, 1)
                else:
                    ends = bb[:, :, CHUNK - 1:T:CHUNK]
                    link(nc.vector.tensor_tensor(dec[:, :, 0:1], ends[:, :, 0:1], ends[:, :, 1:2], ALU.add))
                    for c, op, a, b in ((2, None, None, None),
                                        (3, ALU.add, None, ends[:, :, 2:3]),
                                        (1, ALU.subtract, ends[:, :, 1:2], None),
                                        (0, ALU.subtract, dec[:, :, 0:1], None)):
                        o = to[:, :, c * CHUNK:(c + 1) * CHUNK]
                        bc = bb[:, :, c * CHUNK:(c + 1) * CHUNK]
                        if op is None:
                            ins = nc.vector.tensor_copy(o, bc)
                        elif b is not None:
                            ins = nc.vector.tensor_tensor(o, bc, b.broadcast_to([P, 4, CHUNK]), op)
                        else:
                            ins = nc.vector.tensor_tensor(o, a.broadcast_to([P, 4, CHUNK]), bc, op)
                    ins.then_inc(level_diff, 1)

            def level_operands(l):
                m = seq[l]
                dve.wait_ge(level_exp, l + 1)
                to = X[:, l % 2, :, :]
                x_lo, x_up = halves(to, m)
                q_up = halves(qq[:, :, :], m)[1]
                k_lo = halves(kk[:, :, :], m)[0]
                nc.vector.tensor_tensor(x_up, x_up, q_up, ALU.mult)
                nc.vector.tensor_tensor(x_lo, x_lo, k_lo, ALU.mult).then_inc(level_ready, 1)

            def level_pick(l):
                if l == len(seq) - 1:
                    dve.wait_ge(level_done, 4 * l + 6)
                    nc.vector.tensor_copy(S_off[:, :, :, :],
                                          banks[:, 2:4, :].rearrange("p b (a t) -> p b a t", a=4))\
                        .then_inc(level_read, 1)
                    return
                mask = ident if l < 0 else level_mask[seq[l]]
                for b in range(4):
                    dve.wait_ge(level_done, 4 * (l + 1) + b + 1)
                    nc.vector.copy_predicated(
                        S[:, b, :, :], mask.bitcast(U32).unsqueeze(1).broadcast_to([P, 4, P]),
                        banks[:, b, :].rearrange("p (a t) -> p a t", a=4)).then_inc(level_read, 1)

            nc.vector.memset(S[:, :, :, :], 0.0)
            n = first["w_in"]
            j0 = tile_at["w_in"]
            for i in range(44):
                if i < 4:
                    dve.wait_ge(tile_read["act"], reads("act", j0 + i))
                    ins = nc.vector.tensor_scalar(lf[:, i, :], kk[:, i, :], lbw[:, 7, i:i + 1],
                                                  lbw[:, 6, i:i + 1], ALU.mult, ALU.add)
                    link(ins)
                    ins = nc.vector.tensor_scalar(kk[:, i, :], lf[:, i, :], -1.0, 1.0, ALU.mult, ALU.add)
                    if i == 3:
                        ins.then_inc(forget_ready, 1)
                elif i < 8:
                    dve.wait_ge(tile_read["act"], reads("act", j0 + i))
                    nc.vector.tensor_scalar(qq[:, i - 4, :], qq[:, i - 4, :], SCALE, None, ALU.mult)
                elif 20 <= i < 24:
                    dve.wait_ge(slab_used, n + i + 1)
                    c = i - 20
                    dve.wait_ge(tile_read["act"], reads("act", j0 + 19))
                    nc.vector.tensor_tensor(uu[:, c, 2:T + 2], tile_buf(j0 + i), cc[:, c, :],
                                            ALU.mult).then_inc(tile_read["dve"], 1)
                    dve.wait_ge(tile_read["dve"], reads("dve", j0 + i))
                    link(nc.vector.tensor_scalar(conv[:, c, :], uu[:, c, 0:T], col("conv", c), None, ALU.mult))
                    for tap in (1, 2):
                        link(nc.vector.scalar_tensor_tensor(conv[:, c, :], uu[:, c, tap:tap + T],
                                                            col("conv", 4 * tap + c), conv[:, c, :],
                                                            ALU.mult, ALU.add))
                elif 24 <= i < 28:
                    c = i - 24
                    dve.wait_ge(slab_used, n + i + 1)
                    nc.vector.tensor_tensor(y32[:, 4 + c, :], tile_buf(j0 + i), conv[:, c, :],
                                            ALU.mult).then_inc(tile_read["dve"], 1)
                split_lo(n + i + RING)
                l = (i - FIRST_LEVEL) // 2
                if i == FIRST_LEVEL - 1:
                    dve.wait_ge(logf_ready, 1)
                    for a in range(4):
                        ins = nc.vector.tensor_tensor_scan(bb[:, a, :], chunk_mask, lf[:, a, :], 0.0,
                                                           ALU.mult, ALU.add)
                    link(ins)
                    level_prepare(0)
                if i > FIRST_LEVEL and (i - FIRST_LEVEL) % 2 == 1 and l < 8:
                    if l < 7:
                        level_prepare(l + 1)
                    level_operands(l)
                    level_pick(l - 1)
                if i == FIRST_LEVEL + 17:
                    level_pick(7)
                if i == FIRST_LEVEL + 19:
                    y_low(1, 4, 8)
                if i == FIRST_LEVEL + 23:
                    dve.wait_ge(o_root, 1)
                    link(nc.vector.reciprocal(orr[:, :, :], orr[:, :, :]))
                    link(nc.vector.tensor_tensor(orr[:, :, :], fronts.rearrange("p b (a t) -> p (b a) t", a=2),
                                                 orr[:, :, :], ALU.mult))
                    for a in range(4):
                        ins = nc.vector.scalar_tensor_tensor(y32[:, a, :], orr[:, a, :], col("out_g", a),
                                                             hgs[:, a, :], ALU.mult, ALU.mult)
                    ins.then_inc(y32_ready, 1)
                if i == FIRST_LEVEL + 26:
                    y_low(2, 0, 4)

            n = first["branch"]
            j0 = tile_at["branch"]
            for m in range(8):
                j = j0 + m
                dve.wait_ge(slab_used, n + m + 1)
                nc.vector.tensor_tensor(h32[:, m, :], tile_buf(j), sg[:, m, :], ALU.mult)
                nc.vector.tensor_tensor(sq[:, m, :], tile_buf(j, 1), sg[:, 8 + m, :], ALU.mult)\
                    .then_inc(tile_read["dve"], 1)
                dve.wait_ge(tile_read["dve"], reads("dve", j))
                nc.vector.tensor_tensor(h32[:, m, :], h32[:, m, :], sq[:, m, :], ALU.add)\
                    .then_inc(merged_ready, 1)
                split_lo(n + m + RING)
                dve.wait_ge(merged_hi, m + 1)
                nc.vector.tensor_tensor(h_lo[:, m, :], h32[:, m, :], h_hi[:, m, :].bitcast(F32),
                                        ALU.subtract).then_inc(merged_lo, 1)
            n = first["w_out"]
            for m in range(8):
                add_tile("w_out", m)
                split_lo(n + m + RING)
            if "peer" in first:
                operand_lo(1, 1, "norm_ffn_g")
                inverse_rms(1)
                n = first["wquery"]

                def mark(ins):
                    ins.then_inc(dve_own, 1)
                    own[0] += 1
                    return own[0]

                def best_sixteen(v, ix, s, left):
                    both = range(TT)
                    first8, last8 = slice(0, 8), slice(8, 16)
                    found = [mark(nc.vector.max(v[tt][:, first8], s[tt])) for tt in both]
                    cleared = []
                    for tt in both:
                        dve.wait_ge(dve_own, found[tt])
                        placed = mark(nc.vector.max_index(ix[tt][:, first8], v[tt][:, first8], s[tt]))
                        if left is s:
                            dve.wait_ge(dve_own, placed)
                        cleared.append(mark(nc.vector.match_replace(left[tt], v[tt][:, first8], s[tt], NEG)))
                    found = []
                    for tt in both:
                        dve.wait_ge(dve_own, cleared[tt])
                        found.append(mark(nc.vector.max(v[tt][:, last8], left[tt])))
                    for tt in both:
                        dve.wait_ge(dve_own, found[tt])
                        placed = mark(nc.vector.max_index(ix[tt][:, last8], v[tt][:, last8], left[tt]))
                    return placed

                def best_keys(i):
                    dve.wait_ge(keys_done, i + 1)
                    placed = best_sixteen([top_v[:, tt, i, :] for tt in range(TT)],
                                          [top_i[:, tt, i, :] for tt in range(TT)],
                                          [fronts[:, i % 2, tt * P:(tt + 1) * P] for tt in range(TT)],
                                          [rest[:, tt, :] for tt in range(TT)])
                    dve.wait_ge(dve_own, placed)
                    nc.vector.tensor_copy(top_f[:, :, i, :], top_i[:, :, i, :]).then_inc(keys_read, 1)

                for i in range(16):
                    dve.wait_ge(slab_used, n + i + 1)
                    if i == 1:
                        r_columns(1)
                    if i >= 1:
                        best_keys(i - 1)
                best_keys(15)
                for h in range(HEADS):
                    for tt in range(TT):
                        summed = mark(nc.vector.tensor_tensor(
                            cand[:, tt, :, :],
                            top_v[:, tt, 2 * h, :].unsqueeze(2).broadcast_to([P, TOPK, TOPK]),
                            top_v[:, tt, 2 * h + 1, :].unsqueeze(1).broadcast_to([P, TOPK, TOPK]), ALU.add))
                    dve.wait_ge(dve_own, summed)
                    flat = [cand[:, tt, :, :].rearrange("p a b -> p (a b)") for tt in range(TT)]
                    placed = best_sixteen([best[:, tt, h, :] for tt in range(TT)],
                                          [pos[:, tt, h, :] for tt in range(TT)], flat, flat)
                    dve.wait_ge(dve_own, placed)
                link(nc.vector.tensor_tensor(gts[:, :, :, :], best[:, :, :, :],
                                             best[:, :, :, 0:1].broadcast_to([P, TT, HEADS, TOPK]),
                                             ALU.subtract))
                for tt in range(TT):
                    ins = nc.vector.tensor_scalar(gts[:, tt, :, :], gts[:, tt, :, :], r_col[:, tt:tt + 1],
                                                  None, ALU.mult)
                ins.then_inc(gate_diff, 1)
                link(nc.vector.tensor_scalar(pos1[:, :, :, :], pos[:, :, :, :], 4, None,
                                             ALU.logical_shift_right))
                link(nc.vector.tensor_scalar(pos2[:, :, :, :], pos[:, :, :, :], 15, None,
                                             ALU.bitwise_and))
                nc.vector.tensor_copy(posf[:, 0, :, :, :], pos1[:, :, :, :])
                link(nc.vector.tensor_copy(posf[:, 1, :, :, :], pos2[:, :, :, :]))
                for side in range(2):
                    for tt in range(TT):
                        flat = onehot[:, :, :, :].rearrange("p h k a -> p (h k) a")
                        link(nc.vector.tensor_tensor(
                            flat, posf[:, side, tt, :, :].rearrange("p h k -> p (h k)").unsqueeze(2)
                            .broadcast_to([P, P, TOPK]),
                            iota[:, 0:TOPK].unsqueeze(1).broadcast_to([P, P, TOPK]), ALU.is_equal))
                        link(nc.vector.tensor_tensor(
                            onehot[:, :, :, :], onehot[:, :, :, :],
                            top_f[:, tt, side:PEER_GROUPS:2, :].unsqueeze(2)
                            .broadcast_to([P, HEADS, TOPK, TOPK]), ALU.mult))
                        link(nc.vector.tensor_reduce(
                            idx[:, side, tt, :, :].rearrange("p h k -> p (h k)"), flat, AX_X, ALU.add))
                dve.wait_ge(gate_exp, 1)
                link(nc.vector.tensor_reduce(gsum[:, :, :, 0], gts[:, :, :, :], AX_X, ALU.add))
                link(nc.vector.reciprocal(gsum[:, :, :, 1], gsum[:, :, :, 0]))
                nc.vector.tensor_tensor(gts[:, :, :, :], gts[:, :, :, :],
                                        gsum[:, :, :, 1:2].broadcast_to([P, TT, HEADS, TOPK]),
                                        ALU.mult).then_inc(picks_ready, 1)
                dve.wait_ge(picks_copied, 3)

                def pick_rows(t, k):
                    for rows, idx_T, there in ((pick1, idx1_T, pick1_there), (pick2, idx2_T, pick2_ready)):
                        nc.vector.tensor_tensor(rows[:, k, :, :], iota.unsqueeze(1).broadcast_to([P, 4, P]),
                                                idx_T[:, t].unsqueeze(2).broadcast_to([P, 4, P]),
                                                ALU.is_equal).then_inc(there, 4)

                for k in range(2):
                    pick_rows(slice(4 * k, 4 * k + 4), k)
                with dve.Fori(0, (T - 8) // 8) as turn:
                    for k in range(2):
                        dve.wait_ge(pick_used, turn * 8 + (4 * k + 4))
                        pick_rows(bass.ds(turn * 8 + (8 + 4 * k), 4), k)
                dve.wait_ge(lo_ready, first["peer"] + RING)
                dve.wait_ge(g_copied, T // 4)
                dve.wait_ge(pick_used, T)
                mlp(first["peer"], NKEYS, 1, 0)
                dve.wait_ge(slab_used, first["peer"] + 2 * NKEYS)
                for k in range(0, KT, 2):
                    nc.vector.tensor_copy(x[:, k:k + 2, :], acc[:, k:k + 2, :]).then_inc(x_ready, 1)
                inverse_rms(2)
                scale_x("norm_final_g", x, x_ready)
            done = NKEYS
            q = 3
            ys = 2
            for kind, i in layer_stages():
                operand_lo(q, q - 1, stage_gain(kind, i))
                inverse_rms(q)
                q += 1
                if kind == "ffn":
                    mlp(first[f"ffn{i}"], FT, 2, done)
                    done += FT
                    dve.wait_ge(slab_used, first[f"ffn{i}"] + 3 * FT)
                    for b in range(4):
                        ins = nc.vector.scalar_tensor_tensor(x[:, 2 * b:2 * b + 2, :],
                                                             acc[:, 2 * b:2 * b + 2, :], 0.5,
                                                             x[:, 2 * b:2 * b + 2, :], ALU.mult, ALU.add)\
                            .then_inc(x_ready, 1)
                elif kind == "even":
                    dve.wait_ge(attc_sem, 32)
                    nc.vector.memset(pu[:, :, 0:PAD], 0.0)
                    nc.vector.memset(win[:, :, 0:PAD], 0.0)
                    n = first["even_in"]
                    for i in range(16):
                        if i == 2:
                            r_columns(2)
                        if i < 4:
                            take("even_in", i, aq[:, i, :])
                        elif i < 8:
                            take("even_in", i, ak[:, i - 4, :])
                        elif i >= 12:
                            take("even_in", i, pu[:, i - 12, PAD:PAD + T])
                        split_lo(n + i + RING)
                    j0 = tile_at["even_in"]
                    dve.wait_ge(tile_read["dve"], reads("dve", j0 + 15))
                    for g, w in enumerate(WINDOWS):
                        src = pu[:, g, :]
                        if g:
                            dve.wait_ge(pooled_ready, g)
                        for r in range(g + 1):
                            to = win[:, r % 2, :]
                            link(nc.vector.tensor_tensor(to[:, PAD:], src[:, PAD:],
                                                         src[:, PAD - 2 ** r:PAD - 2 ** r + T], ALU.add))
                            src = to
                        link(nc.vector.tensor_tensor(src[:, PAD:], src[:, PAD:], inv_count[:, g, :],
                                                     ALU.mult))
                        nc.vector.tensor_tensor(pooled[:, g, :], src[:, PAD:], pu[:, g, PAD:],
                                                ALU.subtract).then_inc(pooled_ready, 1)
                    for g in range(2):
                        a, b = 4 * g, 4 * g + 4
                        dve.wait_ge(ln_ready, g + 1)
                        link(nc.vector.scalar_tensor_tensor(asp[:, a:b, :], az[:, a:b, :], 0.0,
                                                            asp[:, a:b, :], ALU.max, ALU.add))
                        nc.vector.tensor_tensor(aL[:, a:b, :], asp[:, a:b, :],
                                                past_neg.unsqueeze(1).broadcast_to([P, 4, 3 * P]),
                                                ALU.mult).then_inc(stick_L, 1)
                        link(nc.vector.tensor_tensor(az[:, a:b, :], az[:, a:b, :], asp[:, a:b, :],
                                                     ALU.subtract))
                    for h in range(HEADS):
                        dve.wait_ge(later_done, h + 1)
                        nc.vector.tensor_tensor(az[:, h, :], banks[:, h % 4, 0:3 * P], az[:, h, :],
                                                ALU.add).then_inc(stick_w, 1)
                    for g in range(2):
                        a, b = 4 * g, 4 * g + 4
                        dve.wait_ge(stick_e, g + 1)
                        nc.vector.scalar_tensor_tensor(az[:, a:b, :], az[:, a:b, :], -1.0,
                                                       past_neg.unsqueeze(1).broadcast_to([P, 4, 3 * P]),
                                                       ALU.mult, ALU.mult).then_inc(stick_a, 1)
                    dve.wait_ge(pool_done, 4)
                    for g in range(4):
                        nc.vector.tensor_scalar(y32[:, 4 + g, :], tile[:, g, :],
                                                col("pool_scale", g), None, ALU.mult)\
                            .then_inc(tile_read["dve"], 1)
                    y_low(ys + 1, 0, 4)
                    y_low(ys + 2, 4, 8)
                    ys += 2
                    n = first["even_out"]
                    for m in range(8):
                        add_tile("even_out", m)
                        split_lo(n + m + RING)
                else:
                    n = first["qkv"]
                    for i in range(24):
                        if i == 2:
                            r_columns(3)
                        if i < 8:
                            take("qkv", i, bq[:, i, :], SCALE)
                        elif i < 16:
                            take("qkv", i, bk[:, i - 8, :])
                        split_lo(n + i + RING)
                    for h in range(ODD_HEADS + 1):
                        if h < ODD_HEADS:
                            k = h % 4
                            slope = float(2.0 ** (-8.0 * (h + 1) / ODD_HEADS))
                            dve.wait_ge(sc_done, h + 1)
                            if h >= 4:
                                dve.wait_ge(p_turned, h - 3)
                            link(nc.vector.scalar_tensor_tensor(sc[:, k, :], dist, slope,
                                                                banks[:, h % 4, 0:3 * P],
                                                                ALU.mult, ALU.add))
                            nc.vector.tensor_reduce(st[:, 0, k, 0:1], sc[:, k, 0:P], AX_X, ALU.max,
                                                    negate=True)
                            nc.vector.tensor_reduce(st[:, 0, k, 1:2], sc[:, k, P:3 * P], AX_X, ALU.max,
                                                    negate=True).then_inc(sc_read, 1)
                        if h >= 1:
                            k = (h - 1) % 4
                            dve.wait_ge(p_exp, 2 * h)
                            link(nc.vector.reciprocal(st[:, 2, k, :], st[:, 1, k, :]))
                            nc.vector.tensor_scalar(sc[:, k, 0:P], sc[:, k, 0:P], st[:, 2, k, 0:1], None,
                                                    ALU.mult)
                            nc.vector.tensor_scalar(sc[:, k, P:3 * P], sc[:, k, P:3 * P],
                                                    st[:, 2, k, 1:2], None, ALU.mult).then_inc(p_norm, 1)
                    y_low(ys + 1, 0, 4)
                    y_low(ys + 2, 4, 8)
                    ys += 2
                    n = first["w_o"]
                    for m in range(8):
                        add_tile("w_o", m)
                        split_lo(n + m + RING)
            if STOP in ("mix", "even", "odd"):
                dve.wait_ge(tile_read["dve"], len([r for r in readers if r == "dve"]))
            elif STOP is not None:
                dve.wait_ge(x_ready, x_pairs if STOP != "peer" else 8)
            if STOP is None:
                inverse_rms(q)
                link(scale_x("norm_final", h32))
            dve.sem_inc(result_ready, 1)

        @block.tensor
        def _(pe):
            def mm(out, lhsT, rhs, start, stop, **kw):
                return nc.tensor.matmul(out, lhsT, rhs, start=start, stop=stop, **kw)

            def wait_slab(n, turn=None, per=0):
                pe.wait_ge(lo_ready, n + 1 if turn is None else turn * per + (n + 1))

            def three(out, s, c, r_hi, r_lo, start, stop, **kw):
                hi, lo = w_hi[:, s, c:c + P], w_lo[:, s, c:c + P]
                mm(out, hi, r_hi, start, False, **kw)
                mm(out, hi, r_lo, False, False, **kw)
                return mm(out, lo, r_hi, False, stop, **kw)

            def free_tile(j):
                if j >= 2:
                    r = readers[j - 2]
                    pe.wait_ge(tile_read[r], reads(r, j - 2))

            def project(name, i, n, hi, lo, lows=None):
                j = tile_at[name] + i
                free_tile(j)
                wait_slab(n)
                for k in range(KT):
                    if lows is not None:
                        pe.wait_ge(nh_lo, lows + k + 1)
                    ins = three(tile_buf(j), n % RING, k * P, hi[:, k, :], lo[:, k, :],
                                k == 0, k == KT - 1)
                ins.then_inc(slab_used, 1)

            def project_tokens(name, i, c, n, hi, lo):
                j = tile_at[name] + i
                if c == 0:
                    free_tile(j)
                    free_tile(j + 1)
                elif c >= 4:
                    pe.wait_ge(tile_read["act"], reads("act", j - 3))
                wait_slab(n + 1)
                s = n % RING
                assert s % 2 == 0
                for tt in range(TT):
                    o = pair_buf(c, tt)
                    for k in range(KT):
                        a, b = hi[:, k, tt * P:(tt + 1) * P], lo[:, k, tt * P:(tt + 1) * P]
                        w = [part[:, s:s + 2, k * P:(k + 1) * P] for part in (w_hi, w_lo)]
                        mm(o, a, w[0], k == 0, False)
                        mm(o, b, w[0], False, False)
                        ins = mm(o, a, w[1], False, k == KT - 1)
                ins.then_inc(slab_used, 2)

            def norm(q):
                pe.wait_ge(sq_summed, q)
                mm(sum_at[q], ones, sq[:, 0, :], True, True).then_inc(sums, 1)

            def turn_rstd(q):
                pe.wait_ge(rstd_ready, q + 1)
                if q >= 3:
                    pe.wait_ge(attc_sem, 32)
                for tt in range(TT):
                    ins = nc.tensor.transpose(front[:, 1, tt * P:(tt + 1) * P], rstd[:, tt * P:(tt + 1) * P],
                                              ident if q < 3 else ident2)
                ins.then_inc(r_turned, 1)

            def mlp(n0, steps, fronts_, done, seeded, q=None):
                per_step = fronts_ + 1

                def wait(turn, turns, sm, v):
                    if turn is None:
                        pe.wait_ge(sm, v)
                    else:
                        pe.wait_ge(sm, turn * turns + v)

                def feed(s, n, turn=None, turns=0):
                    S0 = done + s
                    if s >= 2 or turn is not None:
                        wait(turn, turns, scaled_ready, S0 - 1)
                    for f in range(fronts_):
                        wait_slab(n + f, turn, turns * per_step)
                        for k in range(KT):
                            if q is not None and s == 0 and f == 0:
                                pe.wait_ge(nh_lo, 8 * (q - 1) + k + 1)
                            ins = three(fronts[:, s % 2, f * T:(f + 1) * T], (n + f) % RING, k * P,
                                        h_hi[:, k, :], h_lo[:, k, :], k == 0, k == KT - 1)
                        ins.then_inc(slab_used, 1)

                def drain(s, n, turn=None, turns=0):
                    S0 = done + s
                    wait(turn, turns, mid_lo_ready, S0 + 1)
                    wait_slab(n, turn, turns * per_step)
                    begin = s == 0 and not seeded and turn is None
                    for m in range(KT):
                        ins = three(acc[:, m, :], n % RING, m * P, mid_hi[:, s % 2, :], mid_lo[:, s % 2, :],
                                    begin and m % 2 == 0, False, skip_group_check=True)
                    ins.then_inc(slab_used, 1)

                feed(0, n0)
                n = n0 + fronts_
                turns = 4 if fronts_ == 2 else 2
                feed(1, n)
                if q is not None:
                    norm(q)
                drain(0, n + fronts_)
                n += per_step
                loops = (steps - 2) // turns
                with pe.Fori(0, loops) as turn:
                    for c in range(turns):
                        feed(2 + c, n + c * per_step, turn, turns)
                        drain(1 + c, n + c * per_step + fronts_, turn, turns)
                for s in range(2 + loops * turns, steps):
                    m = n + (s - 2) * per_step
                    feed(s, m)
                    drain(s - 1, m + fronts_)
                drain(steps - 1, n0 + steps * per_step - 1)

            pe.wait_ge(squares, 1)
            for k in range(KT):
                ins = mm(sum_at[0], ones, sq[:, k, :], k == 0, k == KT - 1)
            ins.then_inc(sums, 1)
            pe.wait_ge(nh_lo, 8)
            def head(ap, h, tt):
                p = DH * (h % 2)
                return ap[p:p + DH, h // 2, tt * P:(tt + 1) * P]

            def level_scores(l):
                if l >= 0:
                    pe.wait_ge(level_ready, l + 1)
                else:
                    pe.wait_ge(forget_ready, 1)
                    pe.wait_ge(level_diff, 1)
                for bank in range(4):
                    tt = bank // 2
                    if l == 7 and tt == 0:
                        continue
                    if l >= 0:
                        pe.wait_ge(level_read, 4 * l + bank + 1)
                    for h in range(bank % 2, HEADS, 2):
                        if l < 0:
                            a, b = head(kk, h, tt), head(qq, h, tt)
                        else:
                            a = head(X[:, l % 2, :, :], h, tt if l < 7 else 0)
                            b = head(X[:, l % 2, :, :], h, tt)
                        ins = mm(banks[:, bank, (h // 2) * P:(h // 2 + 1) * P], a, b, True, True)
                    ins.then_inc(level_done, 1)

            def outputs(v, h, to, scores):
                p = DH * (h % 2)
                w = [v[:, tt, h * DH:(h + 1) * DH] for tt in range(TT)]
                o = to[p:p + DH, :]
                mm(o[:, 0:P], w[0], scores[0], True, True)
                mm(o[:, P:T], w[0], scores[1], True, False)
                return mm(o[:, P:T], w[1], scores[2], False, True)

            fr = fronts.rearrange("p b (a t) -> p (b a) t", a=2)
            n = first["w_in"]
            for i in range(44):
                if i in (8, 10):
                    project_tokens("w_in", i, i - 8, n + i, h_hi, h_lo)
                elif i not in (9, 11):
                    project("w_in", i, n + i, h_hi, h_lo)
                l = (i - FIRST_LEVEL) // 2 - 1
                if i >= FIRST_LEVEL and (i - FIRST_LEVEL) % 2 == 0 and l < 8:
                    level_scores(l)
                if i == FIRST_LEVEL + 19:
                    pe.wait_ge(level_read, 33)
                    pe.wait_ge(tile_read["act"], reads("act", tile_at["w_in"] + 11))
                    for h in range(HEADS):
                        ins = outputs(vv, h, fr[:, h // 2, :],
                                      (S[:, h % 2, h // 2, :], S_off[:, h % 2, h // 2, :],
                                       S[:, 2 + h % 2, h // 2, :]))
                    ins.then_inc(o_done, 1)
                if i == FIRST_LEVEL + 21:
                    pe.wait_ge(o_sq, 1)
                    for b in range(2):
                        ins = mm(banks[:, b, :], head_ones,
                                 osq[:, 2 * b:2 * b + 2, :].rearrange("p a t -> p (a t)"), True, True)
                    ins.then_inc(o_sum, 1)
            pe.wait_ge(y_lo_ready, 2)
            n = first["branch"]
            for m in range(8):
                wait_slab(n + m)
                j = tile_at["branch"] + m
                free_tile(j)
                for half in range(2):
                    for k in range(4):
                        kk_ = 4 * half + k
                        ins = three(tile_buf(j, half), (n + m) % RING, kk_ * P, y_hi[:, kk_, :],
                                    y_lo[:, kk_, :], k == 0, k == 3)
                ins.then_inc(slab_used, 1)
            pe.wait_ge(merged_lo, 8)
            n = first["w_out"]
            for m in range(8):
                project("w_out", m, n + m, h_hi, h_lo)
            if "peer" in first:
                for m in range(KT):
                    wait_x(pe, 1, m)
                    ins = mm(acc[:, m, :], ident, x[:, m, :], m % 2 == 0, False, skip_group_check=True)
                ins.then_inc(x_seeded, 1)
                norm(1)
                pe.wait_ge(keys_in_sem, 16)
                n = first["wquery"]

                def key_scores(i):
                    j = tile_at["wquery"] + i
                    pe.wait_ge(tile_read["act"], reads("act", j))
                    if i == 1:
                        pe.wait_ge(r_col_ready, 1)
                    if i >= 2:
                        pe.wait_ge(keys_read, i - 1)
                    for tt in range(TT):
                        ins = mm(fronts[:, i % 2, tt * P:(tt + 1) * P], qT[:, i, tt * P:(tt + 1) * P],
                                 keysT[:, i, :], True, True)
                    ins.then_inc(keys_done, 1)

                for i in range(16):
                    project("wquery", i, n + i, h_hi, h_lo, 8 if i == 0 else None)
                    if i == 0:
                        turn_rstd(1)
                    if i >= 1:
                        key_scores(i - 1)
                key_scores(15)
                pe.wait_ge(picks_ready, 1)
                for i in range(3):
                    for tt in range(TT):
                        src = gts[:, tt, :, :] if i == 2 else idx[:, i, tt, :, :]
                        ins = nc.tensor.transpose(tile[:, i, tt * P:(tt + 1) * P],
                                                  src.rearrange("p h k -> p (h k)"), ident)
                ins.then_inc(picks_turned, 1)
                def weights(b, c, k):
                    if b < 2:
                        o = fronts[:, b, c * P:(c + 1) * P]
                    else:
                        o = tile[:, 2 * b - 4 + c // 2, (c % 2) * P:(c % 2 + 1) * P]
                    mm(o, pick1[:, b % 2, k, :], pick2[:, b % 2, k, :], True, True).then_inc(pick_used, 1)

                pe.wait_ge(picks_copied, 3)
                for t in range(16):
                    pe.wait_ge(pick1_ready, t + 1)
                    pe.wait_ge(pick2_ready, t + 1)
                    weights(t // 4, t % 4, t % 4)
                with pe.Fori(0, T // 16 - 1) as turn:
                    for b in range(4):
                        pe.wait_ge(g_copied, turn * 4 + (b + 1))
                        for c in range(4):
                            pe.wait_ge(pick1_ready, turn * 16 + (16 + 4 * b + c + 1))
                            pe.wait_ge(pick2_ready, turn * 16 + (16 + 4 * b + c + 1))
                            weights(b, c, c)
                pe.wait_ge(g_copied, T // 4)
                mlp(first["peer"], NKEYS, 1, 0, True)
                norm(2)
            done = NKEYS
            q = 3
            ys = 2
            for kind, i in layer_stages():
                lows = 8 * (q - 1)
                q += 1
                if kind == "ffn":
                    mlp(first[f"ffn{i}"], FT, 2, done, False, q - 1)
                    done += FT
                elif kind == "even":
                    n = first["even_in"]
                    for i in range(16):
                        if i in (8, 10):
                            project_tokens("even_in", i, i - 8, n + i, h_hi, h_lo)
                        elif i not in (9, 11):
                            project("even_in", i, n + i, h_hi, h_lo, lows if i == 0 else None)
                        if i == 1:
                            norm(q - 1)
                            turn_rstd(q - 1)
                    for h in range(HEADS):
                        p = DH * (h % 2)
                        if h == 0:
                            pe.wait_ge(tile_read["dve"], reads("dve", tile_at["even_in"] + 15))
                            pe.wait_ge(tile_read["act"], reads("act", tile_at["even_in"] + 15))
                        if h >= 4:
                            pe.wait_ge(z_read, h - 3)
                        k_ = ak[p:p + DH, h // 2, :]
                        q_ = aq[p:p + DH, h // 2, :]
                        mm(banks[:, h % 4, 0:T], k_[:, 0:P], q_, True, True)
                        mm(banks[:, h % 4, T:T + P], k_[:, P:T], q_[:, P:T], True, True)\
                            .then_inc(z_done, 1)
                    for g in range(4):
                        pe.wait_ge(pooled_ready, g + 1)
                        mm(tile[:, g, :], wpool[:, g, :], pooled[:, g, :], True, True)\
                            .then_inc(pool_done, 1)
                    for h in range(HEADS):
                        pe.wait_ge(stick_L, h // 4 + 1)
                        if h < 4:
                            pe.wait_ge(z_read, 8)
                        else:
                            pe.wait_ge(stick_w, h - 3)
                        o = banks[:, h % 4, 0:3 * P]
                        mm(o, later, aL[:, h, :], True, True)
                        mm(o[:, P:2 * P], ones, aL[:, h, 2 * P:3 * P], False, True, skip_group_check=True)\
                            .then_inc(later_done, 1)
                    for h in range(HEADS):
                        pe.wait_ge(stick_a, h // 4 + 1)
                        ins = outputs(av, h, fr[:, h // 2, :], [az[:, h, c * P:(c + 1) * P] for c in range(3)])
                    ins.then_inc(ao_done, 1)
                    pe.wait_ge(y_lo_ready, ys + 2)
                    ys += 2
                    n = first["even_out"]
                    for m in range(8):
                        project("even_out", m, n + m, y_hi, y_lo)
                else:
                    n = first["qkv"]
                    for i in range(24):
                        if i >= 16:
                            if i % 2 == 0:
                                project_tokens("qkv", i, i - 16, n + i, h_hi, h_lo)
                        else:
                            project("qkv", i, n + i, h_hi, h_lo, lows if i == 0 else None)
                        if i == 1:
                            norm(q - 1)
                            turn_rstd(q - 1)
                    pe.wait_ge(tile_read["act"], reads("act", tile_at["qkv"] + 23))
                    for h in range(ODD_HEADS + 3):
                        if h < ODD_HEADS:
                            p = DH * (h % 2)
                            if h >= 4:
                                pe.wait_ge(sc_read, h - 3)
                            k_ = bk[p:p + DH, h // 2, :]
                            q_ = bq[p:p + DH, h // 2, :]
                            mm(banks[:, h % 4, 0:P], q_[:, 0:P], k_[:, 0:P], True, True)
                            mm(banks[:, h % 4, P:3 * P], q_[:, P:T], k_, True, True).then_inc(sc_done, 1)
                        if 2 <= h <= ODD_HEADS + 1:
                            g = h - 2
                            pe.wait_ge(p_norm, g + 1)
                            if g >= 2:
                                pe.wait_ge(p_copied, g - 1)
                            o = fronts[:, g % 2, :]
                            nc.tensor.transpose(o[:, 0:P], sc[:, g % 4, 0:P], ident2)
                            nc.tensor.transpose(o[:, P:2 * P], sc[:, g % 4, P:2 * P], ident2)
                            nc.tensor.transpose(o[:, 2 * P:3 * P], sc[:, g % 4, 2 * P:3 * P], ident2)\
                                .then_inc(p_turned, 1)
                        if h >= 3:
                            g = h - 3
                            pe.wait_ge(p_copied, g + 1)
                            if g == 8:
                                pe.wait_ge(y_hi_ready, ys + 1)
                            outputs(bv, g, tile[:, (g // 2) % 4, :],
                                    [pT[:, g % 2, c * P:(c + 1) * P] for c in range(3)]).then_inc(bo_done, 1)
                    pe.wait_ge(y_lo_ready, ys + 2)
                    ys += 2
                    n = first["w_o"]
                    for m in range(8):
                        project("w_o", m, n + m, y_hi, y_lo)
            if STOP is None:
                norm(q)


def tiles(w):
    K, N = w.shape
    return w.reshape(K // P, P, N // P, P).transpose(2, 1, 0, 3).reshape(N // P, P, K)


def slabs(inputs):
    w_in = inputs["w_in"][0]
    order = [512, 0, 1024, 1536, 2560, 3072, 2048]
    parts = [tiles(w_in[:, o:o + 512]) for o in order] + [tiles(w_in[:, 3584:])]
    wa, wb = tiles(inputs["w_branch_hg"][0]), tiles(inputs["w_branch_conv"][0])
    parts.append(np.concatenate([wa, wb], 2))
    parts.append(tiles(inputs["w_out"][0]))
    parts.append(tiles(inputs["peer_w_query"][0]))
    u = inputs["peer_u"][0].reshape(P, P, KT, P).transpose(1, 3, 2, 0).reshape(P, P, D)
    v = inputs["peer_v"][0].reshape(P, P, D).transpose(1, 0, 2)
    pair = np.stack([u[1:], v[:-1]], 1).reshape(2 * (P - 1), P, D)
    parts += [u[0:1], pair, v[-1:]]

    def ffn(pre, layer):
        g = tiles(inputs[f"{pre}_gate_2"][layer])
        up = tiles(inputs[f"{pre}_up_2"][layer])
        down = inputs[f"{pre}_down_2"][layer].reshape(FT, P, D)
        body = np.stack([g[1:], up[1:], down[:-1]], 1).reshape(3 * (FT - 1), P, D)
        return [g[0:1], up[0:1], body, down[-1:]]

    parts += ffn("ffn1", 0)
    parts += [tiles(inputs["even_w_in_2"][0]), tiles(inputs["even_w_out_2"][0])]
    parts += ffn("ffn2", 0) + ffn("ffn1", 1)
    parts += [tiles(inputs["odd_w_qkv_2"][0]), tiles(inputs["odd_w_o_2"][0])]
    parts += ffn("ffn2", 1)
    return np.concatenate(parts, 0)


def by_feature(v):
    return v.reshape(-1, P).T


def kernel(**inputs):
    import concourse.bacc as _bacc
    from concourse.bass_utils import run_bass_kernel_spmd as _run

    inputs = {k: np.asarray(v) for k, v in inputs.items()}
    n = stream_plan()[1]
    vectors = [inputs["norm_mix_g"][0], inputs["norm_ffn_g"][0], inputs["norm_final_g"]]
    for layer in range(2):
        vectors += [inputs["norm_ffn1_2"][layer], inputs["norm_mix_2"][layer], inputs["norm_ffn2_2"][layer]]
    vectors += [inputs["norm_final_2"], inputs["hg_lb_logits"][0], inputs["hg_lb_logits"][1],
                inputs["hg_out_norm_g"][0], *inputs["conv_w"][0], inputs["even_pool_scale_2"][0]]
    k1, k2 = inputs["peer_keys1"][0], inputs["peer_keys2"][0]
    arrays = {
        "stream": slabs(inputs)[:n],
        "x_t": inputs["x"][0].T.reshape(KT, P, T).transpose(1, 0, 2),
        "columns": np.concatenate([by_feature(v) for v in vectors] + [np.full((P, 1), EPS, np.float32)], 1),
        "lanes": np.stack([np.ones((P, P), np.float32),
                           np.broadcast_to(np.arange(P, dtype=np.float32), (P, P))], 1),
        "keys_t": np.stack([k1, k2], 1).reshape(PEER_GROUPS, NKEYS, P).transpose(2, 0, 1),
        "w_pool": inputs["even_w_pool_2"][0].transpose(1, 0, 2),
        "mixer_constants": mixer_constants(),
        "attention_constants": attention_constants(),
    }
    nc = _bacc.Bacc("TRN2", target_bir_lowering=False, num_devices=1)
    args = []
    for name in arrays:
        arrays[name] = np.ascontiguousarray(arrays[name])
        args.append(nc.dram_tensor(name, arrays[name].shape, F32, kind="ExternalInput").ap())
    args.append(nc.dram_tensor("out_t", (P, KT, T), F32, kind="ExternalOutput").ap())
    build(nc, *args)
    r = _run(nc, [arrays], core_ids=[0])
    got = r.results[0]["out_t"]
    return got.transpose(1, 0, 2).reshape(D, T).T.reshape(1, T, D)
```

```python
from contextlib import ExitStack

import numpy as np

import concourse.bass as bass
from concourse import mybir
from concourse.alu_op_type import AluOpType as ALU

ACT = mybir.ActivationFunctionType
AX_X = mybir.AxisListType.X
F32 = mybir.dt.float32
F32R = mybir.dt.float32r
U32 = mybir.dt.uint32

P = 128
T = 256
D = 1024
KT = D // P
TT = T // P
HEADS = 8
DH = 64
CHUNK = 64
NKEYS = 128
TOPK = 16
PEER_GROUPS = 16
D_FF = 2816
FT = D_FF // P
ODD_HEADS = 16
WINDOWS = (2, 4, 8, 16)
PAD = 16
RING = 4
EPS = 1e-6
NEG = -3.0e38
SCALE = DH ** -0.5

STREAM = [
    ("w_in", 44), ("branch", 8), ("w_out", 8), ("wquery", 16), ("peer", 2 * NKEYS),
    ("ffn0", 3 * FT), ("even_in", 16), ("even_out", 8), ("ffn1", 3 * FT),
    ("ffn2", 3 * FT), ("qkv", 24), ("w_o", 8), ("ffn3", 3 * FT),
]

GAINS = ["norm_mix_g", "norm_ffn_g", "norm_final_g", "norm_ffn1_0", "norm_mix_0", "norm_ffn2_0",
         "norm_ffn1_1", "norm_mix_1", "norm_ffn2_1", "norm_final"]
COL = {name: KT * i for i, name in enumerate(GAINS)}
COL["lb0"] = KT * len(GAINS)
COL["lb1"] = COL["lb0"] + 4
COL["out_g"] = COL["lb1"] + 4
COL["conv"] = COL["out_g"] + 4
COL["pool_scale"] = COL["conv"] + 12
COL["eps"] = COL["pool_scale"] + 4
COL["eps2"] = COL["eps"] + 1
N_COLS = COL["eps2"] + 1

LEVELS = [64, 32, 16, 8, 4, 2, 1]


def mixer_constants():
    i = np.arange(P)
    s, t = i[:, None], i[None, :]
    head_ones = (s // DH == t // DH).astype(np.float32)
    masks = []
    for m in LEVELS:
        masks.append((s // (2 * m) == t // (2 * m)) & (s % (2 * m) < m) & (t % (2 * m) >= m))
    chunk = np.broadcast_to((np.arange(T) % CHUNK != 0).astype(np.float32), (P, T))
    return np.concatenate([np.eye(P, dtype=np.float32), head_ones]
                          + [m.astype(np.float32) for m in masks] + [chunk], 1)


def attention_constants():
    i = np.arange(P)
    s, t = i[:, None], i[None, :]
    later = (s > t).astype(np.float32)
    past = (s < t).astype(np.float32)
    past_neg = np.concatenate([-past, -np.ones((P, P), np.float32), -past], 1)
    dist0 = np.where(t <= s, t - s, -1.0e30)
    dist1 = np.concatenate([np.broadcast_to(t - s - P, (P, P)), dist0], 1)
    dist = np.concatenate([dist0, dist1], 1).astype(np.float32)
    inv = [1.0 / np.minimum(np.arange(T) + 1, w) for w in WINDOWS]
    inv = np.broadcast_to(np.concatenate(inv).astype(np.float32), (P, 4 * T))
    return np.concatenate([np.eye(P, dtype=np.float32), later, past_neg, dist, inv], 1)


FIRST_LEVEL = 15
STICK_AFTER = {9: (0, 1), 11: (2, 3), 12: (4,), 13: (5,), 14: (6,), 15: (7,)}

ODD_AFTER = {17: 0, 19: 1, 21: 2}

N_MIXC = P * (2 + len(LEVELS)) + T
N_ATTC = P * 2 + 3 * P + 3 * P + 4 * T

BASE = 16512
RAW, W_HI, W_LO = 0, RING * D, 2 * RING * D
H_HI = 3 * RING * D
H_LO = H_HI + KT * T
MID = H_LO + KT * T
COLS = MID + 5 * 2 * T
ONES = COLS + P
RSTD = ONES + 2 * P
R_COL = RSTD + T
ARENA = R_COL + 8
X_AT = ARENA + P * T - KT * T
GATES = ARENA + P * T
PRODUCTS = GATES + T
assert BASE + 4 * (PRODUCTS + 2 * KT) <= 229344


N_NORMS = 10


def stream_plan():
    first, at = {}, 0
    for name, n in STREAM:
        first[name] = at
        at += n
    return first, at


def tile_readers():
    order = []
    order += ["act"] * 20 + ["dve"] * 8 + ["act"] * 16
    order += ["dve"] * 8 + ["dve"] * 8
    order += ["act"] * 16
    order += ["dve"] * 8 + ["act"] * 4 + ["dve"] * 4 + ["dve"] * 4 + ["dve"] * 8
    order += ["dve"] * 16 + ["act"] * 8 + ["dve"] * 8
    return order


def build(nc, stream, x_in, cols_in, ones_in, keys_in, wpool_in, mixc_in, attc_in, out):
    first, NSLAB = stream_plan()
    readers = tile_readers()
    tile_at = {}
    at = 0
    for name, n in (("w_in", 44), ("branch", 8), ("w_out", 8), ("wquery", 16), ("even_in", 16),
                    ("pooled", 4), ("even_out", 8), ("qkv", 24), ("w_o", 8)):
        tile_at[name] = at
        at += n

    def slab_of(name, i):
        return first[name] + i

    def tile_buf(j, half=0):
        return tile[:, 2 * (j % 2) + half, :]

    def pair_buf(c, tt):
        return tile[:, 2 * (c // 2 % 2) + tt, :]

    def reads(engine, j):
        return sum(r == engine for r in readers[:j + 1])

    with ExitStack() as ctx:
        def sb(name, at, shape, dt=F32):
            return nc.alloc_sbuf_tensor_at(name, [P] + shape, dt, offset=BASE + 4 * at)

        def sem(name):
            return ctx.enter_context(nc.semaphore(name))

        raw = sb("raw", RAW, [RING, D])
        w_hi = sb("w_hi", W_HI, [RING, D], F32R)
        w_lo = sb("w_lo", W_LO, [RING, D], F32R)
        h_hi = sb("h_hi", H_HI, [KT, T], F32R)
        h_lo = sb("h_lo", H_LO, [KT, T], F32R)
        scaled = sb("scaled", MID, [2, 2 * T])
        hid = sb("hid", MID + 4 * T, [2, T])
        mid_hi = sb("mid_hi", MID + 6 * T, [2, T], F32R)
        mid_lo = sb("mid_lo", MID + 8 * T, [2, T], F32R)
        cols = sb("cols", COLS, [N_COLS])
        lane = sb("lane", ONES, [2, P])
        ones, iota = lane[:, 0, :], lane[:, 1, :]
        rstd = sb("rstd", RSTD, [T])
        r_col = sb("r_col", R_COL, [TT])
        pick1 = sb("pick1", MID, [4, 2, P])
        pick2 = sb("pick2", MID + 8 * P, [2, 4, P])
        idx1_T = sb("idx1_T", MID + 16 * P, [T])
        idx2_T = sb("idx2_T", MID + 16 * P + T, [T])
        gate_T = sb("gate_T", GATES, [T])
        G = sb("G", ARENA, [T, P])
        x = sb("x", X_AT, [KT, T])
        gain_product = sb("gain_product", PRODUCTS, [KT])
        gain_square = sb("gain_square", PRODUCTS + KT, [KT])
        h32 = sb("h32", ARENA + 2560, [KT, T])
        sq = sb("sq", ARENA + 4608, [KT, T])

        A = ARENA + 6656
        square_weights = sb("square_weights", A, [KT, P])
        sq_half = sb("sq_half", A + KT * P, [4, T])
        rstd_x = sb("rstd_x", A + KT * P + 4 * T, [T])
        mixc = sb("mixc", ARENA, [N_MIXC])
        ident = mixc[:, 0:P]
        head_ones = mixc[:, P:2 * P]
        level_mask = {m: mixc[:, (2 + i) * P:(3 + i) * P] for i, m in enumerate(LEVELS)}
        chunk_mask = mixc[:, N_MIXC - T:N_MIXC]
        kk = sb("kk", A, [4, T])
        qq = sb("qq", A + 1024, [4, T])
        hgs = sb("hgs", A + 2048, [4, T])
        bb = sb("bb", A + 3072, [4, T])
        lf = sb("lf", A + 4096, [4, T])
        vv = sb("vv", A + 5120, [TT, 512])
        cc = sb("cc", A + 6144, [4, T])
        uu = sb("uu", A + 7168, [4, T + 2])
        conv = sb("conv", A + 8208, [4, T])
        sg = sb("sg", A + 9232, [16, T])
        y_hi = sb("y_hi", A + 13376, [KT, T], F32R)
        y_lo = sb("y_lo", A + 15424, [KT, T], F32R)
        y32 = sb("y32", A + 17472, [KT, T])
        S = sb("S", A + 19520, [4, 4, P])
        S_off = sb("S_off", A + 21568, [2, 4, P])
        lbw = sb("lbw", A + 22592, [8, 4])
        dec = sb("dec", A + 22624, [4, 4])
        assert A + 22640 <= X_AT
        X = sb("X", ARENA + 2560, [2, 4, T])
        osq = sb("osq", ARENA + 4608, [4, T])
        orr = sb("orr", ARENA + 5632, [4, T])
        keysT = sb("keysT", A, [PEER_GROUPS, NKEYS])
        qT = sb("qT", A + 2048, [PEER_GROUPS, T])
        top_v = sb("top_v", A + 6144, [TT, PEER_GROUPS, TOPK])
        top_i = sb("top_i", A + 6656, [TT, PEER_GROUPS, TOPK], U32)
        top_f = sb("top_f", A + 7168, [TT, PEER_GROUPS, TOPK])
        rest = sb("rest", A + 12704, [TT, NKEYS])
        cand = sb("cand", A + 7808, [2, TOPK, TOPK])
        best = sb("best", A + 8320, [TT, HEADS, TOPK])
        pos = sb("pos", A + 8576, [TT, HEADS, TOPK], U32)
        pos1 = sb("pos1", A + 8832, [TT, HEADS, TOPK], U32)
        pos2 = sb("pos2", A + 9088, [TT, HEADS, TOPK], U32)
        posf = sb("posf", A + 9344, [2, TT, HEADS, TOPK])
        onehot = sb("onehot", A + 9856, [HEADS, TOPK, TOPK])
        idx = sb("idx", A + 11904, [2, TT, HEADS, TOPK])
        gts = sb("gts", A + 12416, [TT, HEADS, TOPK])
        gsum = sb("gsum", A + 12672, [TT, HEADS, 2])
        attc = sb("attc", ARENA, [N_ATTC])
        ident2 = attc[:, 0:P]
        later = attc[:, P:2 * P]
        past_neg = attc[:, 2 * P:5 * P]
        dist = attc[:, 5 * P:8 * P]
        inv_count = attc[:, 8 * P:8 * P + 4 * T].rearrange("p (g t) -> p g t", g=4)
        wpool = sb("wpool", ARENA + N_ATTC, [4, P])
        assert N_ATTC + 4 * P <= 2560
        aq = sb("aq", A, [4, T])
        ak = sb("ak", A + 1024, [4, T])
        av = sb("av", A + 2048, [TT, 512])
        pu = sb("pu", A + 3072, [4, PAD + T])
        az = sb("az", A + 4160, [HEADS, 3 * P])
        asp = sb("asp", A + 7232, [HEADS, 3 * P])
        aL = sb("aL", A + 10304, [HEADS, 3 * P])
        win = sb("win", ARENA + 2560, [2, PAD + T])
        pooled = sb("pooled", ARENA + 4608, [4, T])
        bq = sb("bq", A, [KT, T])
        bk = sb("bk", A + 2048, [KT, T])
        bv = sb("bv", A + 4096, [TT, D])
        sc = sb("sc", A + 6144, [4, 3 * P])
        pT = sb("pT", A + 7680, [2, 3 * P])
        st = sb("st", A + 8448, [3, 4, 2])

        acc = ctx.enter_context(nc.psum_tensor("acc", [P, KT, T], F32))
        front = ctx.enter_context(nc.psum_tensor("front", [P, 2, 2 * T], F32))
        tile = ctx.enter_context(nc.psum_tensor("tile", [P, 4, T], F32))
        banks = acc[:, :, :].rearrange("p (b a) t -> p b (a t)", b=4)
        fronts = front[:, :, :]

        landed = [sem(f"slab_landed{i}") for i in range(RING)]
        hi_ready = sem("slab_hi_ready")
        lo_ready = sem("slab_lo_ready")
        slab_used = sem("slab_used")
        pool_done = sem("pool_products_done")
        tile_read = {"act": sem("tile_read_by_act"), "dve": sem("tile_read_by_dve")}
        x_landed = [sem(f"x_half{i}_landed") for i in range(2)]
        small_in = sem("vectors_landed")
        mixc_landed = sem("mixer_constants_landed")
        keys_in_sem = sem("keys_landed")
        attc_sem = sem("attention_constants_landed")
        dve_own = sem("dve_own_steps")
        act_own = sem("act_own_steps")
        x_ready = sem("x_pairs_ready")
        result_ready = sem("result_ready")
        squares = sem("norm_squares_of_first_tiles")
        weights_ready = sem("square_weights_ready")
        x_scaled = sem("x_times_rstd")
        squares_last = sem("norm_squares_of_last_tiles")
        bank_done = sem("output_bank_done")
        sums = sem("norm_sums")
        sq_summed = sem("norm_squares_added")
        roots = sem("norm_roots")
        rstd_ready = sem("rstd_ready")
        r_turned = sem("rstd_turned")
        r_col_ready = sem("rstd_columns_ready")
        scaled_ready = sem("front_scaled")
        h32_ready = sem("norm_h32")
        nh_hi = sem("norm_h_hi")
        nh_lo = sem("norm_h_lo")
        gate_ready = sem("gate_ready")
        hid_ready = sem("hid_ready")
        mid_hi_ready = sem("mid_hi_ready")
        mid_lo_ready = sem("mid_lo_ready")
        out_done = sem("out_done")
        forget_ready = sem("forget_ready")
        logf_ready = sem("logf_ready")
        lb_diff = sem("lb_diff")
        lb_exp = sem("lb_exp")
        level_diff = sem("level_diff")
        level_exp = sem("level_exp")
        level_ready = sem("level_operands_ready")
        level_done = sem("level_scores_done")
        level_read = sem("level_scores_read")
        o_done = sem("hgrn_o_done")
        o_sq = sem("hgrn_o_squares")
        o_sum = sem("hgrn_o_sums")
        o_root = sem("hgrn_o_roots")
        y32_ready = sem("y32_ready")
        y_hi_ready = sem("y_hi_ready")
        y_lo_ready = sem("y_lo_ready")
        merged_ready = sem("merged_ready")
        merged_hi = sem("merged_hi")
        merged_lo = sem("merged_lo")
        keys_done = sem("key_scores_done")
        keys_read = sem("key_scores_read")
        gate_diff = sem("gate_diff")
        gate_exp = sem("gate_exp")
        picks_ready = sem("picks_ready")
        picks_turned = sem("picks_turned")
        picks_copied = sem("picks_copied")
        pick1_there = sem("pick_rows_of_first_keys_there")
        pick1_ready = sem("pick_rows_with_gates_ready")
        pick2_ready = sem("pick_rows_of_second_keys_ready")
        pick_used = sem("pick_rows_used")
        g_copied = sem("G_copied")
        x_seeded = sem("x_seeded")
        z_done = sem("stick_z_done")
        z_read = sem("stick_z_read")
        ln_ready = sem("stick_ln_ready")
        stick_L = sem("stick_L_ready")
        later_done = sem("stick_later_done")
        stick_w = sem("stick_w_ready")
        stick_e = sem("stick_exp_ready")
        stick_a = sem("stick_a_ready")
        ao_done = sem("stick_o_done")
        pooled_ready = sem("pooled_ready")
        sc_done = sem("odd_scores_done")
        sc_read = sem("odd_scores_read")
        p_exp = sem("odd_exp_ready")
        p_norm = sem("odd_p_ready")
        p_turned = sem("odd_p_turned")
        p_copied = sem("odd_p_copied")
        bo_done = sem("odd_o_done")

        block = ctx.enter_context(nc.Block())

        def layer_stages():
            yield from (("ffn", 0), ("even", 0), ("ffn", 1), ("ffn", 2), ("odd", 0), ("ffn", 3))

        FFN_GAIN = ["norm_ffn1_0", "norm_ffn2_0", "norm_ffn1_1", "norm_ffn2_1"]

        def stage_gain(kind, i):
            return FFN_GAIN[i] if kind == "ffn" else {"even": "norm_mix_0", "odd": "norm_mix_1"}[kind]

        sources = [None, "w_out", 0]
        x_pairs = 4
        for kind, i in layer_stages():
            if (kind, i) == ("ffn", 0):
                sources.append(0)
                x_pairs += 4
                continue
            sources.append({"ffn": x_pairs, "even": x_pairs, "odd": x_pairs}[kind]
                           if (kind, i) not in (("ffn", 1), ("ffn", 3))
                           else {1: "even_out", 3: "w_o"}[i])
            if kind == "ffn":
                x_pairs += 4
        sources.append(x_pairs)

        def wait_x(eng, q, k):
            src = sources[q]
            if isinstance(src, str):
                eng.wait_ge(tile_read["dve"], reads("dve", tile_at[src] + k))
            else:
                eng.wait_ge(x_ready, src + k // 2 + 1)

        SUM_AT = {"mlp": tile[:, 0, :], "project": front[:, 0, 0:T]}
        sum_at = [SUM_AT["project"]] * 2 + [SUM_AT["mlp"]]
        for kind, i in layer_stages():
            if (kind, i) == ("ffn", 0):
                sum_at.append(tile[:, 2, :])
                continue
            sum_at.append(SUM_AT["mlp" if kind == "ffn" else "project"])
        sum_at.append(SUM_AT["mlp"])

        def squaring(q):
            return q if q < 3 else q - 1

        @block.sync
        def _(sp):
            for half in range(2):
                a, b = half * KT // 2, (half + 1) * KT // 2
                sp.dma_start(x[:, a:b, :], x_in[:, a:b, :]).then_inc(x_landed[half], 16)
            sp.dma_start(cols[:, :], cols_in).then_inc(small_in, 16)
            sp.dma_start(lane[:, :, :], ones_in).then_inc(small_in, 16)
            for s in range(RING):
                sp.dma_start(raw[:, s, :], stream[s, :, :]).then_inc(landed[s], 16)
            sp.dma_start(mixc[:, :], mixc_in).then_inc(mixc_landed, 16)
            with sp.Fori(1, NSLAB // RING) as turn:
                for s in range(RING):
                    sp.wait_ge(lo_ready, turn * RING + (s + 1 - RING))
                    sp.dma_start(raw[:, s, :], stream[bass.ds(turn * RING + s, 1), :, :]
                                 .rearrange("a p n -> (a p) n")).then_inc(landed[s], 16)
            for n in range(NSLAB // RING * RING, NSLAB):
                sp.wait_ge(lo_ready, n + 1 - RING)
                sp.dma_start(raw[:, n % RING, :], stream[n, :, :]).then_inc(landed[n % RING], 16)
            for k in range(0, KT, 2):
                sp.wait_ge(result_ready, k // 2 + 1)
                sp.dma_start(out[:, k:k + 2, :],
                             h32[:, k:k + 2, :]).then_inc(out_done, 16)
            sp.wait_ge(out_done, 16 * (KT // 2))

        @block.gpsimd
        def _(pool):
            def pick_gates(t, k):
                nc.gpsimd.tensor_tensor(pick1[:, k, :, :], pick1[:, k, :, :],
                                        gate_T[:, t].unsqueeze(2).broadcast_to([P, 2, P]),
                                        ALU.mult).then_inc(pick1_ready, 2)

            for q in range(1, N_NORMS):
                if q == 2:
                    for n in range(first["wquery"] + RING, first["peer"] + RING):
                        pool.wait_ge(lo_ready, n)
                        pool.wait_ge(hi_ready, n + 1)
                        nc.gpsimd.tensor_tensor(w_lo[:, n % RING, :], raw[:, n % RING, :],
                                                w_hi[:, n % RING, :].bitcast(F32),
                                                ALU.subtract).then_inc(lo_ready, 1)
                    pool.wait_ge(picks_copied, 3)
                    for k in range(4):
                        pool.wait_ge(pick1_there, 2 * k + 2)
                        pick_gates(slice(2 * k, 2 * k + 2), k)
                    with pool.Fori(0, (T - 8) // 8) as turn:
                        for k in range(4):
                            pool.wait_ge(pick1_there, turn * 8 + (10 + 2 * k))
                            pick_gates(bass.ds(turn * 8 + (8 + 2 * k), 2), k)
                    pool.wait_ge(hid_ready, NKEYS)
                    nc.gpsimd.tensor_tensor(square_weights[:, :, :],
                                            ones.unsqueeze(1).broadcast_to([P, KT, P]),
                                            gain_square[:, :].unsqueeze(2).broadcast_to([P, KT, P]),
                                            ALU.mult).then_inc(weights_ready, 1)
                if q == 3:
                    pool.wait_ge(nh_lo, 24)
                    pool.wait_ge(rstd_ready, 4)
                    pool.wait_ge(squares_last, 2)
                    for k in range(0, KT, 4):
                        g = cols[:, COL["norm_final_g"] + k:COL["norm_final_g"] + k + 4]
                        nc.gpsimd.tensor_tensor(x[:, k:k + 4, :], x[:, k:k + 4, :],
                                                rstd_x[:, :].unsqueeze(1).broadcast_to([P, 4, T]),
                                                ALU.mult).then_inc(x_scaled, 1)
                        pool.wait_ge(x_scaled, k // 4 + 1)
                        nc.gpsimd.tensor_tensor(x[:, k:k + 4, :], x[:, k:k + 4, :],
                                                g.unsqueeze(2).broadcast_to([P, 4, T]),
                                                ALU.mult).then_inc(x_ready, 2)
                    continue
                for k in range(0, KT // 2, 2):
                    wait_x(pool, q, k + 1)
                    if k == 0:
                        pool.wait_ge(sums, q)
                    nc.gpsimd.tensor_tensor(sq[:, k:k + 2, :], x[:, k:k + 2, :], x[:, k:k + 2, :], ALU.mult)\
                        .then_inc(squares, 1)

        @block.scalar
        def _(act):
            own = [0]

            def link(ins):
                ins.then_inc(act_own, 1)
                own[0] += 1
                act.wait_ge(act_own, own[0])

            def split_hi(n, turn=None, per=0):
                if turn is None and n >= NSLAB:
                    return
                s = n % RING
                loads = n // RING + 1
                if turn is None:
                    act.wait_ge(landed[s], 16 * loads)
                    if n >= RING:
                        act.wait_ge(slab_used, n + 1 - RING)
                else:
                    act.wait_ge(landed[s], turn * (16 * per // RING) + 16 * loads)
                    act.wait_ge(slab_used, turn * per + (n + 1 - RING))
                nc.scalar.copy(w_hi[:, s, :], raw[:, s, :]).then_inc(hi_ready, 1)

            def root(q):
                act.wait_ge(sums, q + 1)
                eps = COL["eps2" if q == 2 else "eps"]
                nc.scalar.activation((rstd_x if q == 3 else rstd)[:, :], sum_at[q], ACT.Sqrt, scale=1.0 / D,
                                     bias=cols[:, eps:eps + 1]).then_inc(roots, 1)

            def square_last(q):
                wait_x(act, q, KT - 1)
                act.wait_ge(sums, q)
                nc.scalar.activation(sq[:, KT // 2:, :], x[:, KT // 2:, :], ACT.Square)\
                    .then_inc(squares_last, 1)

            def operand_hi(q, gain, ks=range(KT)):
                for k in ks:
                    wait_x(act, q, k)
                    scale = (gain_product[:, k:k + 1] if gain is None
                             else cols[:, COL[gain] + k:COL[gain] + k + 1])
                    nc.scalar.activation(h_hi[:, k, :], x[:, k, :], ACT.Copy, scale=scale).then_inc(nh_hi, 1)

            def take(name, i, out, func=ACT.Copy, scale=1.0):
                j = tile_at[name] + i
                act.wait_ge(slab_used, slab_of(name, i) + 1)
                nc.scalar.activation(out, tile_buf(j), func, scale=scale).then_inc(tile_read["act"], 1)

            def take_v(name, i, c, v, scaled_=True):
                act.wait_ge(slab_used, slab_of(name, i) + 2)
                for tt in range(TT):
                    ins = nc.scalar.activation(v[:, tt, c * P:(c + 2) * P], pair_buf(c, tt), ACT.Copy,
                                               scale=r_col[:, tt:tt + 1] if scaled_ else 1.0)
                ins.then_inc(tile_read["act"], 2)

            def mlp(func, n0, steps, fronts_, done, after_first=None):
                per_step = fronts_ + 1

                def step(s, n, turn=None, turns=0):
                    S0 = done + s
                    k = s % 2
                    spt, slt = turns, turns * per_step

                    if fronts_ == 2:
                        split_hi(n + RING, turn, slt)
                    act.wait_ge(scaled_ready, S0 + 1 if turn is None else turn * spt + (S0 + 1))
                    nc.scalar.activation(scaled[:, k, 0:T], scaled[:, k, 0:T], func).then_inc(gate_ready, 1)
                    split_hi(n + fronts_ - 1 + RING, turn, slt)
                    act.wait_ge(hid_ready, S0 + 1 if turn is None else turn * spt + (S0 + 1))
                    nc.scalar.copy(mid_hi[:, k, :], hid[:, k, :]).then_inc(mid_hi_ready, 1)

                step(0, n0)
                if after_first:
                    after_first()
                n = n0 + fronts_
                turns = 4 if fronts_ == 2 else 2
                loops = (steps - 1) // turns
                with act.Fori(0, loops) as turn:
                    for c in range(turns):
                        step(1 + c, n + c * per_step, turn, turns)
                        split_hi(n + c * per_step + fronts_ + RING, turn, turns * per_step)
                for s in range(1 + loops * turns, steps):
                    m = n + (s - 1) * per_step
                    step(s, m)
                    split_hi(m + fronts_ + RING)

            act.wait_ge(small_in, 32)
            for half in range(2):
                act.wait_ge(x_landed[half], 16)
                a, b = half * KT // 2, (half + 1) * KT // 2
                nc.scalar.activation(sq[:, a:b, :], x[:, a:b, :], ACT.Square).then_inc(squares, 1)
            split_hi(0)
            split_hi(1)
            root(0)
            for k in range(0, KT, 2):
                act.wait_ge(h32_ready, k // 2 + 1)
                nc.scalar.copy(h_hi[:, k:k + 2, :], h32[:, k:k + 2, :]).then_inc(nh_hi, 2)
            split_hi(2)
            split_hi(3)

            act.wait_ge(lb_diff, 1)
            nc.scalar.activation(lbw[:, 3:5, :], lbw[:, 1:3, :], ACT.Exp).then_inc(lb_exp, 1)
            n = first["w_in"]
            for i in range(44):
                if i < 4:
                    take("w_in", i, kk[:, i, :], ACT.Sigmoid)
                elif i < 8:
                    take("w_in", i, qq[:, i - 4, :], ACT.Silu)
                elif i < 12:
                    if i % 2:
                        take_v("w_in", i - 1, i - 9, vv, False)
                elif i < 16:
                    take("w_in", i, hgs[:, i - 12, :], ACT.Silu)
                elif i < 20:
                    take("w_in", i, cc[:, i - 16, :])
                elif i >= 28:
                    take("w_in", i, sg[:, i - 28, :], ACT.Sigmoid)
                else:
                    act.wait_ge(slab_used, n + i + 1)
                split_hi(n + i + RING)
                if i == 12:
                    act.wait_ge(forget_ready, 1)
                    nc.scalar.activation(lf[:, :, :], lf[:, :, :], ACT.Ln).then_inc(logf_ready, 1)
                l = (i - FIRST_LEVEL + 1) // 2
                if i >= FIRST_LEVEL - 1 and (i - FIRST_LEVEL) % 2 == 1 and l < 8:
                    act.wait_ge(level_diff, l + 1)
                    nc.scalar.activation(X[:, l % 2, :, :], X[:, l % 2, :, :], ACT.Exp).then_inc(level_exp, 1)
                if i == FIRST_LEVEL + 18:
                    act.wait_ge(tile_read["dve"], reads("dve", tile_at["w_in"] + 27))
                    nc.scalar.copy(y_hi[:, 4:8, :], y32[:, 4:8, :]).then_inc(y_hi_ready, 1)
                if i == FIRST_LEVEL + 20:
                    act.wait_ge(o_done, 1)
                    nc.scalar.activation(osq[:, :, :], fronts.rearrange("p b (a t) -> p (b a) t", a=2),
                                         ACT.Square).then_inc(o_sq, 1)
                if i == FIRST_LEVEL + 22:
                    act.wait_ge(o_sum, 1)
                    nc.scalar.activation(orr[:, :, :], acc[:, 0:4, :], ACT.Sqrt, scale=1.0 / DH,
                                         bias=cols[:, COL["eps"]:COL["eps"] + 1]).then_inc(o_root, 1)
                if i == FIRST_LEVEL + 25:
                    act.wait_ge(y32_ready, 1)
                    nc.scalar.copy(y_hi[:, 0:4, :], y32[:, 0:4, :]).then_inc(y_hi_ready, 1)
            n = first["branch"]
            for m in range(8):
                act.wait_ge(slab_used, n + m + 1)
                split_hi(n + m + RING)
                act.wait_ge(merged_ready, m + 1)
                nc.scalar.copy(h_hi[:, m, :], h32[:, m, :]).then_inc(merged_hi, 1)
            n = first["w_out"]
            for m in range(8):
                act.wait_ge(slab_used, n + m + 1)
                if m < 7:
                    split_hi(n + m + RING)
            late = n + 7 + RING
            nc.scalar.dma_start(keysT[:, :, :], keys_in).then_inc(keys_in_sem, 16)
            operand_hi(1, "norm_ffn_g")
            square_last(1)
            split_hi(late)
            root(1)
            n = first["wquery"]
            for i in range(16):
                take("wquery", i, qT[:, i, :])
                split_hi(n + i + RING)
            act.wait_ge(gate_diff, 1)
            nc.scalar.activation(gts[:, :, :, :], gts[:, :, :, :], ACT.Exp).then_inc(gate_exp, 1)
            act.wait_ge(picks_turned, 1)
            for i, to in enumerate((idx1_T, idx2_T, gate_T)):
                nc.scalar.copy(to[:, :], tile[:, i, :]).then_inc(picks_copied, 1)
            act.wait_ge(x_seeded, 1)
            with act.Fori(0, T // 16) as turn:
                for b in range(4):
                    act.wait_ge(pick_used, turn * 16 + 4 * b + 4)
                    src = (fronts[:, b, :] if b < 2
                           else tile[:, 2 * b - 4:2 * b - 2, :].rearrange("p a t -> p (a t)"))
                    nc.scalar.copy(G[:, bass.ds(turn * 16 + 4 * b, 4), :],
                                   src.rearrange("p (t j) -> p t j", t=4)).then_inc(g_copied, 1)
            act.wait_ge(pick_used, T)
            mlp(ACT.Gelu, first["peer"], NKEYS, 1, 0)
            late = first["peer"] + 2 * NKEYS - 1 + RING
            q = 3
            done = NKEYS
            for kind, i in layer_stages():
                if q == 3:
                    operand_hi(2, None)
                    square_last(2)
                    split_hi(late)
                    root(2)
                    nc.scalar.dma_start(attc[:, :], attc_in).then_inc(attc_sem, 16)
                    nc.scalar.dma_start(wpool[:, :, :], wpool_in).then_inc(attc_sem, 16)
                else:
                    if not isinstance(sources[q], str):
                        operand_hi(q, stage_gain(kind, i))
                    square_last(q)
                    split_hi(late)
                    root(q)
                q += 1
                if kind == "ffn":
                    mlp(ACT.Silu, first[f"ffn{i}"], FT, 2, done, (lambda: root(3)) if i == 0 else None)
                    done += FT
                    late = first[f"ffn{i}"] + 3 * FT - 1 + RING
                elif kind == "even":
                    def ln_one_plus(g, steps):
                        of = slice(4 * g, 4 * g + 4)
                        for step in steps:
                            if step == 0:
                                act.wait_ge(z_read, 4 * g + 4)
                                link(nc.scalar.activation(asp[:, of, :], az[:, of, :], ACT.Abs))
                            elif step == 1:
                                link(nc.scalar.activation(asp[:, of, :], asp[:, of, :], ACT.Exp, scale=-1.0))
                            else:
                                nc.scalar.activation(asp[:, of, :], asp[:, of, :], ACT.Ln, bias=1.0)\
                                    .then_inc(ln_ready, 1)

                    n = first["even_in"]
                    for i in range(16):
                        act.wait_ge(slab_used, n + i + 1)
                        split_hi(n + i + RING)
                        if i in (9, 11):
                            if i == 9:
                                act.wait_ge(r_col_ready, 2)
                            take_v("even_in", i - 1, i - 9, av)
                        for h in STICK_AFTER.get(i, ()):
                            act.wait_ge(z_done, h + 1)
                            nc.scalar.activation(az[:, h, :], banks[:, h % 4, 0:3 * P], ACT.Copy,
                                                 scale=SCALE).then_inc(z_read, 1)
                        if i >= 12 and i < 15:
                            ln_one_plus(0, [i - 12])
                    ln_one_plus(1, range(3))
                    for g in range(2):
                        a, b = 4 * g, 4 * g + 4
                        act.wait_ge(stick_w, b)
                        nc.scalar.activation(az[:, a:b, :], az[:, a:b, :], ACT.Exp).then_inc(stick_e, 1)
                    act.wait_ge(tile_read["dve"], reads("dve", tile_at["pooled"] + 3))
                    nc.scalar.copy(y_hi[:, 4:8, :], y32[:, 4:8, :]).then_inc(y_hi_ready, 1)
                    act.wait_ge(ao_done, 1)
                    nc.scalar.copy(y_hi[:, 0:4, :], fronts.rearrange("p b (a t) -> p (b a) t", a=2))\
                        .then_inc(y_hi_ready, 1)
                    n = first["even_out"]
                    for m in range(8):
                        act.wait_ge(slab_used, n + m + 1)
                        operand_hi(q, FFN_GAIN[1], [m])
                        if m < 7:
                            split_hi(n + m + RING)
                    late = n + 7 + RING
                else:
                    def take_heads(part):
                        act.wait_ge(bo_done, 4 * part + 4)
                        a = 2 * (part % 2)
                        nc.scalar.copy(y_hi[:, 2 * part:2 * part + 2, :], tile[:, a:a + 2, :])\
                            .then_inc(y_hi_ready, 1)

                    def head_step(h):
                        if h < ODD_HEADS:
                            k = h % 4
                            act.wait_ge(sc_read, h + 1)
                            nc.scalar.activation(sc[:, k, 0:P], sc[:, k, 0:P], ACT.Exp,
                                                 bias=st[:, 0, k, 0:1], accum_out=st[:, 1, k, 0:1])\
                                .then_inc(p_exp, 1)
                            nc.scalar.activation(sc[:, k, P:3 * P], sc[:, k, P:3 * P], ACT.Exp,
                                                 bias=st[:, 0, k, 1:2], accum_out=st[:, 1, k, 1:2])\
                                .then_inc(p_exp, 1)
                        if h >= 2:
                            g = h - 2
                            act.wait_ge(p_turned, g + 1)
                            if g >= 2:
                                act.wait_ge(bo_done, g - 1)
                            nc.scalar.copy(pT[:, g % 2, :], fronts[:, g % 2, 0:3 * P])\
                                .then_inc(p_copied, 1)
                        if h in (8, 12, 16):
                            take_heads((h - 8) // 4)

                    n = first["qkv"]
                    for i in range(24):
                        act.wait_ge(slab_used, n + i + 1)
                        split_hi(n + i + RING)
                        if i >= 16 and i % 2:
                            if i == 17:
                                act.wait_ge(r_col_ready, 3)
                            take_v("qkv", i - 1, i - 17, bv)
                        if i in ODD_AFTER:
                            head_step(ODD_AFTER[i])
                    for h in range(len(ODD_AFTER), ODD_HEADS + 2):
                        head_step(h)
                    take_heads(3)
                    n = first["w_o"]
                    for m in range(8):
                        act.wait_ge(slab_used, n + m + 1)
                        operand_hi(q, FFN_GAIN[3], [m])
                        if m < 7:
                            split_hi(n + m + RING)
                    late = n + 7 + RING
            square_last(q)
            root(q)

        @block.vector
        def _(dve):
            own = [0]

            def link(ins):
                ins.then_inc(dve_own, 1)
                own[0] += 1
                dve.wait_ge(dve_own, own[0])

            def split_lo(n, turn=None, per=0):
                if turn is None and n >= NSLAB:
                    return
                s = n % RING
                dve.wait_ge(hi_ready, n + 1 if turn is None else turn * per + (n + 1))
                nc.vector.tensor_tensor(w_lo[:, s, :], raw[:, s, :], w_hi[:, s, :].bitcast(F32),
                                        ALU.subtract).then_inc(lo_ready, 1)

            def col(name, i=0):
                return cols[:, COL[name] + i:COL[name] + i + 1]

            def add_squares(q):
                to = sq_half if q == 3 else sq
                dve.wait_ge(squares, 2 + 2 * squaring(q))
                dve.wait_ge(squares_last, squaring(q))
                link(nc.vector.tensor_tensor(to[:, 0:4, :], sq[:, 0:4, :], sq[:, 4:8, :], ALU.add))
                link(nc.vector.tensor_tensor(to[:, 0:2, :], to[:, 0:2, :], to[:, 2:4, :], ALU.add))
                nc.vector.tensor_tensor(to[:, 0, :], to[:, 0, :], to[:, 1, :], ALU.add)\
                    .then_inc(sq_summed, 1)

            def inverse_rms(q, late=None):
                if q not in (0, 2, 3):
                    add_squares(q)
                if late is not None:
                    split_lo(late)
                dve.wait_ge(roots, q + 1)
                to = rstd_x if q == 3 else rstd
                nc.vector.reciprocal(to[:, :], to[:, :]).then_inc(rstd_ready, 1)
                dve.wait_ge(rstd_ready, q + 1)

            def operand_lo(i, gain, ks=range(KT)):
                for k in ks:
                    dve.wait_ge(nh_hi, 8 * i + k + 1)
                    scale = gain_product[:, k:k + 1] if gain is None else col(gain, k)
                    nc.vector.scalar_tensor_tensor(h_lo[:, k, :], x[:, k, :], scale,
                                                   h_hi[:, k, :].bitcast(F32), ALU.mult, ALU.subtract)\
                        .then_inc(nh_lo, 1)

            def r_columns(count):
                dve.wait_ge(r_turned, count)
                nc.vector.tensor_copy(r_col[:, :], front[:, 1, 0:T:P]).then_inc(r_col_ready, 1)

            def scale_x(gain, to, after, ks=range(KT)):
                for k in ks:
                    ins = nc.vector.scalar_tensor_tensor(to[:, k, :], x[:, k, :], col(gain, k), rstd[:, :],
                                                         ALU.mult, ALU.mult)
                    if k % 2 == 1:
                        ins.then_inc(after, 1)

            def take(name, i, out, scale=None):
                j = tile_at[name] + i
                dve.wait_ge(slab_used, slab_of(name, i) + 1)
                if scale is None:
                    ins = nc.vector.tensor_tensor(out, tile_buf(j), rstd[:, :], ALU.mult)
                else:
                    ins = nc.vector.scalar_tensor_tensor(out, tile_buf(j), scale, rstd[:, :], ALU.mult,
                                                         ALU.mult)
                ins.then_inc(tile_read["dve"], 1)

            def y_low(count, a, b, y=None):
                dve.wait_ge(y_hi_ready, count)
                nc.vector.tensor_tensor(y_lo[:, a:b, :], y32[:, a:b, :] if y is None else y, y_hi[:, a:b, :].bitcast(F32),
                                        ALU.subtract).then_inc(y_lo_ready, 1)

            def mlp(n0, steps, fronts_, done, after_first=None):
                per_step = fronts_ + 1

                def step(s, n, turn=None, turns=0):
                    S0 = done + s
                    k = s % 2
                    spt, slt = turns, turns * per_step

                    def wait(sm, v):
                        dve.wait_ge(sm, v if turn is None else turn * spt + v)

                    used = n + fronts_
                    dve.wait_ge(slab_used, used if turn is None else turn * slt + used)
                    r = rstd[:, :]
                    if fronts_ == 2:
                        r = r.unsqueeze(1).broadcast_to([P, 2, T])
                        nc.vector.tensor_tensor(scaled[:, k, :].rearrange("p (a t) -> p a t", a=2),
                                                fronts[:, k, :].rearrange("p (a t) -> p a t", a=2), r,
                                                ALU.mult).then_inc(scaled_ready, 1)
                        split_lo(n + RING, turn, slt)
                    else:
                        nc.vector.tensor_tensor(scaled[:, k, 0:T], fronts[:, k, 0:T], r, ALU.mult)\
                            .then_inc(scaled_ready, 1)
                    wait(gate_ready, S0 + 1)
                    if fronts_ == 2:
                        other = scaled[:, k, T:2 * T]
                    else:
                        other = (G[:, :, s] if turn is None
                                 else G[:, :, bass.ds(turn * turns + s, 1)].rearrange("p t a -> p (t a)"))
                    nc.vector.tensor_tensor(hid[:, k, :], scaled[:, k, 0:T], other, ALU.mult)\
                        .then_inc(hid_ready, 1)
                    split_lo(n + fronts_ - 1 + RING, turn, slt)
                    wait(mid_hi_ready, S0 + 1)
                    nc.vector.tensor_tensor(mid_lo[:, k, :], hid[:, k, :], mid_hi[:, k, :].bitcast(F32),
                                            ALU.subtract).then_inc(mid_lo_ready, 1)

                step(0, n0)
                if after_first:
                    after_first()
                n = n0 + fronts_
                turns = 4 if fronts_ == 2 else 2
                loops = (steps - 1) // turns
                with dve.Fori(0, loops) as turn:
                    for c in range(turns):
                        step(1 + c, n + c * per_step, turn, turns)
                        split_lo(n + c * per_step + fronts_ + RING, turn, turns * per_step)
                for s in range(1 + loops * turns, steps):
                    m = n + (s - 1) * per_step
                    step(s, m)
                    split_lo(m + fronts_ + RING)

            def add_tile(name, m):
                j = tile_at[name] + m
                dve.wait_ge(slab_used, slab_of(name, m) + 1)
                nc.vector.tensor_tensor(x[:, m, :], tile_buf(j), x[:, m, :], ALU.add)\
                    .then_inc(tile_read["dve"], 1)

            dve.wait_ge(small_in, 32)
            link(nc.vector.tensor_tensor(lbw[:, 0, :], cols[:, COL["lb0"]:COL["lb0"] + 4],
                                         cols[:, COL["lb1"]:COL["lb1"] + 4], ALU.max))
            nc.vector.tensor_tensor(lbw[:, 1, :], cols[:, COL["lb0"]:COL["lb0"] + 4], lbw[:, 0, :],
                                    ALU.subtract)
            nc.vector.tensor_tensor(lbw[:, 2, :], cols[:, COL["lb1"]:COL["lb1"] + 4], lbw[:, 0, :],
                                    ALU.subtract).then_inc(lb_diff, 1)
            g = cols[:, COL["norm_final_g"]:COL["norm_final_g"] + KT]
            nc.vector.tensor_tensor(gain_product[:, :], g,
                                    cols[:, COL["norm_ffn1_0"]:COL["norm_ffn1_0"] + KT], ALU.mult)
            link(nc.vector.tensor_tensor(gain_square[:, :], g, g, ALU.mult))
            link(nc.vector.tensor_scalar(gain_square[:, :], gain_square[:, :], 1.0, EPS, ALU.mult, ALU.add))
            nc.vector.memset(uu[:, :, 0:2], 0.0)
            nc.vector.memset(S[:, :, :, :], 0.0)
            dve.wait_ge(x_landed[0], 16)
            dve.wait_ge(x_landed[1], 16)
            split_lo(0)
            split_lo(1)
            inverse_rms(0)

            def h_low(k):
                dve.wait_ge(nh_hi, k + 2)
                nc.vector.tensor_tensor(h_lo[:, k:k + 2, :], h32[:, k:k + 2, :],
                                        h_hi[:, k:k + 2, :].bitcast(F32), ALU.subtract).then_inc(nh_lo, 2)

            for k in range(0, KT, 2):
                scale_x("norm_mix_g", h32, h32_ready, [k, k + 1])
                if k >= 2:
                    h_low(k - 2)
            h_low(KT - 2)
            split_lo(2)
            split_lo(3)
            dve.wait_ge(lb_exp, 1)
            link(nc.vector.tensor_tensor(lbw[:, 5, :], lbw[:, 3, :], lbw[:, 4, :], ALU.add))
            link(nc.vector.reciprocal(lbw[:, 5, :], lbw[:, 5, :]))
            link(nc.vector.tensor_tensor(lbw[:, 6, :], lbw[:, 3, :], lbw[:, 5, :], ALU.mult))
            link(nc.vector.tensor_scalar(lbw[:, 7, :], lbw[:, 6, :], -1.0, 1.0, ALU.mult, ALU.add))

            def halves(ap, m):
                flat = ap.rearrange("p a t -> p (a t)")
                v = flat.rearrange("p (n h m) -> p n h m", h=2, m=m)
                return v[:, :, 0, :], v[:, :, 1, :]

            seq = LEVELS + [128]

            def level_prepare(l):
                m = seq[l]
                to = X[:, l % 2, :, :]
                if l >= 2:
                    dve.wait_ge(level_done, 4 * l)
                if m < CHUNK:
                    b_lo, b_up = halves(bb[:, :, :], m)
                    x_lo, x_up = halves(to, m)
                    ref = b_lo[:, :, m - 1:m].broadcast_to([P, 4 * T // (2 * m), m])
                    nc.vector.tensor_tensor(x_up, b_up, ref, ALU.subtract)
                    nc.vector.tensor_tensor(x_lo, ref, b_lo, ALU.subtract).then_inc(level_diff, 1)
                elif m == CHUNK:
                    b_lo, b_up = halves(bb[:, :, :], m)
                    x_lo, x_up = halves(to, m)
                    ref = b_lo[:, :, m - 1:m].broadcast_to([P, 8, m])
                    nc.vector.tensor_copy(x_up, b_up)
                    nc.vector.tensor_tensor(x_lo, ref, b_lo, ALU.subtract).then_inc(level_diff, 1)
                else:
                    ends = bb[:, :, CHUNK - 1:T:CHUNK]
                    link(nc.vector.tensor_tensor(dec[:, :, 0:1], ends[:, :, 0:1], ends[:, :, 1:2], ALU.add))
                    for c, op, a, b in ((2, None, None, None),
                                        (3, ALU.add, None, ends[:, :, 2:3]),
                                        (1, ALU.subtract, ends[:, :, 1:2], None),
                                        (0, ALU.subtract, dec[:, :, 0:1], None)):
                        o = to[:, :, c * CHUNK:(c + 1) * CHUNK]
                        bc = bb[:, :, c * CHUNK:(c + 1) * CHUNK]
                        if op is None:
                            ins = nc.vector.tensor_copy(o, bc)
                        elif b is not None:
                            ins = nc.vector.tensor_tensor(o, bc, b.broadcast_to([P, 4, CHUNK]), op)
                        else:
                            ins = nc.vector.tensor_tensor(o, a.broadcast_to([P, 4, CHUNK]), bc, op)
                    ins.then_inc(level_diff, 1)

            def level_operands(l):
                m = seq[l]
                dve.wait_ge(level_exp, l + 1)
                to = X[:, l % 2, :, :]
                x_lo, x_up = halves(to, m)
                q_up = halves(qq[:, :, :], m)[1]
                k_lo = halves(kk[:, :, :], m)[0]
                nc.vector.tensor_tensor(x_up, x_up, q_up, ALU.mult)
                nc.vector.tensor_tensor(x_lo, x_lo, k_lo, ALU.mult).then_inc(level_ready, 1)

            def level_pick(l):
                if l == len(seq) - 1:
                    dve.wait_ge(level_done, 4 * l + 6)
                    nc.vector.tensor_copy(S_off[:, :, :, :],
                                          banks[:, 2:4, :].rearrange("p b (a t) -> p b a t", a=4))\
                        .then_inc(level_read, 1)
                    return
                mask = ident if l < 0 else level_mask[seq[l]]
                for b in range(4):
                    dve.wait_ge(level_done, 4 * (l + 1) + b + 1)
                    nc.vector.copy_predicated(
                        S[:, b, :, :], mask.bitcast(U32).unsqueeze(1).broadcast_to([P, 4, P]),
                        banks[:, b, :].rearrange("p (a t) -> p a t", a=4)).then_inc(level_read, 1)

            n = first["w_in"]
            j0 = tile_at["w_in"]
            for i in range(44):
                if i < 4:
                    dve.wait_ge(tile_read["act"], reads("act", j0 + i))
                    ins = nc.vector.tensor_scalar(lf[:, i, :], kk[:, i, :], lbw[:, 7, i:i + 1],
                                                  lbw[:, 6, i:i + 1], ALU.mult, ALU.add)
                    link(ins)
                    ins = nc.vector.tensor_scalar(kk[:, i, :], lf[:, i, :], -1.0, 1.0, ALU.mult, ALU.add)
                    if i == 3:
                        ins.then_inc(forget_ready, 1)
                elif i < 8:
                    dve.wait_ge(tile_read["act"], reads("act", j0 + i))
                    nc.vector.tensor_scalar(qq[:, i - 4, :], qq[:, i - 4, :], SCALE, None, ALU.mult)
                elif 20 <= i < 24:
                    dve.wait_ge(slab_used, n + i + 1)
                    c = i - 20
                    dve.wait_ge(tile_read["act"], reads("act", j0 + 19))
                    nc.vector.tensor_tensor(uu[:, c, 2:T + 2], tile_buf(j0 + i), cc[:, c, :],
                                            ALU.mult).then_inc(tile_read["dve"], 1)
                    dve.wait_ge(tile_read["dve"], reads("dve", j0 + i))
                    link(nc.vector.tensor_scalar(conv[:, c, :], uu[:, c, 0:T], col("conv", c), None, ALU.mult))
                    for tap in (1, 2):
                        link(nc.vector.scalar_tensor_tensor(conv[:, c, :], uu[:, c, tap:tap + T],
                                                            col("conv", 4 * tap + c), conv[:, c, :],
                                                            ALU.mult, ALU.add))
                elif 24 <= i < 28:
                    c = i - 24
                    dve.wait_ge(slab_used, n + i + 1)
                    nc.vector.tensor_tensor(y32[:, 4 + c, :], tile_buf(j0 + i), conv[:, c, :],
                                            ALU.mult).then_inc(tile_read["dve"], 1)
                l = (i - FIRST_LEVEL) // 2
                if i >= FIRST_LEVEL and (i - FIRST_LEVEL) % 2 == 0 and l < 8:
                    level_operands(l)
                if i > FIRST_LEVEL and (i - FIRST_LEVEL) % 2 == 1 and l < 8:
                    if l < 7:
                        level_prepare(l + 1)
                    level_pick(l - 1)
                split_lo(n + i + RING)
                if i == FIRST_LEVEL - 1:
                    dve.wait_ge(mixc_landed, 16)
                    dve.wait_ge(logf_ready, 1)
                    for a in range(4):
                        ins = nc.vector.tensor_tensor_scan(bb[:, a, :], chunk_mask, lf[:, a, :], 0.0,
                                                           ALU.mult, ALU.add)
                    link(ins)
                    level_prepare(0)
                if i == FIRST_LEVEL + 17:
                    level_pick(7)
                if i == FIRST_LEVEL + 19:
                    y_low(1, 4, 8)
                if i == FIRST_LEVEL + 23:
                    dve.wait_ge(o_root, 1)
                    link(nc.vector.reciprocal(orr[:, :, :], orr[:, :, :]))
                    link(nc.vector.tensor_tensor(orr[:, :, :], fronts.rearrange("p b (a t) -> p (b a) t", a=2),
                                                 orr[:, :, :], ALU.mult))
                    for a in range(4):
                        ins = nc.vector.scalar_tensor_tensor(y32[:, a, :], orr[:, a, :], col("out_g", a),
                                                             hgs[:, a, :], ALU.mult, ALU.mult)
                    ins.then_inc(y32_ready, 1)
                if i == FIRST_LEVEL + 26:
                    y_low(2, 0, 4)

            n = first["branch"]
            j0 = tile_at["branch"]
            for m in range(8):
                j = j0 + m
                dve.wait_ge(slab_used, n + m + 1)
                nc.vector.tensor_tensor(h32[:, m, :], tile_buf(j), sg[:, m, :], ALU.mult)
                nc.vector.tensor_tensor(sq[:, m, :], tile_buf(j, 1), sg[:, 8 + m, :], ALU.mult)\
                    .then_inc(tile_read["dve"], 1)
                dve.wait_ge(tile_read["dve"], reads("dve", j))
                nc.vector.tensor_tensor(h32[:, m, :], h32[:, m, :], sq[:, m, :], ALU.add)\
                    .then_inc(merged_ready, 1)
                split_lo(n + m + RING)
                dve.wait_ge(merged_hi, m + 1)
                nc.vector.tensor_tensor(h_lo[:, m, :], h32[:, m, :], h_hi[:, m, :].bitcast(F32),
                                        ALU.subtract).then_inc(merged_lo, 1)
            n = first["w_out"]
            for m in range(8):
                add_tile("w_out", m)
                if m < 7:
                    split_lo(n + m + RING)
            late = n + 7 + RING
            operand_lo(1, "norm_ffn_g")
            inverse_rms(1, late)
            n = first["wquery"]

            def mark(ins):
                ins.then_inc(dve_own, 1)
                own[0] += 1
                return own[0]

            def best_sixteen(v, ix, s, left):
                both = range(TT)
                first8, last8 = slice(0, 8), slice(8, 16)
                found = [mark(nc.vector.max(v[tt][:, first8], s[tt])) for tt in both]
                cleared = []
                for tt in both:
                    dve.wait_ge(dve_own, found[tt])
                    placed = mark(nc.vector.max_index(ix[tt][:, first8], v[tt][:, first8], s[tt]))
                    if left is s:
                        dve.wait_ge(dve_own, placed)
                    cleared.append(mark(nc.vector.match_replace(left[tt], v[tt][:, first8], s[tt], NEG)))
                found = []
                for tt in both:
                    dve.wait_ge(dve_own, cleared[tt])
                    found.append(mark(nc.vector.max(v[tt][:, last8], left[tt])))
                for tt in both:
                    dve.wait_ge(dve_own, found[tt])
                    placed = mark(nc.vector.max_index(ix[tt][:, last8], v[tt][:, last8], left[tt]))
                return placed

            def best_keys(i):
                dve.wait_ge(keys_done, i + 1)
                placed = best_sixteen([top_v[:, tt, i, :] for tt in range(TT)],
                                      [top_i[:, tt, i, :] for tt in range(TT)],
                                      [fronts[:, i % 2, tt * P:(tt + 1) * P] for tt in range(TT)],
                                      [rest[:, tt, :] for tt in range(TT)])
                dve.wait_ge(dve_own, placed)
                nc.vector.tensor_copy(top_f[:, :, i, :], top_i[:, :, i, :]).then_inc(keys_read, 1)

            def best_sums(h):
                for tt in range(TT):
                    summed = mark(nc.vector.tensor_tensor(
                        cand[:, tt, :, :],
                        top_v[:, tt, 2 * h, :].unsqueeze(2).broadcast_to([P, TOPK, TOPK]),
                        top_v[:, tt, 2 * h + 1, :].unsqueeze(1).broadcast_to([P, TOPK, TOPK]), ALU.add))
                dve.wait_ge(dve_own, summed)
                flat = [cand[:, tt, :, :].rearrange("p a b -> p (a b)") for tt in range(TT)]
                placed = best_sixteen([best[:, tt, h, :] for tt in range(TT)],
                                      [pos[:, tt, h, :] for tt in range(TT)], flat, flat)
                dve.wait_ge(dve_own, placed)

            for i in range(16):
                dve.wait_ge(slab_used, n + i + 1)
                if i == 1:
                    r_columns(1)
                if i >= 1:
                    best_keys(i - 1)
                if i >= 2 and i % 2 == 0:
                    best_sums(i // 2 - 1)
            best_keys(15)
            best_sums(7)
            link(nc.vector.tensor_tensor(gts[:, :, :, :], best[:, :, :, :],
                                         best[:, :, :, 0:1].broadcast_to([P, TT, HEADS, TOPK]),
                                         ALU.subtract))
            for tt in range(TT):
                ins = nc.vector.tensor_scalar(gts[:, tt, :, :], gts[:, tt, :, :], r_col[:, tt:tt + 1],
                                              None, ALU.mult)
            ins.then_inc(gate_diff, 1)
            link(nc.vector.tensor_scalar(pos1[:, :, :, :], pos[:, :, :, :], 4, None,
                                         ALU.logical_shift_right))
            link(nc.vector.tensor_scalar(pos2[:, :, :, :], pos[:, :, :, :], 15, None,
                                         ALU.bitwise_and))
            nc.vector.tensor_copy(posf[:, 0, :, :, :], pos1[:, :, :, :])
            link(nc.vector.tensor_copy(posf[:, 1, :, :, :], pos2[:, :, :, :]))
            for side in range(2):
                for tt in range(TT):
                    flat = onehot[:, :, :, :].rearrange("p h k a -> p (h k) a")
                    link(nc.vector.tensor_tensor(
                        flat, posf[:, side, tt, :, :].rearrange("p h k -> p (h k)").unsqueeze(2)
                        .broadcast_to([P, P, TOPK]),
                        iota[:, 0:TOPK].unsqueeze(1).broadcast_to([P, P, TOPK]), ALU.is_equal))
                    link(nc.vector.tensor_tensor(
                        onehot[:, :, :, :], onehot[:, :, :, :],
                        top_f[:, tt, side:PEER_GROUPS:2, :].unsqueeze(2)
                        .broadcast_to([P, HEADS, TOPK, TOPK]), ALU.mult))
                    link(nc.vector.tensor_reduce(
                        idx[:, side, tt, :, :].rearrange("p h k -> p (h k)"), flat, AX_X, ALU.add))
            dve.wait_ge(gate_exp, 1)
            link(nc.vector.tensor_reduce(gsum[:, :, :, 0], gts[:, :, :, :], AX_X, ALU.add))
            link(nc.vector.reciprocal(gsum[:, :, :, 1], gsum[:, :, :, 0]))
            nc.vector.tensor_tensor(gts[:, :, :, :], gts[:, :, :, :],
                                    gsum[:, :, :, 1:2].broadcast_to([P, TT, HEADS, TOPK]),
                                    ALU.mult).then_inc(picks_ready, 1)
            dve.wait_ge(picks_copied, 3)

            def pick_rows(rows, idx_T, t, k, n, there):
                nc.vector.tensor_tensor(rows[:, k, :, :], iota.unsqueeze(1).broadcast_to([P, n, P]),
                                        idx_T[:, t].unsqueeze(2).broadcast_to([P, n, P]),
                                        ALU.is_equal).then_inc(there, n)

            for k in range(4):
                pick_rows(pick1, idx1_T, slice(2 * k, 2 * k + 2), k, 2, pick1_there)
                if k % 2:
                    pick_rows(pick2, idx2_T, slice(2 * k - 2, 2 * k + 2), k // 2, 4, pick2_ready)
            with dve.Fori(0, (T - 8) // 8) as turn:
                for k in range(4):
                    dve.wait_ge(pick_used, turn * 8 + (2 * k + 2))
                    pick_rows(pick1, idx1_T, bass.ds(turn * 8 + (8 + 2 * k), 2), k, 2, pick1_there)
                    if k % 2:
                        pick_rows(pick2, idx2_T, bass.ds(turn * 8 + (6 + 2 * k), 4), k // 2, 4,
                                  pick2_ready)
            dve.wait_ge(lo_ready, first["peer"] + RING)
            dve.wait_ge(g_copied, T // 4)
            dve.wait_ge(pick_used, T)
            mlp(first["peer"], NKEYS, 1, 0)
            for k in range(0, KT, 2):
                dve.wait_ge(bank_done, k // 2 + 1)
                nc.vector.tensor_copy(x[:, k:k + 2, :], acc[:, k:k + 2, :]).then_inc(x_ready, 1)
                if k:
                    operand_lo(2, None, [k - 2, k - 1])
            operand_lo(2, None, [6, 7])
            late = first["peer"] + 2 * NKEYS - 1 + RING
            done = NKEYS
            q = 3
            ys = 2
            banks_done = 4
            stages = list(layer_stages())
            for at, (kind, i) in enumerate(stages):
                if at == 0:
                    add_squares(3)
                    inverse_rms(2, late)
                else:
                    inverse_rms(q, late)
                q += 1
                if kind == "ffn":
                    mlp(first[f"ffn{i}"], FT, 2, done, (lambda: inverse_rms(3)) if i == 0 else None)
                    if i == 0:
                        dve.wait_ge(x_ready, 8)
                    done += FT
                    late = first[f"ffn{i}"] + 3 * FT - 1 + RING
                    for b in range(4):
                        dve.wait_ge(bank_done, banks_done + b + 1)
                        nc.vector.scalar_tensor_tensor(x[:, 2 * b:2 * b + 2, :],
                                                       acc[:, 2 * b:2 * b + 2, :], 0.5,
                                                       x[:, 2 * b:2 * b + 2, :], ALU.mult, ALU.add)\
                            .then_inc(x_ready, 1)
                        if b and at + 1 < len(stages):
                            operand_lo(q - 1, stage_gain(*stages[at + 1]), [2 * b - 2, 2 * b - 1])
                    if at + 1 < len(stages):
                        operand_lo(q - 1, stage_gain(*stages[at + 1]), [6, 7])
                    banks_done += 4
                elif kind == "even":
                    dve.wait_ge(attc_sem, 32)
                    nc.vector.memset(pu[:, :, 0:PAD], 0.0)
                    nc.vector.memset(win[:, :, 0:PAD], 0.0)
                    def stick_L_of(g):
                        a, b = 4 * g, 4 * g + 4
                        dve.wait_ge(ln_ready, g + 1)
                        link(nc.vector.scalar_tensor_tensor(asp[:, a:b, :], az[:, a:b, :], 0.0,
                                                            asp[:, a:b, :], ALU.max, ALU.add))
                        nc.vector.tensor_tensor(aL[:, a:b, :], asp[:, a:b, :],
                                                past_neg.unsqueeze(1).broadcast_to([P, 4, 3 * P]),
                                                ALU.mult).then_inc(stick_L, 1)
                        link(nc.vector.tensor_tensor(az[:, a:b, :], az[:, a:b, :], asp[:, a:b, :],
                                                     ALU.subtract))

                    def stick_logs(g):
                        for h in range(4 * g, 4 * g + 4):
                            dve.wait_ge(later_done, h + 1)
                            nc.vector.tensor_tensor(az[:, h, :], banks[:, h % 4, 0:3 * P], az[:, h, :],
                                                    ALU.add).then_inc(stick_w, 1)

                    def stick_shares(g):
                        a, b = 4 * g, 4 * g + 4
                        dve.wait_ge(stick_e, g + 1)
                        nc.vector.scalar_tensor_tensor(az[:, a:b, :], az[:, a:b, :], -1.0,
                                                       past_neg.unsqueeze(1).broadcast_to([P, 4, 3 * P]),
                                                       ALU.mult, ALU.mult).then_inc(stick_a, 1)

                    n = first["even_in"]
                    for i in range(16):
                        if i == 2:
                            r_columns(2)
                        if i < 4:
                            take("even_in", i, aq[:, i, :])
                        elif i < 8:
                            take("even_in", i, ak[:, i - 4, :])
                        elif i >= 12:
                            take("even_in", i, pu[:, i - 12, PAD:PAD + T])
                        if i == 15:
                            stick_L_of(0)
                        split_lo(n + i + RING)
                    stick_L_of(1)
                    stick_logs(0)
                    j0 = tile_at["even_in"]
                    dve.wait_ge(tile_read["dve"], reads("dve", j0 + 15))
                    for g, w in enumerate(WINDOWS):
                        src = pu[:, g, :]
                        if g:
                            dve.wait_ge(pooled_ready, g)
                        for r in range(g + 1):
                            to = win[:, r % 2, :]
                            link(nc.vector.tensor_tensor(to[:, PAD:], src[:, PAD:],
                                                         src[:, PAD - 2 ** r:PAD - 2 ** r + T], ALU.add))
                            src = to
                        link(nc.vector.tensor_tensor(src[:, PAD:], src[:, PAD:], inv_count[:, g, :],
                                                     ALU.mult))
                        nc.vector.tensor_tensor(pooled[:, g, :], src[:, PAD:], pu[:, g, PAD:],
                                                ALU.subtract).then_inc(pooled_ready, 1)
                        if g == 2:
                            stick_shares(0)
                            stick_logs(1)
                    stick_shares(1)
                    dve.wait_ge(pool_done, 4)
                    for g in range(4):
                        nc.vector.tensor_scalar(y32[:, 4 + g, :], tile[:, g, :],
                                                col("pool_scale", g), None, ALU.mult)\
                            .then_inc(tile_read["dve"], 1)
                    y_low(ys + 1, 4, 8)
                    y_low(ys + 2, 0, 4, fronts.rearrange("p b (a t) -> p (b a) t", a=2))
                    ys += 2
                    n = first["even_out"]
                    for m in range(8):
                        add_tile("even_out", m)
                        if at + 1 < len(stages):
                            operand_lo(q - 1, stage_gain(*stages[at + 1]), [m])
                        if m < 7:
                            split_lo(n + m + RING)
                    late = n + 7 + RING
                else:
                    def low_part(part):
                        a = 2 * (part % 2)
                        y_low(ys + part + 1, 2 * part, 2 * part + 2, tile[:, a:a + 2, :])

                    def head_step(h):
                        if h < ODD_HEADS:
                            k = h % 4
                            slope = float(2.0 ** (-8.0 * (h + 1) / ODD_HEADS))
                            dve.wait_ge(sc_done, h + 1)
                            if h >= 4:
                                dve.wait_ge(p_turned, h - 3)
                            link(nc.vector.scalar_tensor_tensor(sc[:, k, :], dist, slope,
                                                                banks[:, h % 4, 0:3 * P],
                                                                ALU.mult, ALU.add))
                            nc.vector.tensor_reduce(st[:, 0, k, 0:1], sc[:, k, 0:P], AX_X, ALU.max,
                                                    negate=True)
                            nc.vector.tensor_reduce(st[:, 0, k, 1:2], sc[:, k, P:3 * P], AX_X, ALU.max,
                                                    negate=True).then_inc(sc_read, 1)
                        if h >= 1:
                            k = (h - 1) % 4
                            dve.wait_ge(p_exp, 2 * h)
                            link(nc.vector.reciprocal(st[:, 2, k, :], st[:, 1, k, :]))
                            nc.vector.tensor_scalar(sc[:, k, 0:P], sc[:, k, 0:P], st[:, 2, k, 0:1], None,
                                                    ALU.mult)
                            nc.vector.tensor_scalar(sc[:, k, P:3 * P], sc[:, k, P:3 * P],
                                                    st[:, 2, k, 1:2], None, ALU.mult).then_inc(p_norm, 1)
                        if h in (9, 13):
                            low_part((h - 9) // 4)

                    n = first["qkv"]
                    for i in range(24):
                        if i == 2:
                            r_columns(3)
                        if i < 8:
                            take("qkv", i, bq[:, i, :], SCALE)
                        elif i < 16:
                            take("qkv", i, bk[:, i - 8, :])
                        if i in ODD_AFTER:
                            head_step(ODD_AFTER[i])
                        split_lo(n + i + RING)
                    for h in range(len(ODD_AFTER), ODD_HEADS + 1):
                        head_step(h)
                    low_part(2)
                    low_part(3)
                    ys += 4
                    n = first["w_o"]
                    for m in range(8):
                        add_tile("w_o", m)
                        if at + 1 < len(stages):
                            operand_lo(q - 1, stage_gain(*stages[at + 1]), [m])
                        if m < 7:
                            split_lo(n + m + RING)
                    late = n + 7 + RING
            inverse_rms(q)
            scale_x("norm_final", h32, result_ready)

        @block.tensor
        def _(pe):
            def mm(out, lhsT, rhs, start, stop, **kw):
                return nc.tensor.matmul(out, lhsT, rhs, start=start, stop=stop, **kw)

            def wait_slab(n, turn=None, per=0):
                pe.wait_ge(lo_ready, n + 1 if turn is None else turn * per + (n + 1))

            def three(out, s, c, r_hi, r_lo, start, stop, **kw):
                hi, lo = w_hi[:, s, c:c + P], w_lo[:, s, c:c + P]
                mm(out, hi, r_hi, start, False, **kw)
                mm(out, hi, r_lo, False, False, **kw)
                return mm(out, lo, r_hi, False, stop, **kw)

            def free_tile(j):
                if j >= 2:
                    r = readers[j - 2]
                    pe.wait_ge(tile_read[r], reads(r, j - 2))

            def project(name, i, n, hi, lo, lows=None):
                j = tile_at[name] + i
                free_tile(j)
                wait_slab(n)
                for k in range(KT):
                    if lows is not None:
                        pe.wait_ge(nh_lo, lows + k + 1)
                    ins = three(tile_buf(j), n % RING, k * P, hi[:, k, :], lo[:, k, :],
                                k == 0, k == KT - 1)
                ins.then_inc(slab_used, 1)

            def project_tokens(name, i, c, n, hi, lo):
                j = tile_at[name] + i
                if c == 0:
                    free_tile(j)
                    free_tile(j + 1)
                elif c >= 4:
                    pe.wait_ge(tile_read["act"], reads("act", j - 3))
                wait_slab(n + 1)
                s = n % RING
                assert s % 2 == 0
                for tt in range(TT):
                    o = pair_buf(c, tt)
                    for k in range(KT):
                        a, b = hi[:, k, tt * P:(tt + 1) * P], lo[:, k, tt * P:(tt + 1) * P]
                        w = [part[:, s:s + 2, k * P:(k + 1) * P] for part in (w_hi, w_lo)]
                        mm(o, a, w[0], k == 0, False)
                        mm(o, b, w[0], False, False)
                        ins = mm(o, a, w[1], False, k == KT - 1)
                ins.then_inc(slab_used, 2)

            def norm(q):
                pe.wait_ge(sq_summed, squaring(q))
                mm(sum_at[q], ones, (sq_half if q == 3 else sq)[:, 0, :], True, True).then_inc(sums, 1)

            def weighted_norm():
                pe.wait_ge(weights_ready, 1)
                pe.wait_ge(squares, 6)
                pe.wait_ge(squares_last, 2)
                for k in range(KT):
                    ins = mm(sum_at[2], square_weights[:, k, :], sq[:, k, :], k == 0, k == KT - 1)
                ins.then_inc(sums, 1)

            def turn_rstd(q):
                pe.wait_ge(rstd_ready, q + 1)
                if q >= 3:
                    pe.wait_ge(attc_sem, 32)
                for tt in range(TT):
                    ins = nc.tensor.transpose(front[:, 1, tt * P:(tt + 1) * P], rstd[:, tt * P:(tt + 1) * P],
                                              ident if q < 3 else ident2)
                ins.then_inc(r_turned, 1)

            def mlp(n0, steps, fronts_, done, seeded, banks_done, q=None):
                per_step = fronts_ + 1

                def wait(turn, turns, sm, v):
                    if turn is None:
                        pe.wait_ge(sm, v)
                    else:
                        pe.wait_ge(sm, turn * turns + v)

                def feed(s, n, turn=None, turns=0):
                    S0 = done + s
                    if s >= 2 or turn is not None:
                        wait(turn, turns, scaled_ready, S0 - 1)
                    for f in range(fronts_):
                        wait_slab(n + f, turn, turns * per_step)
                        for k in range(KT):
                            if q is not None and s == 0 and f == 0:
                                pe.wait_ge(nh_lo, 8 * (q - 1) + k + 1)
                            ins = three(fronts[:, s % 2, f * T:(f + 1) * T], (n + f) % RING, k * P,
                                        h_hi[:, k, :], h_lo[:, k, :], k == 0, k == KT - 1)
                        ins.then_inc(slab_used, 1)

                def drain(s, n, turn=None, turns=0, last=False):
                    S0 = done + s
                    wait(turn, turns, mid_lo_ready, S0 + 1)
                    wait_slab(n, turn, turns * per_step)
                    begin = s == 0 and not seeded and turn is None
                    for m in range(KT):
                        ins = three(acc[:, m, :], n % RING, m * P, mid_hi[:, s % 2, :], mid_lo[:, s % 2, :],
                                    begin and m % 2 == 0, False, skip_group_check=True)
                        if last and m % 2:
                            ins.then_inc(bank_done, 1)
                    if not last:
                        ins.then_inc(slab_used, 1)
                    else:
                        pe.wait_ge(bank_done, banks_done + 4)
                        pe.sem_inc(slab_used, 1)

                feed(0, n0)
                n = n0 + fronts_
                turns = 4 if fronts_ == 2 else 2
                if q == 3:
                    weighted_norm()
                elif q is not None:
                    norm(q)
                feed(1, n)
                if q == 3:
                    norm(3)
                drain(0, n + fronts_)
                n += per_step
                loops = (steps - 2) // turns
                with pe.Fori(0, loops) as turn:
                    for c in range(turns):
                        feed(2 + c, n + c * per_step, turn, turns)
                        drain(1 + c, n + c * per_step + fronts_, turn, turns)
                for s in range(2 + loops * turns, steps):
                    m = n + (s - 2) * per_step
                    feed(s, m)
                    drain(s - 1, m + fronts_)
                drain(steps - 1, n0 + steps * per_step - 1, last=True)

            pe.wait_ge(small_in, 32)
            for k in range(KT):
                pe.wait_ge(squares, 2 * k // KT + 1)
                ins = mm(sum_at[0], ones, sq[:, k, :], k == 0, k == KT - 1)
            ins.then_inc(sums, 1)
            def head(ap, h, tt):
                p = DH * (h % 2)
                return ap[p:p + DH, h // 2, tt * P:(tt + 1) * P]

            def level_scores(l):
                if l >= 0:
                    pe.wait_ge(level_ready, l + 1)
                else:
                    pe.wait_ge(forget_ready, 1)
                    pe.wait_ge(level_diff, 1)
                for bank in range(4):
                    tt = bank // 2
                    if l == 7 and tt == 0:
                        continue
                    if l >= 0:
                        pe.wait_ge(level_read, 4 * l + bank + 1)
                    for h in range(bank % 2, HEADS, 2):
                        if l < 0:
                            a, b = head(kk, h, tt), head(qq, h, tt)
                        else:
                            a = head(X[:, l % 2, :, :], h, tt if l < 7 else 0)
                            b = head(X[:, l % 2, :, :], h, tt)
                        ins = mm(banks[:, bank, (h // 2) * P:(h // 2 + 1) * P], a, b, True, True)
                    ins.then_inc(level_done, 1)

            def outputs(v, h, to, scores):
                p = DH * (h % 2)
                w = [v[:, tt, h * DH:(h + 1) * DH] for tt in range(TT)]
                o = to[p:p + DH, :]
                mm(o[:, 0:P], w[0], scores[0], True, True)
                mm(o[:, P:T], w[0], scores[1], True, False)
                return mm(o[:, P:T], w[1], scores[2], False, True)

            fr = fronts.rearrange("p b (a t) -> p (b a) t", a=2)
            n = first["w_in"]
            for i in range(44):
                if i in (8, 10):
                    project_tokens("w_in", i, i - 8, n + i, h_hi, h_lo)
                elif i not in (9, 11):
                    project("w_in", i, n + i, h_hi, h_lo, 0 if i == 0 else None)
                l = (i - FIRST_LEVEL) // 2 - 1
                if i >= FIRST_LEVEL and (i - FIRST_LEVEL) % 2 == 0 and l < 8:
                    level_scores(l)
                if i == FIRST_LEVEL + 19:
                    pe.wait_ge(level_read, 33)
                    pe.wait_ge(tile_read["act"], reads("act", tile_at["w_in"] + 11))
                    for h in range(HEADS):
                        ins = outputs(vv, h, fr[:, h // 2, :],
                                      (S[:, h % 2, h // 2, :], S_off[:, h % 2, h // 2, :],
                                       S[:, 2 + h % 2, h // 2, :]))
                    ins.then_inc(o_done, 1)
                if i == FIRST_LEVEL + 21:
                    pe.wait_ge(o_sq, 1)
                    pe.wait_ge(mixc_landed, 16)
                    for b in range(2):
                        ins = mm(banks[:, b, :], head_ones,
                                 osq[:, 2 * b:2 * b + 2, :].rearrange("p a t -> p (a t)"), True, True)
                    ins.then_inc(o_sum, 1)
            pe.wait_ge(y_lo_ready, 2)
            n = first["branch"]
            for m in range(8):
                wait_slab(n + m)
                j = tile_at["branch"] + m
                free_tile(j)
                for half in range(2):
                    for k in range(4):
                        kk_ = 4 * half + k
                        ins = three(tile_buf(j, half), (n + m) % RING, kk_ * P, y_hi[:, kk_, :],
                                    y_lo[:, kk_, :], k == 0, k == 3)
                ins.then_inc(slab_used, 1)
            pe.wait_ge(merged_lo, 8)
            n = first["w_out"]
            for m in range(8):
                project("w_out", m, n + m, h_hi, h_lo)
            for m in range(KT):
                wait_x(pe, 1, m)
                ins = mm(acc[:, m, :], ident, x[:, m, :], m % 2 == 0, False, skip_group_check=True)
            ins.then_inc(x_seeded, 1)
            norm(1)
            pe.wait_ge(keys_in_sem, 16)
            n = first["wquery"]

            def key_scores(i):
                j = tile_at["wquery"] + i
                pe.wait_ge(tile_read["act"], reads("act", j))
                if i == 1:
                    pe.wait_ge(r_col_ready, 1)
                if i >= 2:
                    pe.wait_ge(keys_read, i - 1)
                for tt in range(TT):
                    ins = mm(fronts[:, i % 2, tt * P:(tt + 1) * P], qT[:, i, tt * P:(tt + 1) * P],
                             keysT[:, i, :], True, True)
                ins.then_inc(keys_done, 1)

            for i in range(16):
                project("wquery", i, n + i, h_hi, h_lo, 8 if i == 0 else None)
                if i == 0:
                    turn_rstd(1)
                if i >= 1:
                    key_scores(i - 1)
            key_scores(15)
            pe.wait_ge(picks_ready, 1)
            for i in range(3):
                for tt in range(TT):
                    src = gts[:, tt, :, :] if i == 2 else idx[:, i, tt, :, :]
                    ins = nc.tensor.transpose(tile[:, i, tt * P:(tt + 1) * P],
                                              src.rearrange("p h k -> p (h k)"), ident)
            ins.then_inc(picks_turned, 1)
            def weights(b, c, k):
                if b < 2:
                    o = fronts[:, b, c * P:(c + 1) * P]
                else:
                    o = tile[:, 2 * b - 4 + c // 2, (c % 2) * P:(c % 2 + 1) * P]
                mm(o, pick1[:, 2 * (b % 2) + k // 2, k % 2, :], pick2[:, b % 2, k, :], True, True).then_inc(pick_used, 1)

            pe.wait_ge(picks_copied, 3)
            for t in range(16):
                pe.wait_ge(pick1_ready, t + 1)
                pe.wait_ge(pick2_ready, t + 1)
                weights(t // 4, t % 4, t % 4)
            with pe.Fori(0, T // 16 - 1) as turn:
                for b in range(4):
                    pe.wait_ge(g_copied, turn * 4 + (b + 1))
                    for c in range(4):
                        pe.wait_ge(pick1_ready, turn * 16 + (16 + 4 * b + c + 1))
                        pe.wait_ge(pick2_ready, turn * 16 + (16 + 4 * b + c + 1))
                        weights(b, c, c)
            pe.wait_ge(g_copied, T // 4)
            mlp(first["peer"], NKEYS, 1, 0, True, 0)
            done = NKEYS
            q = 3
            ys = 2
            for kind, i in layer_stages():
                lows = 8 * (q - 1)
                q += 1
                if kind == "ffn":
                    mlp(first[f"ffn{i}"], FT, 2, done, False, 4 * (i + 1), q - 1)
                    done += FT
                elif kind == "even":
                    n = first["even_in"]
                    for i in range(16):
                        if i in (8, 10):
                            project_tokens("even_in", i, i - 8, n + i, h_hi, h_lo)
                        elif i not in (9, 11):
                            project("even_in", i, n + i, h_hi, h_lo, lows if i == 0 else None)
                        if i == 1:
                            norm(q - 1)
                            turn_rstd(q - 1)
                        for h in STICK_AFTER.get(i, ()):
                            p = DH * (h % 2)
                            if h == 0:
                                pe.wait_ge(tile_read["dve"], reads("dve", tile_at["even_in"] + 7))
                            if h >= 4:
                                pe.wait_ge(z_read, h - 3)
                            k_ = ak[p:p + DH, h // 2, :]
                            q_ = aq[p:p + DH, h // 2, :]
                            mm(banks[:, h % 4, 0:T], k_[:, 0:P], q_, True, True)
                            mm(banks[:, h % 4, T:T + P], k_[:, P:T], q_[:, P:T], True, True)\
                                .then_inc(z_done, 1)
                    def later_sums(g):
                        pe.wait_ge(stick_L, g + 1)
                        for h in range(4 * g, 4 * g + 4):
                            if g == 0:
                                pe.wait_ge(z_read, 8)
                            else:
                                pe.wait_ge(stick_w, h - 3)
                            o = banks[:, h % 4, 0:3 * P]
                            mm(o, later, aL[:, h, :], True, True)
                            mm(o[:, P:2 * P], ones, aL[:, h, 2 * P:3 * P], False, True,
                               skip_group_check=True).then_inc(later_done, 1)

                    later_sums(0)
                    later_sums(1)
                    pe.wait_ge(tile_read["act"], reads("act", tile_at["even_in"] + 15))
                    for h in range(HEADS):
                        pe.wait_ge(stick_a, h // 4 + 1)
                        ins = outputs(av, h, fr[:, h // 2, :], [az[:, h, c * P:(c + 1) * P] for c in range(3)])
                        if h == 3:
                            for g in range(4):
                                pe.wait_ge(pooled_ready, g + 1)
                                mm(tile[:, g, :], wpool[:, g, :], pooled[:, g, :], True, True)\
                                    .then_inc(pool_done, 1)
                    ins.then_inc(ao_done, 1)
                    pe.wait_ge(y_lo_ready, ys + 2)
                    ys += 2
                    n = first["even_out"]
                    for m in range(8):
                        project("even_out", m, n + m, y_hi, y_lo)
                else:
                    def head_step(h):
                        if h < ODD_HEADS:
                            p = DH * (h % 2)
                            if h >= 4:
                                pe.wait_ge(sc_read, h - 3)
                            k_ = bk[p:p + DH, h // 2, :]
                            q_ = bq[p:p + DH, h // 2, :]
                            mm(banks[:, h % 4, 0:P], q_[:, 0:P], k_[:, 0:P], True, True)
                            mm(banks[:, h % 4, P:3 * P], q_[:, P:T], k_, True, True).then_inc(sc_done, 1)
                        if 2 <= h <= ODD_HEADS + 1:
                            g = h - 2
                            pe.wait_ge(p_norm, g + 1)
                            if g >= 2:
                                pe.wait_ge(p_copied, g - 1)
                            o = fronts[:, g % 2, :]
                            nc.tensor.transpose(o[:, 0:P], sc[:, g % 4, 0:P], ident2)
                            nc.tensor.transpose(o[:, P:2 * P], sc[:, g % 4, P:2 * P], ident2)
                            nc.tensor.transpose(o[:, 2 * P:3 * P], sc[:, g % 4, 2 * P:3 * P], ident2)\
                                .then_inc(p_turned, 1)
                        if h >= 3:
                            g = h - 3
                            if g == 0:
                                pe.wait_ge(tile_read["act"], reads("act", tile_at["qkv"] + 23))
                            pe.wait_ge(p_copied, g + 1)
                            if g in (8, 12):
                                pe.wait_ge(y_lo_ready, ys + g // 4 - 1)
                            outputs(bv, g, tile[:, (g // 2) % 4, :],
                                    [pT[:, g % 2, c * P:(c + 1) * P] for c in range(3)]).then_inc(bo_done, 1)

                    n = first["qkv"]
                    for i in range(24):
                        if i >= 16:
                            if i % 2 == 0:
                                project_tokens("qkv", i, i - 16, n + i, h_hi, h_lo)
                        else:
                            project("qkv", i, n + i, h_hi, h_lo, lows if i == 0 else None)
                        if i == 1:
                            norm(q - 1)
                            turn_rstd(q - 1)
                        if i + 1 in ODD_AFTER:
                            head_step(ODD_AFTER[i + 1])
                    for h in range(len(ODD_AFTER), ODD_HEADS + 3):
                        head_step(h)
                    pe.wait_ge(y_lo_ready, ys + 4)
                    ys += 4
                    n = first["w_o"]
                    for m in range(8):
                        project("w_o", m, n + m, y_hi, y_lo)
            norm(q)


def tiles(w):
    K, N = w.shape
    return w.reshape(K // P, P, N // P, P).transpose(2, 1, 0, 3).reshape(N // P, P, K)


def slabs(inputs):
    w_in = inputs["w_in"][0]
    order = [512, 0, 1024, 1536, 2560, 3072, 2048]
    parts = [tiles(w_in[:, o:o + 512]) for o in order] + [tiles(w_in[:, 3584:])]
    wa, wb = tiles(inputs["w_branch_hg"][0]), tiles(inputs["w_branch_conv"][0])
    parts.append(np.concatenate([wa, wb], 2))
    parts.append(tiles(inputs["w_out"][0]))
    parts.append(tiles(inputs["peer_w_query"][0]))
    u = inputs["peer_u"][0].reshape(P, P, KT, P).transpose(1, 3, 2, 0).reshape(P, P, D)
    v = inputs["peer_v"][0].reshape(P, P, D).transpose(1, 0, 2)
    pair = np.stack([u[1:], v[:-1]], 1).reshape(2 * (P - 1), P, D)
    parts += [u[0:1], pair, v[-1:]]

    def ffn(pre, layer):
        g = tiles(inputs[f"{pre}_gate_2"][layer])
        up = tiles(inputs[f"{pre}_up_2"][layer])
        down = inputs[f"{pre}_down_2"][layer].reshape(FT, P, D)
        body = np.stack([g[1:], up[1:], down[:-1]], 1).reshape(3 * (FT - 1), P, D)
        return [g[0:1], up[0:1], body, down[-1:]]

    parts += ffn("ffn1", 0)
    parts += [tiles(inputs["even_w_in_2"][0]), tiles(inputs["even_w_out_2"][0])]
    parts += ffn("ffn2", 0) + ffn("ffn1", 1)
    parts += [tiles(inputs["odd_w_qkv_2"][0]), tiles(inputs["odd_w_o_2"][0])]
    parts += ffn("ffn2", 1)
    return np.concatenate(parts, 0)


def by_feature(v):
    return v.reshape(-1, P).T


def kernel(**inputs):
    import concourse.bacc as _bacc
    from concourse.bass_utils import run_bass_kernel_spmd as _run

    inputs = {k: np.asarray(v) for k, v in inputs.items()}
    n = stream_plan()[1]
    vectors = [inputs["norm_mix_g"][0], inputs["norm_ffn_g"][0], inputs["norm_final_g"]]
    for layer in range(2):
        vectors += [inputs["norm_ffn1_2"][layer], inputs["norm_mix_2"][layer], inputs["norm_ffn2_2"][layer]]
    vectors += [inputs["norm_final_2"], inputs["hg_lb_logits"][0], inputs["hg_lb_logits"][1],
                inputs["hg_out_norm_g"][0], *inputs["conv_w"][0], inputs["even_pool_scale_2"][0]]
    k1, k2 = inputs["peer_keys1"][0], inputs["peer_keys2"][0]
    arrays = {
        "stream": slabs(inputs)[:n],
        "x_t": inputs["x"][0].T.reshape(KT, P, T).transpose(1, 0, 2),
        "columns": np.concatenate([by_feature(v) for v in vectors] + [np.full((P, 1), EPS, np.float32),
                                     np.full((P, 1), EPS * EPS, np.float32)], 1),
        "lanes": np.stack([np.ones((P, P), np.float32),
                           np.broadcast_to(np.arange(P, dtype=np.float32), (P, P))], 1),
        "keys_t": np.stack([k1, k2], 1).reshape(PEER_GROUPS, NKEYS, P).transpose(2, 0, 1),
        "w_pool": inputs["even_w_pool_2"][0].transpose(1, 0, 2),
        "mixer_constants": mixer_constants(),
        "attention_constants": attention_constants(),
    }
    nc = _bacc.Bacc("TRN2", target_bir_lowering=False, num_devices=1)
    args = []
    for name in arrays:
        arrays[name] = np.ascontiguousarray(arrays[name])
        args.append(nc.dram_tensor(name, arrays[name].shape, F32, kind="ExternalInput").ap())
    args.append(nc.dram_tensor("out_t", (P, KT, T), F32, kind="ExternalOutput").ap())
    build(nc, *args)
    r = _run(nc, [arrays], core_ids=[0])
    got = r.results[0]["out_t"]
    return got.transpose(1, 0, 2).reshape(D, T).T.reshape(1, T, D)
```
